# Optimizing a Trainium2 kernel written in Bass

```python
import math
import jax
import jax.numpy as jnp
from jax import lax
import numpy as np

D_MODEL = 1024
BATCH = 1
SEQ = 1024
DEPTH = 1

CHUNK = 64
GDN_HEADS = 4
GDN_DIM = 128
GDN_WIDTH = GDN_HEADS * GDN_DIM
CONV_WIDTH = 4
RWKV_HEADS = 8
RWKV_DIM = 64
RWKV_WIDTH = RWKV_HEADS * RWKV_DIM
RWKV_DECAY_RANK = 64
RWKV_A_RANK = 64
RWKV_V_RANK = 32
RWKV_G_RANK = 128
SWA_Q_HEADS = 8
SWA_KV_HEADS = 2
SWA_GROUP = SWA_Q_HEADS // SWA_KV_HEADS
SWA_DIM = 64
WINDOW = 128
WINDOW_CHUNKS = WINDOW // CHUNK
N_BRANCH = 3
D_FF = -(-8 * D_MODEL // (3 * 256)) * 256
ALPHA = (2 * DEPTH) ** 0.25
DEEPNORM_BETA = (8 * DEPTH) ** -0.25
LN_EPS = 1e-5
GDN_NORM_EPS = 1e-6
RWKV_LNX_EPS = 64e-5
A_COLS = (GDN_WIDTH, GDN_WIDTH, GDN_WIDTH, GDN_WIDTH, GDN_HEADS, GDN_HEADS)
B_COLS = (RWKV_WIDTH, RWKV_WIDTH, RWKV_WIDTH, RWKV_DECAY_RANK, RWKV_A_RANK, RWKV_G_RANK)
C_COLS = (SWA_Q_HEADS * SWA_DIM, SWA_KV_HEADS * SWA_DIM, SWA_KV_HEADS * SWA_DIM)
G_COLS = (N_BRANCH * D_MODEL,)
GROUP_COLS = (sum(A_COLS), sum(B_COLS), sum(C_COLS), sum(G_COLS))
N_IN = sum(GROUP_COLS)

kernel_name = "hybrid_gdn_rwkv7_swa_deepnorm"

F32 = jnp.float32

def _split(u, sizes):
    offs = [int(o) for o in np.cumsum(sizes)[:-1]]
    return jnp.split(u, offs, axis=-1)

def _heads(u, h):
    return u.reshape(u.shape[:-1] + (h, u.shape[-1] // h))

def _l2norm(u, eps=1e-6):
    u = u.astype(F32)
    return u * lax.rsqrt(jnp.sum(u * u, -1, keepdims=True) + eps)

def _layer_norm(x, w, b):
    x32 = x.astype(F32)
    mu = jnp.mean(x32, -1, keepdims=True)
    var = jnp.mean(jnp.square(x32 - mu), -1, keepdims=True)
    return ((x32 - mu) * lax.rsqrt(var + LN_EPS) * w + b).astype(x.dtype)

def _causal_conv(u, w):
    k_w = w.shape[0]
    t = u.shape[1]
    up = jnp.pad(u, ((0, 0), (k_w - 1, 0), (0, 0)))
    out = up[:, 0:t] * w[0]
    for j in range(1, k_w):
        out = out + up[:, j:j + t] * w[j]
    return out

def _gated_delta_chunked(q, k, v, g, beta):
    bsz, t, h, dk = q.shape
    dv = v.shape[-1]
    n = t // CHUNK

    def to_chunks(u):
        return u.reshape(bsz, n, CHUNK, h, u.shape[-1]).transpose(0, 1, 3, 2, 4)

    q, k, v = to_chunks(q), to_chunks(k), to_chunks(v)
    g = g.reshape(bsz, n, CHUNK, h).transpose(0, 1, 3, 2)
    beta = beta.reshape(bsz, n, CHUNK, h).transpose(0, 1, 3, 2)
    gc = jnp.cumsum(g, -1)
    causal = jnp.tril(jnp.ones((CHUNK, CHUNK), bool))
    strict = jnp.tril(jnp.ones((CHUNK, CHUNK), bool), -1)
    decay = jnp.exp(jnp.where(causal, gc[..., :, None] - gc[..., None, :], -jnp.inf))
    k_beta = k * beta[..., None]
    lower = jnp.where(strict, jnp.einsum('bnhid,bnhjd->bnhij', k_beta, k) * decay, 0.0)
    eye = jnp.broadcast_to(jnp.eye(CHUNK, dtype=F32), lower.shape)
    t_inv = lax.linalg.triangular_solve(lower + eye, eye, left_side=True, lower=True,
                                        unit_diagonal=True)
    value = jnp.einsum('bnhij,bnhjd->bnhid', t_inv, v * beta[..., None])
    k_cum = jnp.einsum('bnhij,bnhjd->bnhid', t_inv, k_beta * jnp.exp(gc)[..., None])
    attn = jnp.where(causal, jnp.einsum('bnhid,bnhjd->bnhij', q, k) * decay, 0.0)
    q_dec = q * jnp.exp(gc)[..., None]
    g_last = gc[..., -1]
    k_tail = k * jnp.exp(g_last[..., None] - gc)[..., None]

    def step(s, inp):
        q_i, val_i, kc_i, at_i, gl_i, kt_i = inp
        v_new = val_i - jnp.einsum('bhcd,bhde->bhce', kc_i, s)
        o = jnp.einsum('bhcd,bhde->bhce', q_i, s) + jnp.einsum('bhij,bhje->bhie', at_i, v_new)
        s = s * jnp.exp(gl_i)[..., None, None] + jnp.einsum('bhcd,bhce->bhde', kt_i, v_new)
        return s, o

    xs = tuple(jnp.moveaxis(a, 1, 0) for a in (q_dec, value, k_cum, attn, g_last, k_tail))
    s0 = jnp.zeros((bsz, h, dk, dv), F32)
    _, o = lax.scan(step, s0, xs)
    return o.transpose(1, 0, 3, 2, 4).reshape(bsz, t, h, dv)

def _gdn_branch(ua, conv_w, a_log, dt_bias, norm_w):
    bsz, t, _ = ua.shape
    q, k, v, z, b_raw, a_raw = _split(ua, A_COLS)
    qkv = jax.nn.silu(_causal_conv(jnp.concatenate([q, k, v], -1), conv_w))
    q, k, v = _split(qkv, (GDN_WIDTH, GDN_WIDTH, GDN_WIDTH))
    q = _l2norm(_heads(q, GDN_HEADS)) * (GDN_DIM ** -0.5)
    k = _l2norm(_heads(k, GDN_HEADS))
    v = _heads(v, GDN_HEADS).astype(F32)
    beta = jax.nn.sigmoid(b_raw.astype(F32))
    g = -jnp.exp(a_log.astype(F32)) * jax.nn.softplus(a_raw.astype(F32) + dt_bias.astype(F32))
    o = _gated_delta_chunked(q, k, v, g, beta)
    o = o * lax.rsqrt(jnp.mean(o * o, -1, keepdims=True) + GDN_NORM_EPS) * norm_w
    o = o * jax.nn.silu(_heads(z, GDN_HEADS).astype(F32))
    return o.reshape(bsz, t, GDN_WIDTH).astype(ua.dtype)

def _rwkv7_scan(r, w, k, v, kk, a):
    bsz, t, h, n = r.shape

    def step(s, inp):
        r_t, w_t, k_t, v_t, kk_t, a_t = inp
        sa = jnp.einsum('bhvk,bhk->bhv', s, -kk_t)
        s = (s * w_t[:, :, None, :] + sa[..., None] * (kk_t * a_t)[:, :, None, :]
             + v_t[..., None] * k_t[:, :, None, :])
        return s, jnp.einsum('bhvk,bhk->bhv', s, r_t)

    xs = tuple(jnp.moveaxis(u, 1, 0) for u in (r, w, k, v, kk, a))
    s0 = jnp.zeros((bsz, h, n, n), F32)
    _, out = lax.scan(step, s0, xs)
    return jnp.moveaxis(out, 0, 1)

def _rwkv7_branch(ub, x, mu, w0, w_up, a0, a_up, g_up, k_k, k_a, r_k, lnx_w, lnx_b, v_first, vres):
    bsz, t, _ = ub.shape
    ub = ub.astype(F32)
    prev = jnp.pad(ub, ((0, 0), (1, 0), (0, 0)))[:, :-1]
    ub = ub + (prev - ub) * mu
    r, k, v, w_low, a_low, g_low = _split(ub, B_COLS)
    w_log = -jax.nn.softplus(-(w0 + jnp.tanh(w_low) @ w_up)) - 0.5
    decay = jnp.exp(-jnp.exp(w_log))
    a = jax.nn.sigmoid(a0 + a_low @ a_up)
    gate = jax.nn.sigmoid(g_low) @ g_up
    if vres is None:
        v_first = v
    else:
        vd, vu, v0 = vres
        v = v + (v_first - v) * jax.nn.sigmoid(v0 + (x.astype(F32) @ vd) @ vu)
    kk = _l2norm(_heads(k * k_k, RWKV_HEADS))
    k = k * (1.0 + (a - 1.0) * k_a)
    r_h, k_h, v_h = _heads(r, RWKV_HEADS), _heads(k, RWKV_HEADS), _heads(v, RWKV_HEADS)
    o = _rwkv7_scan(r_h, _heads(decay, RWKV_HEADS), k_h, v_h, kk, _heads(a, RWKV_HEADS))
    mean = jnp.mean(o, -1, keepdims=True)
    var = jnp.mean(jnp.square(o - mean), -1, keepdims=True)
    o = ((o - mean) * lax.rsqrt(var + RWKV_LNX_EPS)).reshape(bsz, t, RWKV_WIDTH) * lnx_w + lnx_b
    bonus = jnp.sum(r_h * k_h * r_k, -1, keepdims=True) * v_h
    o = (o + bonus.reshape(bsz, t, RWKV_WIDTH)) * gate
    return o.astype(x.dtype), v_first

def _swa_branch(uc, sinks):
    bsz, t, _ = uc.shape
    nc = t // CHUNK
    w = WINDOW_CHUNKS
    q, k, v = _split(uc.astype(F32), C_COLS)
    qc = q.reshape(bsz, nc, CHUNK, SWA_KV_HEADS, SWA_GROUP, SWA_DIM)

    def band(u):
        uc_ = u.reshape(bsz, nc, CHUNK, SWA_KV_HEADS, SWA_DIM)
        up = jnp.pad(uc_, ((0, 0), (w - 1, 0), (0, 0), (0, 0), (0, 0)))
        return jnp.concatenate([up[:, j:j + nc] for j in range(w)], axis=2)

    kb, vb = band(k), band(v)
    s = jnp.einsum('bnikgd,bnjkd->bnkgij', qc, kb) * (SWA_DIM ** -0.5)
    qi = jnp.arange(CHUNK)[:, None]
    kj = jnp.arange(w * CHUNK)[None, :]
    dist = jnp.abs(qi + (w - 1) * CHUNK - kj).astype(F32)
    slopes = jnp.exp2(-8.0 * jnp.arange(1, SWA_Q_HEADS + 1, dtype=F32) / SWA_Q_HEADS)
    s = s - slopes.reshape(SWA_KV_HEADS, SWA_GROUP, 1, 1) * dist
    key_chunk = jnp.arange(nc)[:, None] - (w - 1) + jnp.arange(w * CHUNK)[None, :] // CHUNK
    s = jnp.where((key_chunk >= 0)[None, :, None, None, None, :], s, -jnp.inf)
    sink = jnp.broadcast_to(sinks.astype(F32).reshape(SWA_KV_HEADS, SWA_GROUP, 1, 1),
                            s.shape[:-1] + (1,))
    p = jax.nn.softmax(jnp.concatenate([s, sink], -1), axis=-1)[..., :-1]
    o = jnp.einsum('bnkgij,bnjkd->bnikgd', p, vb)
    return o.reshape(bsz, t, SWA_Q_HEADS * SWA_DIM).astype(uc.dtype)

def setup_inputs(seed: int = 0) -> dict:
    key = jax.random.key(seed)
    ks = iter(jax.random.split(key, 48))
    L, D = DEPTH, D_MODEL

    def nrm(shape, scale):
        return jax.random.normal(next(ks), shape, F32) * scale

    def unif(shape, lo, hi):
        return jax.random.uniform(next(ks), shape, F32, lo, hi)

    dt = jnp.exp(unif((L, GDN_HEADS), math.log(1e-3), math.log(1e-1)))
    return {
        "x": nrm((BATCH, SEQ, D), 1.0),
        "w_in": nrm((L, D, N_IN), D ** -0.5),
        "gdn_conv": nrm((L, CONV_WIDTH, 3 * GDN_WIDTH), CONV_WIDTH ** -0.5),
        "gdn_a_log": jnp.log(unif((L, GDN_HEADS), 1.0, 16.0)),
        "gdn_dt_bias": dt + jnp.log(-jnp.expm1(-dt)),
        "gdn_norm_w": 1.0 + nrm((L, GDN_DIM), 0.05),
        "rwkv_mu": unif((L, sum(B_COLS)), 0.0, 1.0),
        "rwkv_w0": unif((L, RWKV_WIDTH), -6.0, 0.0),
        "rwkv_w_up": nrm((L, RWKV_DECAY_RANK, RWKV_WIDTH), RWKV_DECAY_RANK ** -0.5),
        "rwkv_a0": nrm((L, RWKV_WIDTH), 0.1),
        "rwkv_a_up": nrm((L, RWKV_A_RANK, RWKV_WIDTH), RWKV_A_RANK ** -0.5),
        "rwkv_g_up": nrm((L, RWKV_G_RANK, RWKV_WIDTH), RWKV_G_RANK ** -0.5),
        "rwkv_k_k": 0.85 + nrm((L, RWKV_WIDTH), 0.05),
        "rwkv_k_a": 1.0 + nrm((L, RWKV_WIDTH), 0.05),
        "rwkv_r_k": nrm((L, RWKV_HEADS, RWKV_DIM), 0.1),
        "rwkv_lnx_w": 1.0 + nrm((L, RWKV_WIDTH), 0.05),
        "rwkv_lnx_b": nrm((L, RWKV_WIDTH), 0.02),
        "rwkv_vres_down": nrm((L - 1, D, RWKV_V_RANK), D ** -0.5),
        "rwkv_vres_up": nrm((L - 1, RWKV_V_RANK, RWKV_WIDTH), RWKV_V_RANK ** -0.5),
        "rwkv_v0": nrm((L - 1, RWKV_WIDTH), 0.5),
        "swa_sinks": nrm((L, SWA_Q_HEADS), 0.5),
        "w_branch_a": nrm((L, GDN_WIDTH, D), GDN_WIDTH ** -0.5),
        "w_branch_b": nrm((L, RWKV_WIDTH, D), RWKV_WIDTH ** -0.5),
        "w_branch_c": nrm((L, SWA_Q_HEADS * SWA_DIM, D), (SWA_Q_HEADS * SWA_DIM) ** -0.5),
        "w_out": nrm((L, D, D), DEEPNORM_BETA * D ** -0.5),
        "ln1_w": 1.0 + nrm((L, D), 0.02),
        "ln1_b": nrm((L, D), 0.02),
        "ffn_gate": nrm((L, D, D_FF), D ** -0.5),
        "ffn_up": nrm((L, D, D_FF), D ** -0.5),
        "ffn_down": nrm((L, D_FF, D), DEEPNORM_BETA * D_FF ** -0.5),
        "ln2_w": 1.0 + nrm((L, D), 0.02),
        "ln2_b": nrm((L, D), 0.02),
    }

def reference(x, w_in, gdn_conv, gdn_a_log, gdn_dt_bias, gdn_norm_w, rwkv_mu, rwkv_w0, rwkv_w_up,
              rwkv_a0, rwkv_a_up, rwkv_g_up, rwkv_k_k, rwkv_k_a, rwkv_r_k, rwkv_lnx_w, rwkv_lnx_b,
              rwkv_vres_down, rwkv_vres_up, rwkv_v0, swa_sinks, w_branch_a, w_branch_b, w_branch_c,
              w_out, ln1_w, ln1_b, ffn_gate, ffn_up, ffn_down, ln2_w, ln2_b):
    bsz, t, d = x.shape
    v_first = None
    for l in range(DEPTH):
        u = x @ w_in[l]
        ua, ub, uc, ug = _split(u, GROUP_COLS)
        oa = _gdn_branch(ua, gdn_conv[l], gdn_a_log[l], gdn_dt_bias[l], gdn_norm_w[l])
        vres = None if l == 0 else (rwkv_vres_down[l - 1], rwkv_vres_up[l - 1], rwkv_v0[l - 1])
        ob, v_first = _rwkv7_branch(ub, x, rwkv_mu[l], rwkv_w0[l], rwkv_w_up[l], rwkv_a0[l],
                                    rwkv_a_up[l], rwkv_g_up[l], rwkv_k_k[l], rwkv_k_a[l],
                                    rwkv_r_k[l], rwkv_lnx_w[l], rwkv_lnx_b[l], v_first, vres)
        oc = _swa_branch(uc, swa_sinks[l])
        gates = jax.nn.sigmoid(ug).reshape(bsz, t, N_BRANCH, d)
        merged = (gates[:, :, 0] * (oa @ w_branch_a[l]) + gates[:, :, 1] * (ob @ w_branch_b[l])
                  + gates[:, :, 2] * (oc @ w_branch_c[l]))
        x = _layer_norm(ALPHA * x + merged @ w_out[l], ln1_w[l], ln1_b[l])
        hid = jax.nn.silu(x @ ffn_gate[l]) * (x @ ffn_up[l])
        x = _layer_norm(ALPHA * x + hid @ ffn_down[l], ln2_w[l], ln2_b[l])
    return x


_drawn_inputs = setup_inputs


def setup_inputs(seed=0):
    import zlib

    import numpy as np

    out = dict(_drawn_inputs(seed))
    spreads = {}
    factors = {'gdn_a_log': 4.576,
     'gdn_norm_w': 5.977,
     'rwkv_w_up': 7.82,
     'rwkv_a0': 8.0,
     'rwkv_k_k': 36.107,
     'rwkv_k_a': 7.187,
     'rwkv_lnx_w': 7.757,
     'rwkv_lnx_b': 30.915,
     'swa_sinks': 22.292,
     'ln1_w': 2.688,
     'ln1_b': 2.668,
     'ln2_w': 7.675,
     'ln2_b': 8.019}
    for name, (base, spread) in spreads.items():
        noise = np.random.default_rng([zlib.crc32(name.encode()), seed]).standard_normal(out[name].shape)
        drawn = base * np.exp(spread * noise) if base else spread * noise
        out[name] = jnp.asarray(drawn.astype(out[name].dtype))
    for name, factor in factors.items():
        out[name] = (out[name] * factor).astype(out[name].dtype)
    return out
```

```python
import math
from contextlib import ExitStack

import numpy as np

import concourse.bass as bass
from concourse import mybir

F32 = mybir.dt.float32
F32R = mybir.dt.float32r
ALU = mybir.AluOpType
ACT = mybir.ActivationFunctionType
AX = mybir.AxisListType

P = 128
D = 1024
T = 1024
KT = D // P
HALF = 512
C = 64
NCH = T // C
GH, GD = 4, 128
RH, RD = 8, 64
SH, SKV, SD = 8, 2, 64
FF = 2816
ALPHA = 2 ** 0.25
LN_EPS, GDN_EPS, LNX_EPS, L2_EPS = 1e-5, 1e-6, 64e-5, 1e-6

A_TILES = 16
SMALL = A_TILES * P
REST = SMALL + 2 * GH
N_IN = 7688
ALL_TILES = (N_IN - 2 * GH) // P
U_Q, U_K, U_V, U_Z = 0, 4, 8, 12
U_R, U_RK, U_RV, U_WA, U_G = 16, 20, 24, 28, 29
U_SQ, U_SK, U_SV, U_GATE = 30, 34, 35, 36
U_SMALL = ALL_TILES

O_A, O_R, O_B, O_K, O_V, O_GKB, O_GQ, O_GK, O_GQD, O_GV = range(10)
N_OP = 10
R_GC, R_NBEG, R_TAIL, R_BETA, R_EG = range(5)
NPAIR = 6
NB = 32


def constants():
    at, cols, out = {}, 0, []

    def put(name, a):
        nonlocal cols
        a = np.asarray(a, np.float32)
        at[name] = (cols, a.shape[1])
        cols += a.shape[1]
        out.append(a)

    r, c = np.arange(P)[:, None], np.arange(P)[None, :]
    put("ident", r == c)
    put("ones", np.ones((P, P)))
    put("head_ones", r // 64 == c // 64)
    s, t = np.arange(P)[:, None] % C, np.arange(C)[None, :]
    put("ident2", s == t)
    put("strict", t > s)
    put("causal", t >= s)
    put("minus_strict", -1.0 * (t > s))
    put("causal_again", t >= s)
    put("corner", (s < 32) & (t >= 32))
    put("in_chunk", np.broadcast_to(np.arange(T) % C != 0, (P, T)))
    q, k = np.arange(P)[:, None] % C, np.arange(2 * C)[None, :]
    for first in (0, 1):
        for j in range(4):
            head = 2 * j + np.arange(P)[:, None] // C
            m = -np.exp2(-8.0 * (head + 1) / SH) * np.abs(q + C - k)
            put(f"alibi{first}{j}", np.where((k < C) & (first == 1), -1e30, m))
    return at, np.concatenate(out, axis=1)


CONST_AT, CONST = constants()


class Tables:

    def __init__(self, tile):
        self.tile = tile

    def __call__(self, name, n=None, rows=P):
        at, width = CONST_AT[name]
        return self.tile[0:rows, at:at + (n or width)]


class Phase(ExitStack):

    def __init__(self, nc):
        super().__init__()
        self.nc, self.sems = nc, []

    def sem(self, name):
        self.sems.append(self.enter_context(self.nc.semaphore(name)))
        return self.sems[-1]

    def open_block(self):
        self.callback(self.clear)
        return self.enter_context(self.nc.Block())

    def clear(self):
        with self.nc.Block() as block:
            @block.gpsimd
            def _(pool):
                for s in self.sems:
                    pool.sem_clear(s)


def turn(eng, turns):
    eng.sem_inc(turns, 1)


def split_dot(pe, out, w_hi, w_lo, x_hi, x_lo, first, last):
    pe.matmul(out, w_hi, x_hi, start=first, stop=False)
    pe.matmul(out, w_hi, x_lo, start=False, stop=False)
    return pe.matmul(out, w_lo, x_hi, start=False, stop=last)


def as_f32(t):
    return t.bitcast(F32)


def transpose_x(nc, x, xin, xhi, xlo, tab, const_dram=None, scaled=None):
    with Phase(nc) as local:
        tag = "" if scaled is None else "1"
        bank = [local.enter_context(nc.psum_tensor(f"xt{tag}{b}", [P, HALF], F32)) for b in range(8)]
        landed = [local.sem(f"x_landed{tag}_{i}") for i in range(8)]
        const_landed = local.sem("const_landed" + tag)
        turned = local.sem("x_turned" + tag)
        hi_done = local.sem("x_hi_done" + tag)
        lo_done = local.sem("x_lo_done" + tag)
        block = local.open_block()

        @block.sync
        def _(sp):
            if const_dram is not None:
                sp.dma_start(tab.tile[:, :], const_dram).then_inc(const_landed, 16)
            for i in range(8):
                sp.dma_start(xin[:, i, :], x[i * P:(i + 1) * P, :]).then_inc(landed[i], 16)

        @block.tensor
        def _(pe):
            if const_dram is not None:
                pe.wait_ge(const_landed, 16)
            for n in range(16):
                half, k = n // 8, n % 8
                if k == 0:
                    for i in range(4):
                        pe.wait_ge(landed[4 * half + i], 16)
                if n >= 8:
                    pe.wait_ge(lo_done, n - 7)
                for i in range(4):
                    last = pe.transpose(bank[n % 8][:, i * P:(i + 1) * P],
                                        xin[:, 4 * half + i, k * P:(k + 1) * P], tab("ident"))
                last.then_inc(turned, 1)

        @block.scalar
        def _(act):
            for n in range(16):
                half, k = n // 8, n % 8
                act.wait_ge(turned, n + 1)
                act.activation(xhi[:, k, half * HALF:(half + 1) * HALF], bank[n % 8][:, :],
                               ACT.Copy).then_inc(hi_done, 1)

        @block.vector
        def _(dve):
            for n in range(16):
                half, k = n // 8, n % 8
                cols = slice(half * HALF, (half + 1) * HALF)
                dve.wait_ge(hi_done, n + 1)
                dve.tensor_tensor(xlo[:, k, cols], bank[n % 8][:, :], as_f32(xhi[:, k, cols]),
                                  ALU.subtract).then_inc(lo_done, 1)
                if scaled is not None and k == KT - 1:
                    dve.tensor_scalar(xin[:, 4 * half:4 * half + 4, :], xin[:, 4 * half:4 * half + 4, :], scaled, None, ALU.mult)


def project_in(nc, w_in, xhi, xlo, u):
    W = 2 * P
    w_rows = w_in.rearrange("(k p) n -> p k n", p=P)
    u_rows = u.rearrange("(n p) t -> p n t", p=P)
    with Phase(nc) as local:
        raw = [local.enter_context(nc.sbuf_tensor(f"w_raw{b}", [P, KT, W], F32)) for b in range(2)]
        whi = [local.enter_context(nc.sbuf_tensor(f"w_hi{b}", [P, KT, W], F32R)) for b in range(2)]
        wlo = [local.enter_context(nc.sbuf_tensor(f"w_lo{b}", [P, KT, W], F32R)) for b in range(2)]
        res = [local.enter_context(nc.sbuf_tensor(f"u_out{b}", [P, 2, T], F32)) for b in range(2)]
        bank = [[local.enter_context(nc.psum_tensor(f"u_ps{b}{a}", [P, 2, HALF], F32))
                 for a in range(2)] for b in range(2)]
        sem = lambda name: local.sem(name)
        landed = [sem(f"w_landed{b}") for b in range(2)]
        stored = [sem(f"u_stored{b}") for b in range(2)]
        hi_done, lo_done, mm_done, evacuated = sem("w_hi_done"), sem("w_lo_done"), sem("u_mm_done"), sem("u_evac")
        block = local.open_block()

        LOOPS = ((0, 0, A_TILES // 4), (REST, A_TILES, (U_GATE - A_TILES) // 4))

        def loads(eng, step):
            j0 = 0
            for col0, row0, n in LOOPS:
                with eng.Fori(0, n) as i:
                    for b in range(2):
                        step(i * 2 + (2 * j0 + b), i + j0, b, i * (2 * W) + (col0 + b * W),
                             i * 4 + (row0 + 2 * b), 2)
                j0 += n
            step(2 * j0, j0, 0, REST - P, U_SMALL, 1)

        @block.sync
        def _(sp):
            def step(m, j, b, col, row, tiles):
                sp.wait_ge(hi_done, m + 1)
                sp.wait_ge(lo_done, m + 1)
                sp.dma_start(raw[b][:, :, 0:tiles * P],
                             w_rows[:, :, bass.ds(col, tiles * P)]).then_inc(landed[b], 16)
            loads(sp, step)

        @block.vector
        def _(dve):
            dve.sem_inc(hi_done, 2)
            dve.sem_inc(lo_done, 2)

            def step(m, j, b, col, row, tiles):
                n = slice(0, tiles * P)
                dve.wait_ge(landed[b], j * 16 + 16)
                dve.wait_ge(mm_done, m * 2 + 2)
                dve.tensor_copy(whi[b][:, :, n], raw[b][:, :, n]).then_inc(hi_done, 1)
                dve.wait_ge(hi_done, m + 3)
                dve.tensor_tensor(wlo[b][:, :, n], raw[b][:, :, n], as_f32(whi[b][:, :, n]),
                                  ALU.subtract).then_inc(lo_done, 1)
            loads(dve, step)

        @block.tensor
        def _(pe):
            pe.sem_inc(mm_done, 4)

            def step(m, j, b, col, row, tiles):
                pe.wait_ge(lo_done, m + 3)
                for a in range(tiles):
                    pe.wait_ge(evacuated, m * 2 + (a + 1))
                    for k in range(KT):
                        for h in range(2):
                            last = split_dot(pe, bank[b][a][:, h, :],
                                             whi[b][:, k, a * P:(a + 1) * P], wlo[b][:, k, a * P:(a + 1) * P],
                                             xhi[:, k, h * HALF:(h + 1) * HALF], xlo[:, k, h * HALF:(h + 1) * HALF],
                                             k == 0, k == KT - 1)
                    last.then_inc(mm_done, 1)
            loads(pe, step)

        @block.scalar
        def _(act):
            act.sem_inc(evacuated, 4)
            for b in range(2):
                act.sem_inc(stored[b], 16)

            def step(m, j, b, col, row, tiles):
                act.wait_ge(stored[b], j * 16 + 16)
                for a in range(tiles):
                    act.wait_ge(mm_done, m * 2 + (a + 5))
                    act.activation(res[b][:, a, :], bank[b][a][:, :, :].rearrange("p h t -> p (h t)"),
                                   ACT.Copy).then_inc(evacuated, 1)
                act.wait_ge(evacuated, m * 2 + (tiles + 4))
                act.dma_start(u_rows[:, bass.ds(row, tiles), :], res[b][:, 0:tiles, :]).then_inc(stored[b], 16)
            loads(act, step)
            for b in range(2):
                act.wait_ge(stored[b], 16 * (2 + sum(n for _, _, n in LOOPS) - b))


class GateColumns:

    def __init__(self, nc, local, w_in, u, xhi, xlo, first, count, per):
        self.nc, self.w_in, self.u, self.xhi, self.xlo = nc, w_in, u, xhi, xlo
        self.first, self.count, self.per = first, count, per
        sb = lambda name, shape, dt=F32: [local.enter_context(nc.sbuf_tensor(f"{name}{first}_{b}", shape, dt)) for b in range(2)]
        sem = lambda name: local.sem(f"{name}{first}")
        self.raw, self.whi, self.wlo = sb("gc_raw", [P, KT, P]), sb("gc_hi", [P, KT, P], F32R), sb("gc_lo", [P, KT, P], F32R)
        self.res = sb("gc_res", [P, T])
        self.bank = [local.enter_context(nc.psum_tensor(f"gc_ps{first}_{h}", [P, HALF], F32)) for h in range(2)]
        self.landed, self.stored = [sem(f"gc_landed{b}_") for b in range(2)], [sem(f"gc_stored{b}_") for b in range(2)]
        self.hi_done, self.lo_done, self.mm_done, self.evacuated, self.turns = (
            sem("gc_" + n) for n in ("hi_done", "lo_done", "mm_done", "evacuated", "turns"))

    def load(self, act, m, b):
        w_rows = self.w_in.rearrange("(k p) n -> p k n", p=P)
        col0 = REST + (self.first - A_TILES) * P
        act.dma_start(self.raw[b][:, :, :], w_rows[:, :, bass.ds(m * P + col0, P)]).then_inc(self.landed[b], 16)

    def pool_program(self, pool):
        with pool.Fori(0, self.count // 2) as i:
            for b in range(2):
                m = i * 2 + b
                pool.wait_ge(self.landed[b], i * 16 + 16)
                pool.wait_ge(self.mm_done, m * 2 + 2)
                turn(pool, self.turns)
                pool.tensor_copy(self.whi[b][:, :, :], self.raw[b][:, :, :]).then_inc(self.hi_done, 1)
                pool.wait_ge(self.hi_done, m + 1)
                pool.tensor_tensor(self.wlo[b][:, :, :], self.raw[b][:, :, :], as_f32(self.whi[b][:, :, :]),
                                   ALU.subtract).then_inc(self.lo_done, 1)

    def pe_begin(self, pe):
        pe.sem_inc(self.mm_done, 4)

    def pe_tile(self, pe, i, q):
        m, b = i * self.per + q, q % 2
        pe.wait_ge(self.lo_done, m + 1)
        for h in range(2):
            pe.wait_ge(self.evacuated, m * 2 + (h + 1))
            for k in range(KT):
                cols = slice(h * HALF, (h + 1) * HALF)
                last = split_dot(pe, self.bank[h][:, :], self.whi[b][:, k, :], self.wlo[b][:, k, :],
                                 self.xhi[:, k, cols], self.xlo[:, k, cols], k == 0, k == KT - 1)
            last.then_inc(self.mm_done, 1)

    def act_begin(self, act):
        for b in range(2):
            self.load(act, b, b)
        act.sem_inc(self.evacuated, 2)
        for b in range(2):
            act.sem_inc(self.stored[b], 16)

    def act_tile(self, act, i, q, last_round):
        m, b = i * self.per + q, q % 2
        act.wait_ge(self.stored[b], i * (16 * self.per // 2) + (16 * (q // 2) + 16))
        for h in range(2):
            act.wait_ge(self.mm_done, m * 2 + (h + 5))
            act.activation(self.res[b][:, h * HALF:(h + 1) * HALF], self.bank[h][:, :], ACT.Copy).then_inc(self.evacuated, 1)
        if not (last_round and q + 2 >= self.per):
            self.load(act, m + 2, b)
        act.wait_ge(self.evacuated, m * 2 + 4)
        act.dma_start(self.u[bass.ds(m * P + self.first * P, P), :], self.res[b][:, :]).then_inc(self.stored[b], 16)

    def act_end(self, act):
        for b in range(2):
            act.wait_ge(self.stored[b], 16 + 16 * self.count // 2)


PARAMS = {}


def _params():
    at = 0
    for name, n in (("mu", 14), ("w0", 4), ("a0", 4), ("k_k", 4), ("k_a", 4), ("r_k", 4), ("lnx_w", 4),
                    ("lnx_b", 4), ("conv", 48), ("norm_w", 1), ("a_log", 1), ("dt_bias", 1), ("sinks", 4),
                    ("one_minus_k_a", 4), ("minus_a", 1), ("eps_q", 1), ("eps_k", 1), ("eps_gdn", 1), ("eps_lnx", 1), ("eps_ln", 1)):
        PARAMS[name] = (at, n)
        at += n
    return at


N_PARAM = _params()


class Params:

    def __init__(self, tile):
        self.tile = tile

    def __call__(self, name, j=0, n=1, rows=P):
        return self.tile[0:rows, bass.ds(PARAMS[name][0] + j, n)]


def load_params(nc, sp, par, A, landed):
    n = 0

    def load(name, src, rows=slice(0, P)):
        nonlocal n
        at, width = PARAMS[name]
        sp.dma_start(par.tile[rows, at:at + width] if src.ndim == 2 else src, src).then_inc(landed, 16)
        n += 16

    with nc.allow_non_contiguous_dma(reason="parameters, once"):
        load("mu", A["rwkv_mu"][0].rearrange("(j p) -> p j", p=P))
        for name in ("w0", "a0", "k_k", "k_a", "lnx_w", "lnx_b"):
            load(name, A["rwkv_" + name][0].rearrange("(j p) -> p j", p=P))
        load("r_k", A["rwkv_r_k"][0].rearrange("(j e) d -> (e d) j", e=2))
        at = PARAMS["conv"][0]
        for tap in range(4):
            sp.dma_start(par.tile[:, at + 12 * tap:at + 12 * tap + 12],
                         A["gdn_conv"][0, tap].rearrange("(j p) -> p j", p=P)).then_inc(landed, 16)
            n += 16
        load("norm_w", A["gdn_norm_w"].rearrange("o p -> p o"))
        load("a_log", A["gdn_a_log"].rearrange("o p -> p o"), slice(0, GH))
        load("dt_bias", A["gdn_dt_bias"].rearrange("o p -> p o"), slice(0, GH))
        sinks = A["swa_sinks"].rearrange("o (j e) -> o e j", e=2)
        for e in range(2):
            load("sinks", sinks[:, e, :].to_broadcast([64, 4]), slice(64 * e, 64 * e + 64))
    return n


class Chain:

    def __init__(self, eng, sem, base=0):
        self.eng, self.sem, self.base, self.n = eng, sem, base, 0

    def __call__(self, instruction):
        instruction.then_inc(self.sem, 1)
        self.n += 1
        self.eng.wait_ge(self.sem, self.base + self.n)


def prepare_rows(nc, u, rows, egl, par, tab, wa, gl):
    with Phase(nc) as local:
        sb = lambda name, shape: local.enter_context(nc.sbuf_tensor(name, shape, F32))
        sem = lambda name: local.sem(name)
        r = {n: sb("row_" + n, [GH, T]) for n in ("b", "a", "x", "y", "u", "d", "z", "gc", "beta", "eg", "nbeg", "tail")}
        el = sb("row_el", [GH, NCH])
        uw, ug, dw = sb("uw", [P, 1 + T]), sb("ug", [P, 1 + T]), sb("dw", [P, T])
        landed_rows, landed_w, dve_step, act_step = sem("rows_landed"), sem("wg_landed"), sem("rows_dve"), sem("rows_act")
        stored, shifted = sem("rows_stored"), sem("wg_shifted")
        x_ready, y_ready, gc_ready, gc_exp_ready, b_ready, tail_ready = (
            sem(n) for n in ("x_ready", "y_ready", "gc_ready", "gc_exp_ready", "beta_ready", "tail_arg_ready"))
        rows_ready, tail_exp = sem("rows_ready"), sem("tail_exp")
        block = local.open_block()
        chunks = lambda t: t[:, :].rearrange("p (c s) -> p c s", s=C)

        @block.sync
        def _(sp):
            sp.dma_start(r["b"][:, :], u[U_SMALL * P + P - 2 * GH:U_SMALL * P + P - GH, :]).then_inc(landed_rows, 16)
            sp.dma_start(r["a"][:, :], u[U_SMALL * P + P - GH:U_SMALL * P + P, :]).then_inc(landed_rows, 16)
            sp.dma_start(uw[:, 1:], u[U_WA * P:(U_WA + 1) * P, :]).then_inc(landed_w, 16)
            sp.dma_start(ug[:, 1:], u[U_G * P:(U_G + 1) * P, :]).then_inc(landed_w, 16)
            sp.wait_ge(rows_ready, 1)
            sp.wait_ge(tail_exp, 2)
            for n, name in ((R_GC, "gc"), (R_NBEG, "nbeg"), (R_TAIL, "tail"), (R_BETA, "beta"), (R_EG, "eg")):
                sp.dma_start(rows[n], r[name][:, :]).then_inc(stored, 16)
            sp.dma_start(egl, el[:, :]).then_inc(stored, 16)
            sp.wait_ge(stored, 96)

        @block.vector
        def _(dve):
            step = Chain(dve, dve_step)
            dve.memset(uw[:, 0:1], 0.0)
            step(dve.memset(ug[:, 0:1], 0.0))
            step(dve.tensor_scalar(par("one_minus_k_a", 0, 4), par("k_a", 0, 4), -1.0, 1.0, ALU.mult, ALU.add))
            dve.memset(par("eps_q"), GD * L2_EPS)
            for name, value in (("eps_k", L2_EPS), ("eps_gdn", GDN_EPS), ("eps_lnx", LNX_EPS), ("eps_ln", LN_EPS)):
                step(dve.memset(par(name), value))
            dve.wait_ge(act_step, 1)
            step(dve.tensor_scalar(par("minus_a", rows=GH), par("minus_a", rows=GH), -1.0, None, ALU.mult))
            dve.wait_ge(landed_rows, 32)
            step(dve.tensor_scalar(r["x"][:, :], r["a"][:, :], par("dt_bias", rows=GH), None, ALU.add))
            step(dve.tensor_scalar(r["z"][:, :], r["x"][:, :], -1.0, None, ALU.mult))
            dve.tensor_tensor(r["z"][:, :], r["x"][:, :], r["z"][:, :], ALU.min).then_inc(x_ready, 1)
            dve.wait_ge(y_ready, 1)
            step(dve.tensor_scalar(r["u"][:, :], r["y"][:, :], 1.0, None, ALU.add))
            step(dve.tensor_scalar(r["d"][:, :], r["u"][:, :], -1.0, None, ALU.add))
            step(dve.tensor_scalar(r["z"][:, :], r["d"][:, :], 0.0, None, ALU.is_equal))
            dve.wait_ge(y_ready, 2)
            step(dve.tensor_tensor(r["d"][:, :], r["d"][:, :], r["z"][:, :], ALU.add))
            step(dve.reciprocal(r["d"][:, :], r["d"][:, :]))
            step(dve.tensor_tensor(r["a"][:, :], r["a"][:, :], r["z"][:, :], ALU.add))
            step(dve.tensor_tensor(r["a"][:, :], r["a"][:, :], r["d"][:, :], ALU.mult))
            step(dve.tensor_tensor(r["a"][:, :], r["a"][:, :], r["y"][:, :], ALU.mult))
            step(dve.scalar_tensor_tensor(r["a"][:, :], r["x"][:, :], 0.0, r["a"][:, :], ALU.max, ALU.add))
            step(dve.tensor_scalar(r["a"][:, :], r["a"][:, :], par("minus_a", rows=GH), None, ALU.mult))
            dve.tensor_tensor_scan(r["gc"][:, :], tab("in_chunk", rows=GH), r["a"][:, :], 0.0,
                                   ALU.mult, ALU.add).then_inc(gc_ready, 1)
            dve.wait_ge(gc_ready, 1)
            dve.tensor_tensor(chunks(r["tail"]), chunks(r["gc"])[:, :, C - 1:C].to_broadcast([GH, NCH, C]),
                              chunks(r["gc"]), ALU.subtract).then_inc(tail_ready, 1)
            dve.wait_ge(gc_exp_ready, 1)
            dve.wait_ge(b_ready, 1)
            dve.scalar_tensor_tensor(r["nbeg"][:, :], r["beta"][:, :], -1.0, r["eg"][:, :],
                                     ALU.mult, ALU.mult).then_inc(rows_ready, 1)
            dve.wait_ge(landed_w, 32)
            for raw, out, j in ((uw, wa, 12), (ug, gl, 13)):
                step(dve.tensor_tensor(dw[:, :], raw[:, 0:T], raw[:, 1:], ALU.subtract))
                step(dve.scalar_tensor_tensor(out[:, :], dw[:, :], par("mu", j), raw[:, 1:], ALU.mult, ALU.add))
            dve.sem_inc(shifted, 1)

        @block.scalar
        def _(act):
            act.activation(par("minus_a", rows=GH), par("a_log", rows=GH), ACT.Exp).then_inc(act_step, 1)
            act.wait_ge(x_ready, 1)
            act.activation(r["y"][:, :], r["z"][:, :], ACT.Exp).then_inc(y_ready, 1)
            act.wait_ge(y_ready, 1)
            act.activation(r["a"][:, :], r["y"][:, :], ACT.Ln, bias=1.0).then_inc(y_ready, 1)
            act.wait_ge(gc_ready, 1)
            act.activation(r["eg"][:, :], r["gc"][:, :], ACT.Exp).then_inc(gc_exp_ready, 1)
            act.activation(el[:, :], chunks(r["gc"])[:, :, C - 1], ACT.Exp).then_inc(tail_exp, 1)
            act.wait_ge(tail_ready, 1)
            act.activation(r["tail"][:, :], r["tail"][:, :], ACT.Exp).then_inc(tail_exp, 1)
            act.wait_ge(landed_rows, 32)
            act.activation(r["beta"][:, :], r["b"][:, :], ACT.Sigmoid).then_inc(b_ready, 1)
            act.wait_ge(shifted, 1)
            act.activation(wa[0:64, :], wa[0:64, :], ACT.Tanh).then_inc(act_step, 1)
            act.activation(gl[:, :], gl[:, :], ACT.Sigmoid).then_inc(act_step, 1)
            act.wait_ge(act_step, 3)


def prepare_rwkv(nc, A, u, opnd, bonus, plast, par, tab, wa, xhi, xlo):
    E5 = -math.exp(-0.5)
    with Phase(nc) as local:
        sb = lambda name, shape: local.enter_context(nc.sbuf_tensor(name, shape, F32))
        sem = lambda name: local.sem(name)
        raw = [sb("raw_" + n, [P, 1 + T]) for n in "rkv"]
        low_up = sb("low_up", [P, P])
        t = {n: sb("rw_" + n, [P, T]) for n in
             ("d", "r", "k", "v", "sw", "a", "lc", "lp", "ep", "en", "ec", "kk", "nrm", "ao", "bo", "ko", "ro", "bonus")}
        t["sq"] = t["ep"]
        t["rk"] = t["bonus"]
        z_ps, a_ps, n_ps = (local.enter_context(nc.psum_tensor(n, [P, 2, HALF], F32)) for n in ("z_ps", "a_ps", "n_ps"))
        b_ps = z_ps
        gates = GateColumns(nc, local, A["w_in"][0], u, xhi, xlo, U_GATE, 16, 4)
        flat = lambda p: p[:, :, :].rearrange("p h t -> p (h t)")
        landed, up_landed, stored = [sem(f"rkv_landed{n}") for n in range(3)], sem("up_landed"), sem("rw_stored")
        low_done, sig_done, dve_step, lc_done, exp_done = (sem(n) for n in ("low_done", "sig_done", "rw_dve", "lc_done", "rw_exp_done"))
        kk0_done, sq_done, norm_mm, norm_done, rk_done, rk_mm, outs = (
            sem(n) for n in ("kk0_done", "sq_done", "norm_mm", "norm_done", "rk_done", "rk_mm", "rw_outs"))
        round_done, raw_used = sem("rw_round_done"), sem("raw_used")
        block = local.open_block()
        STEPS = 20

        def opnd_part(n, j):
            return opnd[:, :, bass.ds(j * C + n * 256, C)].rearrange("c p s -> p c s")

        @block.sync
        def _(sp):
            sp.sem_inc(round_done, 1)

            def load(i):
                for n, row in enumerate((U_R, U_RK, U_RV)):
                    sp.dma_start(raw[n][:, 1:], u[bass.ds(i * P + row * P, P), :]).then_inc(landed[n], 16)
                sp.dma_start(low_up[0:64, :], A["rwkv_w_up"][0][:, bass.ds(i * P, P)]).then_inc(up_landed, 16)
                sp.dma_start(low_up[64:128, :], A["rwkv_a_up"][0][:, bass.ds(i * P, P)]).then_inc(up_landed, 16)

            def store(i):
                sp.wait_ge(outs, i + 2)
                for n, name in ((O_A, "ao"), (O_R, "ro"), (O_B, "bo"), (O_K, "ko"), (O_V, "v")):
                    sp.dma_start(opnd_part(n, i), t[name][:, :].rearrange("p (c s) -> p c s", s=C)).then_inc(stored, 16)
                sp.dma_start(bonus[bass.ds(i * P, P), :], t["bonus"][:, :]).then_inc(stored, 16)
                sp.wait_ge(stored, i * 96 + 96)
                sp.sem_inc(round_done, 1)
            load(0)
            with sp.Fori(0, 3) as i:
                sp.wait_ge(raw_used, i + 1)
                load(i + 1)
                store(i)
            store(3)

        @block.gpsimd
        def _(pool):
            gates.pool_program(pool)

        @block.tensor
        def _(pe):
            gates.pe_begin(pe)
            with pe.Fori(0, 4) as i:
                pe.wait_ge(up_landed, i * 32 + 32)
                pe.wait_ge(outs, i + 1)
                for h in range(2):
                    cols = slice(h * HALF, (h + 1) * HALF)
                    pe.matmul(z_ps[:, h, :], low_up[0:64, :], wa[0:64, cols], start=True, stop=True)
                    last = pe.matmul(a_ps[:, h, :], low_up[64:128, :], wa[64:128, cols], start=True, stop=True)
                last.then_inc(low_done, 1)
                gates.pe_tile(pe, i, 0)
                pe.wait_ge(sq_done, i + 1)
                for h in range(2):
                    last = pe.matmul(n_ps[:, h, :], tab("head_ones"), t["sq"][:, h * HALF:(h + 1) * HALF], start=True, stop=True)
                last.then_inc(norm_mm, 1)
                gates.pe_tile(pe, i, 1)
                pe.wait_ge(rk_done, i + 1)
                for h in range(2):
                    last = pe.matmul(b_ps[:, h, :], tab("head_ones"), t["rk"][:, h * HALF:(h + 1) * HALF], start=True, stop=True)
                last.then_inc(rk_mm, 1)
                gates.pe_tile(pe, i, 2)
                gates.pe_tile(pe, i, 3)

        @block.scalar
        def _(act):
            act.sem_inc(outs, 1)
            gates.act_begin(act)
            def one_round(i, last):
                act.wait_ge(low_done, i + 1)
                act.activation(t["sw"][:, :], flat(z_ps), ACT.Sigmoid, bias=par("w0", i)).then_inc(sig_done, 1)
                act.activation(t["a"][:, :], flat(a_ps), ACT.Sigmoid, bias=par("a0", i)).then_inc(sig_done, 1)
                act.wait_ge(kk0_done, i + 1)
                act.activation(t["sq"][:, :], t["kk"][:, :], ACT.Square).then_inc(sq_done, 1)
                gates.act_tile(act, i, 0, last)
                act.wait_ge(norm_mm, i + 1)
                act.activation(t["nrm"][:, :], flat(n_ps), ACT.Sqrt, bias=par("eps_k")).then_inc(norm_done, 1)
                act.wait_ge(lc_done, i + 1)
                act.activation(t["ep"][:, :], t["lp"][:, :], ACT.Exp).then_inc(exp_done, 1)
                act.activation(t["en"][:, :], t["lc"][:, :], ACT.Exp, scale=-1.0).then_inc(exp_done, 1)
                act.activation(t["ec"][:, :], t["lc"][:, :], ACT.Exp).then_inc(exp_done, 1)
                for q in (1, 2, 3):
                    gates.act_tile(act, i, q, last)
            with act.Fori(0, 4 - 1) as i:
                one_round(i, False)
            one_round(4 - 1, True)
            gates.act_end(act)

        @block.vector
        def _(dve):
            for n in range(3):
                dve.memset(raw[n][:, 0:1], 0.0).then_inc(dve_step, 1)
            dve.wait_ge(dve_step, 3)
            with dve.Fori(0, 4) as i:
                step = Chain(dve, dve_step, i * STEPS + 3)
                def shift(n, name):
                    dve.wait_ge(landed[n], i * 16 + 16)
                    step(dve.tensor_tensor(t["d"][:, :], raw[n][:, 0:T], raw[n][:, 1:], ALU.subtract))
                    step(dve.scalar_tensor_tensor(t[name][:, :], t["d"][:, :], par("mu", i + 4 * n), raw[n][:, 1:], ALU.mult, ALU.add))
                shift(0, "r")
                shift(1, "k")
                dve.tensor_scalar(t["kk"][:, :], t["k"][:, :], par("k_k", i), None, ALU.mult).then_inc(kk0_done, 1)
                dve.wait_ge(sig_done, i * 2 + 2)
                step(dve.tensor_scalar(t["sw"][:, :], t["sw"][:, :], E5, None, ALU.mult))
                step(dve.tensor_tensor_scan(t["lc"][:, :], tab("in_chunk"), t["sw"][:, :], 0.0, ALU.mult, ALU.add))
                dve.tensor_tensor(t["lp"][:, :], t["lc"][:, :], t["sw"][:, :], ALU.subtract).then_inc(lc_done, 1)
                step(dve.tensor_scalar(t["d"][:, :], t["a"][:, :], par("k_a", i), par("one_minus_k_a", i), ALU.mult, ALU.add))
                step(dve.tensor_tensor(t["k"][:, :], t["k"][:, :], t["d"][:, :], ALU.mult))
                step(dve.tensor_scalar(t["d"][:, :], t["r"][:, :], par("r_k", i), None, ALU.mult))
                dve.wait_ge(round_done, i + 1)
                dve.tensor_tensor(t["rk"][:, :], t["d"][:, :], t["k"][:, :], ALU.mult).then_inc(rk_done, 1)
                dve.wait_ge(rk_done, i + 1)
                shift(2, "v")
                dve.sem_inc(raw_used, 1)
                dve.wait_ge(norm_done, i + 1)
                step(dve.reciprocal(t["nrm"][:, :], t["nrm"][:, :]))
                step(dve.tensor_tensor(t["kk"][:, :], t["kk"][:, :], t["nrm"][:, :], ALU.mult))
                dve.wait_ge(exp_done, i * 3 + 3)
                step(dve.scalar_tensor_tensor(t["ao"][:, :], t["kk"][:, :], -1.0, t["ep"][:, :], ALU.mult, ALU.mult))
                step(dve.tensor_tensor(t["bo"][:, :], t["kk"][:, :], t["a"][:, :], ALU.mult))
                step(dve.tensor_tensor(t["bo"][:, :], t["bo"][:, :], t["en"][:, :], ALU.mult))
                step(dve.tensor_tensor(t["ko"][:, :], t["k"][:, :], t["en"][:, :], ALU.mult))
                step(dve.tensor_tensor(t["ro"][:, :], t["r"][:, :], t["ec"][:, :], ALU.mult))
                step(dve.tensor_copy(plast[:, bass.ds(i * NCH, NCH)], t["ec"][:, :].rearrange("p (c s) -> p c s", s=C)[:, :, C - 1]))
                dve.wait_ge(rk_mm, i + 1)
                step(dve.tensor_tensor(t["bonus"][:, :], flat(b_ps), t["v"][:, :], ALU.mult))
                assert step.n == STEPS
                dve.sem_inc(outs, 1)


def prepare_gdn(nc, A, u, rows, opnd, par, tab, xhi, xlo):
    with Phase(nc) as local:
        sb = lambda name, shape: local.enter_context(nc.sbuf_tensor(name, shape, F32))
        sem = lambda name: local.sem(name)
        raw = [sb("graw_" + n, [P, 3 + T]) for n in "qkv"]
        conv = [sb("conv_" + n, [P, T]) for n in "qkv"]
        out = {n: sb("g_" + n, [P, T]) for n in ("q", "k", "v", "qd", "kb")}
        sq, nrm = [sb(f"g_sq{n}", [P, T]) for n in range(2)], [sb(f"g_nrm{n}", [P, T]) for n in range(2)]
        eg, beta = sb("g_eg", [P, T]), sb("g_beta", [P, T])
        ps = [local.enter_context(nc.psum_tensor(f"g_ps{n}", [P, 2, HALF], F32)) for n in range(2)]
        landed, rows_landed, stored = [sem(f"g_landed{n}") for n in range(3)], sem("g_rows_landed"), sem("g_stored")
        conv_done, silu_done, sq_done, norm_mm, norm_done, dve_step, outs, round_done = (
            sem(n) for n in ("conv_done", "silu_done", "g_sq_done", "g_norm_mm", "g_norm_done", "g_dve", "g_outs", "g_round_done"))
        gates = GateColumns(nc, local, A["w_in"][0], u, xhi, xlo, U_GATE + 16, 8, 2)
        block = local.open_block()
        STEPS = 15

        @block.sync
        def _(sp):
            sp.sem_inc(round_done, 1)

            def load(i):
                for n, row in enumerate((U_Q, U_K, U_V)):
                    sp.dma_start(raw[n][:, 3:], u[bass.ds(i * P + row * P, P), :]).then_inc(landed[n], 16)

            def load_scales(i):
                for q, tile in ((R_EG, eg), (R_BETA, beta)):
                    sp.dma_start(tile[:, :], rows[q][bass.ds(i, 1), :].to_broadcast([P, T])).then_inc(rows_landed, 16)

            def store(i):
                for n, name in ((O_GQ, "q"), (O_GQD, "qd"), (O_GK, "k"), (O_GKB, "kb"), (O_GV, "v")):
                    sp.dma_start(opnd[:, :, bass.ds(i * C + n * 256, C)].rearrange("c p s -> p c s"),
                                 out[name][:, :].rearrange("p (c s) -> p c s", s=C)).then_inc(stored, 16)
                sp.wait_ge(stored, i * 80 + 80)
                sp.sem_inc(round_done, 1)
            load(0)
            load_scales(0)
            with sp.Fori(0, GH - 1) as i:
                sp.wait_ge(conv_done, i * 3 + 3)
                load(i + 1)
                sp.wait_ge(outs, i + 1)
                load_scales(i + 1)
                store(i)
            sp.wait_ge(outs, GH)
            store(GH - 1)

        @block.gpsimd
        def _(pool):
            gates.pool_program(pool)

        @block.tensor
        def _(pe):
            gates.pe_begin(pe)
            with pe.Fori(0, GH) as i:
                gates.pe_tile(pe, i, 0)
                for n in range(2):
                    pe.wait_ge(sq_done, i * 2 + n + 1)
                    for h in range(2):
                        last = pe.matmul(ps[n][:, h, :], tab("ones"), sq[n][:, h * HALF:(h + 1) * HALF], start=True, stop=True)
                    last.then_inc(norm_mm, 1)
                gates.pe_tile(pe, i, 1)

        @block.scalar
        def _(act):
            gates.act_begin(act)
            def one_round(i, last):
                act.wait_ge(round_done, i + 1)
                for n, name in enumerate("qkv"):
                    act.wait_ge(conv_done, i * 3 + n + 1)
                    act.activation(out[name][:, :], conv[n][:, :], ACT.Silu).then_inc(silu_done, 1)
                act.wait_ge(silu_done, i * 3 + 3)
                for n, name in enumerate("qk"):
                    act.activation(sq[n][:, :], out[name][:, :], ACT.Square).then_inc(sq_done, 1)
                gates.act_tile(act, i, 0, last)
                for n, name in enumerate("qk"):
                    act.wait_ge(norm_mm, i * 2 + n + 1)
                    act.activation(nrm[n][:, :], ps[n][:, :, :].rearrange("p h t -> p (h t)"), ACT.Sqrt,
                                   bias=par("eps_" + name), scale=float(GD) if n == 0 else 1.0).then_inc(norm_done, 1)
                gates.act_tile(act, i, 1, last)
            with act.Fori(0, GH - 1) as i:
                one_round(i, False)
            one_round(GH - 1, True)
            gates.act_end(act)

        @block.vector
        def _(dve):
            for n in range(3):
                dve.memset(raw[n][:, 0:3], 0.0).then_inc(dve_step, 1)
            dve.wait_ge(dve_step, 3)
            with dve.Fori(0, GH) as i:
                step = Chain(dve, dve_step, i * STEPS + 3)
                for n in range(3):
                    dve.wait_ge(landed[n], i * 16 + 16)
                    tap = lambda k: par("conv", i + (12 * k + 4 * n))
                    step(dve.tensor_scalar(conv[n][:, :], raw[n][:, 3:], tap(3), None, ALU.mult))
                    for k in (2, 1):
                        step(dve.scalar_tensor_tensor(conv[n][:, :], raw[n][:, k:k + T], tap(k), conv[n][:, :], ALU.mult, ALU.add))
                    dve.scalar_tensor_tensor(conv[n][:, :], raw[n][:, 0:T], tap(0), conv[n][:, :], ALU.mult, ALU.add).then_inc(conv_done, 1)
                dve.wait_ge(silu_done, i * 3 + 3)
                dve.wait_ge(rows_landed, i * 32 + 32)
                for n, (name, other, scale) in enumerate((("q", "qd", eg), ("k", "kb", beta))):
                    dve.wait_ge(norm_done, i * 2 + n + 1)
                    step(dve.reciprocal(nrm[n][:, :], nrm[n][:, :]))
                    step(dve.tensor_tensor(out[name][:, :], out[name][:, :], nrm[n][:, :], ALU.mult))
                    step(dve.tensor_tensor(out[other][:, :], out[name][:, :], scale[:, :], ALU.mult))
                assert step.n == STEPS
                dve.sem_inc(outs, 1)


def prepare_decays(nc, rows, egl, gates_tile, cols, egl_bc, tab):
    with Phase(nc) as local:
        sb = lambda name, shape: local.enter_context(nc.sbuf_tensor(name, shape, F32))
        sem = lambda name: local.sem(name)
        along, col = sb("gc_along", [P, NCH, 2, C]), sb("gc_col", [P, NCH, 2])
        landed, step_done, exp_done = sem("gc_landed"), sem("gc_step"), sem("gc_exp")
        block = local.open_block()

        @block.sync
        def _(sp):
            n = 0
            with nc.allow_non_contiguous_dma(reason="one value per head and token, once"):
                for e in range(2):
                    half = slice(64 * e, 64 * e + 64)
                    for p in range(2):
                        row = rows[R_GC, 2 * p + e].rearrange("(c s) -> c s", s=C)
                        sp.dma_start(along[half, :, p, :], row.unsqueeze(0).to_broadcast([64, NCH, C])).then_inc(landed, 16)
                        sp.dma_start(col[half, :, p], row.rearrange("c s -> s c")).then_inc(landed, 16)
                        n += 32
                        for k, q in enumerate((R_TAIL, R_BETA, R_NBEG)):
                            sp.dma_start(cols[half, :, k, p], rows[q, 2 * p + e].rearrange("(c s) -> s c", s=C)).then_inc(landed, 16)
                            n += 16
                sp.dma_start(egl_bc[:, :, :], egl.unsqueeze(0).to_broadcast([P, GH, NCH])).then_inc(landed, 16)
                n += 16
            sp.wait_ge(landed, n)
            sp.sem_inc(step_done, 1)

        @block.vector
        def _(dve):
            dve.wait_ge(step_done, 1)
            step = Chain(dve, step_done, 1)
            step(dve.tensor_tensor(along[:, :, :, :], along[:, :, :, :], col[:, :, :].unsqueeze(3).to_broadcast([P, NCH, 2, C]), ALU.subtract))
            step(dve.tensor_scalar(along[:, :, :, :], along[:, :, :, :], 0.0, None, ALU.min))
            dve.wait_ge(exp_done, 1)
            for k, mask in enumerate(("minus_strict", "causal_again")):
                for p in range(2):
                    step(dve.tensor_tensor(gates_tile[:, :, p, k, :], along[:, :, p, :],
                                           tab(mask).unsqueeze(1).to_broadcast([P, NCH, C]), ALU.mult))

        @block.scalar
        def _(act):
            act.wait_ge(step_done, 3)
            act.activation(along[:, :, :, :], along[:, :, :, :], ACT.Exp).then_inc(exp_done, 1)


def rwkv_rows(e):
    return slice(64 * e, 64 * e + 64)


def diagonal_blocks(nc, opnd, gates_tile, nt, tab):
    with Phase(nc) as local:
        sem = lambda name: local.sem(name)
        op = [local.enter_context(nc.sbuf_tensor(f"dop{b}", [P, 8, 4, C], F32)) for b in range(2)]
        n = [local.enter_context(nc.sbuf_tensor(f"dn{b}", [P, NPAIR, C], F32)) for b in range(2)]
        ps = [local.enter_context(nc.psum_tensor(f"dps{b}", [P, 8, C], F32)) for b in range(2)]
        landed, stored = [sem(f"dop_landed{b}") for b in range(2)], [sem(f"nt_stored{b}") for b in range(2)]
        mm_done, masked, turns = sem("d_mm_done"), sem("d_masked"), sem("d_turns")
        block = local.open_block()

        def chunks(eng, step):
            with eng.Fori(0, NCH // 2) as i:
                for b in range(2):
                    step(i * 2 + b, i, b)

        @block.sync
        def _(sp):
            def step(c, i, b):
                sp.wait_ge(mm_done, c + 1)
                sp.dma_start(op[b][:, :, :, :], opnd[bass.ds(c, 1), :, 0:8 * 256].rearrange("o p (n j s) -> p (o n) j s", n=8, j=4)).then_inc(landed[b], 16)
            chunks(sp, step)

        @block.tensor
        def _(pe):
            pe.sem_inc(mm_done, 2)

            def step(c, i, b):
                pe.wait_ge(landed[b], i * 16 + 16)
                pe.wait_ge(masked, c * 2 + 2)
                turn(pe, turns)
                for j in range(4):
                    for e in range(2):
                        h = rwkv_rows(e)
                        pe.matmul(ps[b][h, j, :], op[b][h, O_B, j, :], op[b][h, O_A, j, :], start=True, stop=True)
                for p in range(2):
                    for e in range(2):
                        last = pe.matmul(ps[b][rwkv_rows(e), 4 + p, :], op[b][:, O_GK, 2 * p + e, :], op[b][:, O_GKB, 2 * p + e, :],
                                         start=True, stop=True)
                last.then_inc(mm_done, 1)
            chunks(pe, step)

        @block.vector
        def _(dve):
            dve.sem_inc(masked, 4)
            for b in range(2):
                dve.sem_inc(stored[b], 64)

            def step(c, i, b):
                dve.wait_ge(mm_done, c + 3)
                dve.wait_ge(stored[b], i * 64 + 64)
                dve.tensor_tensor(n[b][:, 0:4, :], ps[b][:, 0:4, :], tab("strict").unsqueeze(1).to_broadcast([P, 4, C]), ALU.mult).then_inc(masked, 1)
                dve.tensor_tensor(n[b][:, 4:6, :], ps[b][:, 4:6, :], gates_tile[:, bass.ds(c, 1), :, 0, :].rearrange("p o g s -> p (o g) s"), ALU.mult).then_inc(masked, 1)
            chunks(dve, step)

        @block.scalar
        def _(act):
            def step(c, i, b):
                act.wait_ge(masked, c * 2 + 6)
                for q in range(4):
                    t0 = NB * (q % 2)
                    act.dma_start(nt[bass.ds(c, 1), 32 * q:32 * q + 32, :, :].rearrange("o s p t -> s (o p) t"),
                                  n[b][32 * q:32 * q + 32, :, t0:t0 + NB]).then_inc(stored[b], 16)
            chunks(act, step)
            for b in range(2):
                act.wait_ge(stored[b], 64 + 64 * (NCH // 2))


def invert_blocks(nc, nt, xinv):
    R = NPAIR // 2
    with Phase(nc) as local:
        sb = lambda name, shape: local.enter_context(nc.sbuf_tensor(name, shape, F32))
        sem = lambda name: local.sem(name)
        n, x, xt = sb("inv_n", [P, R, NB, NB]), sb("inv_x", [P, R, NB, NB]), sb("inv_xt", [P, R, NB, NB])
        prod = sb("inv_prod", [P, R, NB, NB])
        landed, step_done, stored = sem("inv_landed"), sem("inv_step"), sem("inv_stored")
        cleared = sem("inv_cleared")
        block = local.open_block()
        STEPS = 2 + 2 * (NB - 1)
        blocks = nt.rearrange("c (b s) p t -> (c b) s p t", s=NB)
        out = xinv.rearrange("c (b s) x p t -> (c b) s x p t", s=NB)

        @block.sync
        def _(sp):
            for pp in range(2):
                for r in range(R):
                    sp.dma_start(n[64 * pp:64 * pp + 64, r, :, :], blocks[:, :, 2 * r + pp, :]).then_inc(landed, 16)
            sp.wait_ge(step_done, STEPS)
            for which, tile in enumerate((x, xt)):
                for pp in range(2):
                    for r in range(R):
                        sp.dma_start(out[:, :, which, 2 * r + pp, :], tile[64 * pp:64 * pp + 64, r, :, :]).then_inc(stored, 16)
            sp.wait_ge(stored, 16 * 4 * R)

        @block.gpsimd
        def _(pool):
            pool.memset(x[:, :, :, :], 0.0).then_inc(cleared, 1)

        @block.vector
        def _(dve):
            step = Chain(dve, step_done)
            dve.wait_ge(cleared, 1)
            step(dve.memset(x[:, :, :, :].rearrange("p r i j -> p r (i j)")[:, :, 0:NB * NB:NB + 1], 1.0))
            dve.wait_ge(landed, 16 * 2 * R)
            for i in range(1, NB):
                step(dve.tensor_tensor(prod[:, :, 0:i, 0:i], n[:, :, 0:i, i].unsqueeze(2).to_broadcast([P, R, i, i]),
                                       x[:, :, 0:i, 0:i].rearrange("p r j c -> p r c j"), ALU.mult))
                step(dve.tensor_reduce(x[:, :, i, 0:i], prod[:, :, 0:i, 0:i], AX.X, ALU.add))
            step(dve.tensor_copy(xt[:, :, :, :], x[:, :, :, :].rearrange("p r i j -> p r j i")))


def scan_chunks(nc, opnd, xinv, gates_tile, cols, egl_bc, plast, mixed, tab):
    with Phase(nc) as local:
        sem = lambda name: local.sem(name)
        two = lambda name, shape: [local.enter_context(nc.sbuf_tensor(f"{name}{b}", [P] + shape, F32)) for b in range(2)]
        bank = lambda name, shape: local.enter_context(nc.psum_tensor(name, [P] + shape, F32))
        op = two("op", [N_OP, 4, C])
        packed = two("inv_packed", [2, NPAIR, NB])
        inv = two("inv", [2, NPAIR, C])
        m1, m2 = two("m1", [NPAIR, 2, C]), two("m2", [4, 2, C])
        tok_bk, tok_v = two("tok_bk", [2, 4, C]), two("tok_v", [4, C])
        tok_g = two("tok_g", [2, 2, GD])
        join, y = two("join", [NPAIR, C]), two("y", [NPAIR, C])
        zt = two("zt", [NPAIR, C])
        r_rw, r_g, w = two("r_rw", [4, C]), two("r_g", [2, GD]), two("w", [512])
        s_rw, s_g, s_dec = two("s_rw", [4, C]), two("s_g", [GH, GD]), two("s_dec", [GH, GD])
        s_sum, r_tmp = two("s_sum", [4, C]), two("r_tmp", [2, GD])
        o = two("o", [8, C])
        ps_m1, ps_m2 = bank("ps_m1", [8, C]), bank("ps_m2", [8, C])
        ps_bk, ps_vg, ps_kv = bank("ps_bk", [2, 4, C]), bank("ps_vg", [8, C]), bank("ps_kv", [2, 2, GD])
        ps_r, ps_w, ps_o = bank("ps_r", [512]), bank("ps_w", [512]), bank("ps_o", [8, C])

        landed, inv_landed, stored = ([sem(f"{n}{b}") for b in range(2)] for n in ("op_landed", "inv_landed", "o_stored"))
        mm_m1, mm_m2, mm_bk, mm_vg, mm_kv, mm_y, mm_zt = (sem("mm_" + n) for n in ("m1", "m2", "bk", "vg", "kv", "y", "zt"))
        mm_r, mm_w, mm_s, mm_o = (sem("mm_" + n) for n in ("r", "w", "s", "o"))
        m1_done, m1g_done, m2_done, bk_done, v_done, kv_done, inv_done, join_done, y_done, zt_done = (
            sem(n) for n in ("m1_done", "m1g_done", "m2_done", "bk_done", "v_done", "kv_done", "inv_done", "join_done", "y_done", "zt_done"))
        r_rw_done, r_tmp_done, r_g_done, w_done, s_sum_done, s_rw_done, dec_done, s_g_done, o_done, cleared, turns = (
            sem(n) for n in ("r_rw_done", "r_tmp_done", "r_g_done", "w_done", "s_sum_done", "s_rw_done", "dec_done", "s_g_done", "o_done", "s_cleared", "turns"))
        block = local.open_block()
        bc = lambda name, n: tab(name).unsqueeze(1).to_broadcast([P, n, C])
        both = lambda name: tab(name, 2 * C).rearrange("p (k s) -> p k s", k=2)

        def at_least(eng, s, n, scale=1):
            if not (isinstance(n, int) and n <= 0):
                eng.wait_ge(s, n * scale)

        def run(eng, product, state):
            def beside(c, n, b, j, nj):
                s, p = state(c, j, b), product(n, nj, 1 - b)
                for part in TURNS:
                    next(s if part == "state" else p, None)
            first = product(0, 0, 0)
            for _ in range(4):
                next(first, None)
            with eng.Fori(0, NCH // 2 - 1) as i:
                beside(i * 2, i * 2 + 1, 0, i, i)
                beside(i * 2 + 1, i * 2 + 2, 1, i, i + 1)
            beside(NCH - 2, NCH - 1, 0, NCH // 2 - 1, NCH // 2 - 1)
            last = state(NCH - 1, NCH // 2 - 1, 1)
            for _ in range(4):
                next(last, None)

        TURNS = ("state", "product", "state", "product", "state", "product", "state", "product")

        @block.sync
        def _(sp):
            sp.sem_inc(mm_o, 2)
            def load(c, i, b):
                sp.wait_ge(mm_o, c + 1)
                sp.dma_start(op[b][:, :, :, :], opnd[bass.ds(c, 1), :, :].rearrange("o p (n j s) -> p (o n) j s", n=N_OP, j=4)).then_inc(landed[b], 16)
                sp.dma_start(packed[b][:, :, :, :], xinv[bass.ds(c, 1)].rearrange("o r x p t -> r (o x) p t")).then_inc(inv_landed[b], 16)
            with sp.Fori(0, NCH // 2) as i:
                for b in range(2):
                    load(i * 2 + b, i, b)

        @block.tensor
        def _(pe):
            def product(c, i, b):
                pe.wait_ge(landed[b], i * 16 + 16)
                at_least(pe, y_done, c)
                turn(pe, turns)
                for j in range(4):
                    for e in range(2):
                        h = rwkv_rows(e)
                        last = pe.matmul(ps_m1[h, 2 * j:2 * j + 2, :], op[b][h, O_B, j, :], op[b][h, O_A:O_R + 1, j, :], start=True, stop=True)
                last.then_inc(mm_m1, 1)
                at_least(pe, zt_done, c)
                turn(pe, turns)
                for j in range(4):
                    for e in range(2):
                        h = rwkv_rows(e)
                        last = pe.matmul(ps_m2[h, 2 * j:2 * j + 2, :], op[b][h, O_K, j, :], op[b][h, O_A:O_R + 1, j, :], start=True, stop=True)
                last.then_inc(mm_m2, 1)
                yield
                at_least(pe, bk_done, c)
                turn(pe, turns)
                for n, src in enumerate((O_B, O_K)):
                    for j in range(4):
                        for e in range(2):
                            h = rwkv_rows(e)
                            last = pe.matmul(ps_bk[h, n, j, :], op[b][h, src, j, :], tab("ident2")[h, :], start=True, stop=True)
                last.then_inc(mm_bk, 1)
                at_least(pe, v_done, c)
                at_least(pe, m1g_done, c)
                turn(pe, turns)
                for j in range(4):
                    for e in range(2):
                        h = rwkv_rows(e)
                        pe.matmul(ps_vg[h, j, :], op[b][h, O_V, j, :], tab("ident2")[h, :], start=True, stop=True)
                for p in range(2):
                    for e in range(2):
                        last = pe.matmul(ps_vg[rwkv_rows(e), 4 + 2 * p:6 + 2 * p, :], op[b][:, O_GK, 2 * p + e, :],
                                         op[b][:, O_GKB:O_GQ + 1, 2 * p + e, :], start=True, stop=True)
                last.then_inc(mm_vg, 1)
                yield
                at_least(pe, kv_done, c)
                for n, src in enumerate((O_GK, O_GV)):
                    for p in range(2):
                        for e in range(2):
                            last = pe.matmul(ps_kv[rwkv_rows(e), n, p, :], op[b][:, src, 2 * p + e, :], tab("ident"), start=True, stop=True)
                last.then_inc(mm_kv, 1)
                pe.wait_ge(join_done, c + 1)
                pe.wait_ge(inv_done, c * 4 + 4)
                pe.wait_ge(m1_done, c + 1)
                turn(pe, turns)
                for u in range(NPAIR):
                    for e in range(2):
                        h = rwkv_rows(e)
                        last = pe.matmul(ps_m1[h, u, :], join[b][h, u, :], inv[b][h, 0, u, :], start=True, stop=True)
                last.then_inc(mm_y, 1)
                yield
                pe.wait_ge(y_done, c + 1)
                pe.wait_ge(m2_done, c + 1)
                turn(pe, turns)
                for u in range(NPAIR):
                    for e in range(2):
                        h = rwkv_rows(e)
                        last = pe.matmul(ps_m2[h, u, :], y[b][h, u, :], inv[b][h, 1, u, :], start=True, stop=True)
                last.then_inc(mm_zt, 1)
                yield

            def state(c, i, b):
                pe.wait_ge(bk_done, c + 1)
                pe.wait_ge(v_done, c + 1)
                pe.wait_ge(s_rw_done, c + 1)
                pe.wait_ge(s_g_done, c * 2 + 2)
                for p in range(2):
                    for e in range(2):
                        at = 256 + p * GD
                        pe.matmul(ps_r[rwkv_rows(e), at:at + GD], op[b][:, O_GK, 2 * p + e, :], s_g[b][:, 2 * p + e, :], start=True, stop=True)
                for j in range(4):
                    for e in range(2):
                        h = rwkv_rows(e)
                        out = ps_r[h, j * C:(j + 1) * C]
                        pe.matmul(out, op[b][h, O_A, j, :], s_rw[b][h, j, :], start=True, stop=False)
                        last = pe.matmul(out, m2[b][h, j, 0, :], tok_v[b][h, j, :], start=False, stop=True)
                last.then_inc(mm_r, 1)
                yield
                at_least(pe, o_done, c, 3)
                pe.wait_ge(zt_done, c + 1)
                pe.wait_ge(r_rw_done, c + 1)
                pe.wait_ge(r_g_done, c + 1)
                turn(pe, turns)
                for j in range(4):
                    for e in range(2):
                        h = rwkv_rows(e)
                        pe.matmul(ps_w[h, j * C:(j + 1) * C], zt[b][h, j, :], r_rw[b][h, j, :], start=True, stop=True)
                for p in range(2):
                    for e in range(2):
                        h, at = rwkv_rows(e), 256 + p * GD
                        last = pe.matmul(ps_w[h, at:at + GD], zt[b][h, 4 + p, :], r_g[b][h, p, :], start=True, stop=True)
                last.then_inc(mm_w, 1)
                yield
                pe.wait_ge(w_done, c + 1)
                pe.wait_ge(kv_done, c + 1)
                for p in range(2):
                    for e in range(2):
                        h, out = rwkv_rows(e), (ps_w[:, p * GD:(p + 1) * GD], ps_r[:, 256 + p * GD:256 + (p + 1) * GD])[e]
                        pe.matmul(out, tok_g[b][h, 0, p, :], w[b][h, 256 + p * GD:256 + (p + 1) * GD], start=True, stop=True)
                for j in range(4):
                    for e in range(2):
                        h = rwkv_rows(e)
                        out = ps_r[h, j * C:(j + 1) * C]
                        pe.matmul(out, tok_bk[b][h, 0, j, :], w[b][h, j * C:(j + 1) * C], start=True, stop=False)
                        last = pe.matmul(out, tok_bk[b][h, 1, j, :], tok_v[b][h, j, :], start=False, stop=True)
                last.then_inc(mm_s, 1)
                yield
                at_least(pe, o_done, c, 3)
                pe.wait_ge(m1g_done, c + 1)
                pe.wait_ge(s_g_done, c * 2 + 4)
                turn(pe, turns)
                for j in range(4):
                    for e in range(2):
                        h = rwkv_rows(e)
                        out = ps_o[h, j, :]
                        pe.matmul(out, s_rw[b][h, j, :], op[b][h, O_R, j, :], start=True, stop=False)
                        pe.matmul(out, w[b][h, j * C:(j + 1) * C], m1[b][h, j, 1, :], start=False, stop=False)
                        pe.matmul(out, tok_v[b][h, j, :], m2[b][h, j, 1, :], start=False, stop=True)
                for p in range(2):
                    for e in range(2):
                        h = rwkv_rows(e)
                        out = (ps_o[:, 4 + p, :], ps_w[:, 256 + p * C:256 + (p + 1) * C])[e]
                        pe.matmul(out, s_g[b][:, 2 * p + e, :], op[b][:, O_GQD, 2 * p + e, :], start=True, stop=False)
                        last = pe.matmul(out, w[b][h, 256 + p * GD:256 + (p + 1) * GD], m1[b][h, 4 + p, 1, :], start=False, stop=True)
                last.then_inc(mm_o, 1)
                yield

            run(pe, product, state)

        @block.vector
        def _(dve):
            dve.memset(s_rw[0][:, :, :], 0.0).then_inc(s_rw_done, 1)
            dve.memset(s_g[0][:, :, :], 0.0).then_inc(s_g_done, 2)

            def product(c, i, b):
                dve.wait_ge(mm_m1, c + 1)
                dve.tensor_tensor(m1[b][:, 0:4, :, :], ps_m1[:, :, :].rearrange("p (j k) s -> p j k s", k=2),
                                  both("strict").unsqueeze(1).to_broadcast([P, 4, 2, C]), ALU.mult).then_inc(m1_done, 1)
                dve.wait_ge(mm_m2, c + 1)
                dve.tensor_tensor(m2[b][:, :, :, :], ps_m2[:, :, :].rearrange("p (j k) s -> p j k s", k=2),
                                  both("strict").unsqueeze(1).to_broadcast([P, 4, 2, C]), ALU.mult).then_inc(m2_done, 1)
                yield
                dve.wait_ge(mm_vg, c + 1)
                dve.tensor_tensor(m1[b][:, 4:6, :, :].rearrange("p g k s -> p (g k s)"), ps_vg[:, 4:8, :].rearrange("p g s -> p (g s)"),
                                  gates_tile[:, bass.ds(c, 1), :, :, :].rearrange("p o g k s -> p (o g k s)"), ALU.mult).then_inc(m1g_done, 1)
                yield
                dve.wait_ge(mm_kv, c + 1)
                dve.tensor_tensor(tok_g[b][:, :, :, :].rearrange("p n g d -> p (n g) d"), ps_kv[:, :, :, :].rearrange("p n g d -> p (n g) d"),
                                  cols[:, bass.ds(c, 1), 0:2, :].rearrange("p o n g -> p (o n g)").unsqueeze(2).to_broadcast([P, 4, GD]),
                                  ALU.mult).then_inc(kv_done, 1)
                yield
                dve.wait_ge(mm_zt, c + 1)
                dve.wait_ge(inv_done, c * 4 + 4)
                dve.tensor_tensor(zt[b][:, :, :], ps_m2[:, 0:NPAIR, :], inv[b][:, 1, :, :], ALU.add).then_inc(zt_done, 1)
                yield

            def state(c, i, b):
                dve.wait_ge(mm_r, c + 1)
                dve.tensor_tensor(r_tmp[b][:, :, :], ps_r[:, 256:512].rearrange("p (g d) -> p g d", g=2),
                                  cols[:, bass.ds(c, 1), 2, :].rearrange("p o g -> p (o g)").unsqueeze(2).to_broadcast([P, 2, GD]), ALU.mult).then_inc(r_tmp_done, 1)
                dve.wait_ge(r_tmp_done, c + 1)
                dve.wait_ge(kv_done, c + 1)
                dve.tensor_tensor(r_g[b][:, :, :], r_tmp[b][:, :, :], tok_g[b][:, 1, :, :], ALU.add).then_inc(r_g_done, 1)
                yield
                yield
                dve.wait_ge(mm_s, c + 1)
                dve.wait_ge(dec_done, c + 1)
                for e, src in enumerate((ps_w[:, 0:256], ps_r[:, 256:512])):
                    last = dve.tensor_tensor(s_g[1 - b][:, :, :].rearrange("p (g e) d -> p g e d", e=2)[:, :, e, :],
                                             s_dec[b][:, :, :].rearrange("p (g e) d -> p g e d", e=2)[:, :, e, :],
                                             src.rearrange("p (g d) -> p g d", g=2), ALU.add)
                    last.then_inc(s_g_done, 1)
                dve.tensor_tensor(s_sum[b][:, :, :], s_rw[b][:, :, :], ps_r[:, 0:256].rearrange("p (j d) -> p j d", j=4), ALU.add).then_inc(s_sum_done, 1)
                dve.wait_ge(s_sum_done, c + 1)
                dve.tensor_tensor(s_rw[1 - b][:, :, :], s_sum[b][:, :, :],
                                  plast[:, :].rearrange("p (j c) -> p j c", j=4)[:, :, bass.ds(c, 1)].to_broadcast([P, 4, C]), ALU.mult).then_inc(s_rw_done, 1)
                yield

            run(dve, product, state)

        @block.scalar
        def _(act):
            for b in range(2):
                act.sem_inc(stored[b], 16)

            def product(c, i, b):
                act.wait_ge(mm_bk, c + 1)
                act.activation(tok_bk[b][:, :, :, :], ps_bk[:, :, :, :], ACT.Copy).then_inc(bk_done, 1)
                act.wait_ge(m1g_done, c + 1)
                act.activation(tok_v[b][:, :, :], ps_vg[:, 0:4, :], ACT.Copy).then_inc(v_done, 1)
                yield
                act.wait_ge(mm_y, c + 1)
                act.activation(y[b][:, :, :], ps_m1[:, 0:NPAIR, :], ACT.Copy).then_inc(y_done, 1)
                yield

            def state(c, i, b):
                act.wait_ge(r_tmp_done, c + 1)
                act.activation(r_rw[b][:, :, :], ps_r[:, 0:256].rearrange("p (j d) -> p j d", j=4), ACT.Copy).then_inc(r_rw_done, 1)
                act.wait_ge(mm_w, c + 1)
                act.activation(w[b][:, :], ps_w[:, :], ACT.Copy).then_inc(w_done, 1)
                yield
                act.wait_ge(mm_o, c + 3)
                act.wait_ge(stored[b], i * 16 + 16)
                act.activation(o[b][:, 0:4, :], ps_o[:, 0:4, :], ACT.Copy).then_inc(o_done, 1)
                heads = o[b][:, 4:8, :].rearrange("p (g e) s -> p g e s", e=2)
                act.activation(heads[:, :, 0, :], ps_o[:, 4:6, :], ACT.Copy).then_inc(o_done, 1)
                act.activation(heads[:, :, 1, :], ps_w[:, 256:384].rearrange("p (g s) -> p g s", g=2), ACT.Copy).then_inc(o_done, 1)
                act.wait_ge(o_done, c * 3 + 3)
                act.dma_start(mixed[bass.ds(c, 1)].rearrange("o p n s -> p (o n) s"), o[b][:, :, :]).then_inc(stored[b], 16)
                yield
            run(act, product, state)
            for b in range(2):
                act.wait_ge(stored[b], 16 + 16 * (NCH // 2))

        @block.gpsimd
        def _(pool):
            for b in range(2):
                pool.memset(inv[b][:, :, :, :], 0.0).then_inc(cleared, 1)
            pool.wait_ge(cleared, 2)

            def product(c, i, b):
                pool.wait_ge(inv_landed[b], i * 16 + 16)
                at_least(pool, dec_done, c)
                turn(pool, turns)
                for q in range(4):
                    rows, t0 = slice(32 * q, 32 * q + 32), NB * (q % 2)
                    last = pool.tensor_copy(inv[b][rows, :, :, t0:t0 + NB], packed[b][rows, :, :, :])
                    last.then_inc(inv_done, 1)
                pool.wait_ge(inv_done, c * 4 + 4)
                pool.wait_ge(m1_done, c + 1)
                pool.wait_ge(m1g_done, c + 1)
                pool.tensor_tensor(join[b][:, :, :], m1[b][:, :, 0, :], bc("corner", NPAIR), ALU.mult).then_inc(join_done, 1)
                yield

            def state(c, i, b):
                pool.wait_ge(join_done, c + 1)
                pool.wait_ge(s_g_done, c * 2 + 2)
                pool.tensor_tensor(s_dec[b][:, :, :], s_g[b][:, :, :], egl_bc[:, :, bass.ds(c, 1)].to_broadcast([P, GH, GD]), ALU.mult).then_inc(dec_done, 1)
                yield
            run(pool, product, state)


def window_attention(nc, u, attended, par, tab):
    W = 2 * C
    with Phase(nc) as local:
        sem = lambda name: local.sem(name)
        two = lambda name, shape: [local.enter_context(nc.sbuf_tensor(f"{name}{b}", [P] + shape, F32)) for b in range(2)]
        bank = lambda name, shape: [local.enter_context(nc.psum_tensor(f"{name}{b}", [P] + shape, F32)) for b in range(2)]
        q, k, v = two("at_q", [4, C]), two("at_k", [SKV, W]), two("at_v", [W])
        s, pt, vt, o = two("at_s", [4, W]), two("at_pt", [4, W]), two("at_vt", [P]), two("at_o", [4, C])
        top, own, rest = two("at_top", [4]), two("at_own", [4]), two("at_rest", [4])
        ps_s, ps_t, ps_vo, ps_o = bank("ps_s", [4, W]), bank("ps_t", [4, W]), bank("ps_v", [P]), bank("ps_ao", [4, C])
        landed, stored = [sem(f"at_landed{b}") for b in range(2)], [sem(f"at_stored{b}") for b in range(2)]
        mm_s, mm_v, mm_t, mm_o = (sem("at_mm_" + n) for n in "svto")
        dve_step, shifted, exp_done, p_done, vt_done, pt_done, o_done, padded, turns = (
            sem("at_" + n) for n in ("dve", "shifted", "exp_done", "p_done", "vt_done", "pt_done", "o_done", "padded", "turns"))
        block = local.open_block()
        STEPS = 6

        def over_chunks(eng, score, gather):
            def both(c, j, b, nj):
                score(c + 1, nj, 1 - b, False)
                gather(c, j, b)
            score(0, 0, 0, True)
            with eng.Fori(0, NCH // 2 - 1) as i:
                both(i * 2, i, 0, i)
                both(i * 2 + 1, i, 1, i + 1)
            both(NCH - 2, NCH // 2 - 1, 0, NCH // 2 - 1)
            gather(NCH - 1, NCH // 2 - 1, 1)

        @block.sync
        def _(sp):
            def score(c, i, b, first):
                if first:
                    sp.wait_ge(padded, 1)
                else:
                    sp.wait_ge(mm_s, c)
                    sp.wait_ge(mm_v, c)
                n = C if first else W
                at = 0 if first else c * C - C
                to = slice(W - n, W)
                sp.dma_start(q[b][:, :, :], u[U_SQ * P:(U_SQ + 4) * P, bass.ds(c * C, C)].rearrange("(j p) t -> p j t", p=P)).then_inc(landed[b], 16)
                for g in range(SKV):
                    src = u[U_SK * P + g * SD:U_SK * P + (g + 1) * SD, bass.ds(at, n)]
                    for e in range(2):
                        sp.dma_start(k[b][rwkv_rows(e), g, to], src).then_inc(landed[b], 16)
                sp.dma_start(v[b][:, to], u[U_SV * P:(U_SV + 1) * P, bass.ds(at, n)]).then_inc(landed[b], 16)

            over_chunks(sp, score, lambda *a: None)

        @block.tensor
        def _(pe):
            def score(c, i, b, first):
                pe.wait_ge(landed[b], i * 96 + 96)
                if not first:
                    pe.wait_ge(p_done, c)
                    pe.wait_ge(vt_done, c)
                    turn(pe, turns)
                for j in range(4):
                    for e in range(2):
                        h = rwkv_rows(e)
                        last = pe.matmul(ps_s[b][h, j, :], q[b][h, j, :], k[b][h, j // 2, :], start=True, stop=True)
                last.then_inc(mm_s, 1)
                pe.transpose(ps_vo[b][:, :], v[b][:, :], tab("ident")).then_inc(mm_v, 1)

            def gather(c, i, b):
                pe.wait_ge(p_done, c + 1)
                pe.wait_ge(pt_done, c + 1)
                for j in range(4):
                    last = pe.transpose(ps_t[b][:, j, :], s[b][:, j, :], tab("ident"))
                last.then_inc(mm_t, 1)
                pe.wait_ge(vt_done, c + 1)
                pe.wait_ge(pt_done, c + 3)
                pe.wait_ge(o_done, c + 1)
                for g in range(SKV):
                    for e in range(2):
                        last = pe.matmul(ps_o[b][rwkv_rows(e), 2 * g:2 * g + 2, :], vt[b][:, g * SD:(g + 1) * SD],
                                         pt[b][:, 2 * g:2 * g + 2, e * C:(e + 1) * C], start=True, stop=True)
                last.then_inc(mm_o, 1)

            pe.sem_inc(o_done, 2)
            pe.sem_inc(pt_done, 2)
            pe.sem_inc(mm_o, 2)
            over_chunks(pe, score, gather)

        @block.vector
        def _(dve):
            dve.memset(k[0][:, :, 0:C], 0.0).then_inc(dve_step, 1)
            dve.memset(v[0][:, 0:C], 0.0).then_inc(dve_step, 1)
            dve.wait_ge(dve_step, 2)
            dve.sem_inc(padded, 1)

            def score(c, i, b, first):
                step = Chain(dve, dve_step, c * STEPS + 2)
                at = CONST_AT["alibi10" if first else "alibi00"][0]
                alibi = tab.tile[:, at:at + 4 * W].rearrange("p (j k) -> p j k", j=4)
                wide = lambda t: t[:, :].unsqueeze(2).to_broadcast([P, 4, W])
                dve.wait_ge(mm_s, c + 1)
                if not first:
                    dve.wait_ge(mm_t, c)
                step(dve.scalar_tensor_tensor(s[b][:, :, :].rearrange("p j k -> p (j k)"), ps_s[b][:, :, :].rearrange("p j k -> p (j k)"), SD ** -0.5,
                                              alibi.rearrange("p j k -> p (j k)"), ALU.mult, ALU.add))
                step(dve.tensor_reduce(top[b][:, :], s[b][:, :, :], AX.X, ALU.max))
                step(dve.tensor_tensor(top[b][:, :], top[b][:, :], par("sinks", 0, 4), ALU.max))
                dve.tensor_tensor(own[b][:, :], par("sinks", 0, 4), top[b][:, :], ALU.subtract).then_inc(shifted, 1)
                dve.tensor_tensor(s[b][:, :, :], s[b][:, :, :], wide(top[b]), ALU.subtract).then_inc(shifted, 1)
                dve.wait_ge(exp_done, c * 2 + 2)
                step(dve.tensor_reduce(rest[b][:, :], s[b][:, :, :], AX.X, ALU.add))
                step(dve.tensor_tensor(rest[b][:, :], rest[b][:, :], own[b][:, :], ALU.add))
                step(dve.reciprocal(rest[b][:, :], rest[b][:, :]))
                dve.tensor_tensor(s[b][:, :, :], s[b][:, :, :], wide(rest[b]), ALU.mult).then_inc(p_done, 1)

            def gather(c, i, b):
                pass
            over_chunks(dve, score, gather)

        @block.scalar
        def _(act):
            for b in range(2):
                act.sem_inc(stored[b], 16)

            def score(c, i, b, first):
                act.wait_ge(mm_v, c + 1)
                act.wait_ge(mm_o, c + 1)
                act.activation(vt[b][:, :], ps_vo[b][:, :], ACT.Copy).then_inc(vt_done, 1)
                act.wait_ge(shifted, c * 2 + 2)
                act.activation(own[b][:, :], own[b][:, :], ACT.Exp).then_inc(exp_done, 1)
                act.activation(s[b][:, :, :], s[b][:, :, :], ACT.Exp).then_inc(exp_done, 1)

            def gather(c, i, b):
                act.wait_ge(mm_t, c + 1)
                act.activation(pt[b][:, :, :], ps_t[b][:, :, :], ACT.Copy).then_inc(pt_done, 1)
                act.wait_ge(mm_o, c + 3)
                act.wait_ge(stored[b], i * 16 + 16)
                act.activation(o[b][:, :, :], ps_o[b][:, :, :], ACT.Copy).then_inc(o_done, 1)
                act.wait_ge(o_done, c + 3)
                act.dma_start(attended[bass.ds(c, 1)].rearrange("o p n s -> p (o n) s"), o[b][:, :, :]).then_inc(stored[b], 16)
            over_chunks(act, score, gather)
            for b in range(2):
                act.wait_ge(stored[b], 16 + 16 * (NCH // 2))


def finish_mixers(nc, A, u, mixed, attended, bonus, gl, oh, ol, par, tab):
    with Phase(nc) as local:
        sb = lambda name, shape: local.enter_context(nc.sbuf_tensor(name, shape, F32))
        sem = lambda name: local.sem(name)
        t = [{n: sb(f"f_{n}{b}", [P, T]) for n in ("g", "r", "s", "z", "bonus")} for b in range(2)]
        for shared in ("sq_g", "sq_r", "n_g", "n_r"):
            t[0][shared] = t[1][shared] = sb("f_" + shared, [P, T])
        up = [sb(f"f_up{b}", [P, P]) for b in range(2)]
        ps = {n: local.enter_context(nc.psum_tensor("f_ps_" + n, [P, 2, HALF], F32)) for n in ("mean", "gate", "r", "g")}
        flat = lambda p: p[:, :, :].rearrange("p h t -> p (h t)")
        landed = [{n: sem(f"f_landed_{n}{b}") for n in ("g", "r", "s", "z", "bonus", "up")} for b in range(2)]
        mm_mean, mm_gate, mm_r, mm_g = (sem("f_mm_" + n) for n in ("mean", "gate", "r", "g"))
        centred, sq_r_done, sq_g_done, root_done, silu_done, dve_step, hi_done, round_done = (
            sem("f_" + n) for n in ("centred", "sq_r_done", "sq_g_done", "root_done", "silu_done", "dve", "hi_done", "round_done"))
        block = local.open_block()
        STEPS = 11
        of_tile = lambda src, n: src[:, :, bass.ds(n, 1), :].rearrange("c p o s -> p c (o s)")
        chunks = lambda x: x[:, :].rearrange("p (c s) -> p c s", s=C)

        def rounds(eng, one):
            with eng.Fori(0, 2) as j:
                for b in range(2):
                    one(j * 2 + b, j, t[b], up[b], landed[b])

        @block.sync
        def _(sp):
            sp.sem_inc(round_done, 2)
            def one(i, j, t, up, landed):
                sp.wait_ge(round_done, i + 1)
                sp.dma_start(chunks(t["r"]), of_tile(mixed, i)).then_inc(landed["r"], 16)
                sp.dma_start(up[:, :], A["rwkv_g_up"][0][:, bass.ds(i * P, P)]).then_inc(landed["up"], 16)
                sp.dma_start(chunks(t["g"]), of_tile(mixed, i + 4)).then_inc(landed["g"], 16)
                sp.dma_start(t["z"][:, :], u[bass.ds(i * P + U_Z * P, P), :]).then_inc(landed["z"], 16)
                sp.dma_start(t["bonus"][:, :], bonus[bass.ds(i * P, P), :]).then_inc(landed["bonus"], 16)
                sp.dma_start(chunks(t["s"]), of_tile(attended, i)).then_inc(landed["s"], 16)
            rounds(sp, one)

        @block.tensor
        def _(pe):
            def one(i, j, t, up, landed):
                def dot(out, w, x, done):
                    for h in range(2):
                        last = pe.matmul(out[:, h, :], w, x[:, h * HALF:(h + 1) * HALF], start=True, stop=True)
                    last.then_inc(done, 1)
                pe.wait_ge(landed["r"], j * 16 + 16)
                pe.wait_ge(round_done, i + 2)
                dot(ps["mean"], tab("head_ones"), t["r"], mm_mean)
                pe.wait_ge(landed["up"], j * 16 + 16)
                dot(ps["gate"], up[:, :], gl, mm_gate)
                pe.wait_ge(sq_g_done, i + 1)
                dot(ps["g"], tab("ones"), t["sq_g"], mm_g)
                pe.wait_ge(sq_r_done, i + 1)
                dot(ps["r"], tab("head_ones"), t["sq_r"], mm_r)
            rounds(pe, one)

        @block.scalar
        def _(act):
            def one(i, j, t, up, landed):
                act.wait_ge(round_done, i + 2)
                act.wait_ge(landed["z"], j * 16 + 16)
                act.activation(t["z"][:, :], t["z"][:, :], ACT.Silu).then_inc(silu_done, 1)
                act.wait_ge(landed["g"], j * 16 + 16)
                act.activation(t["sq_g"][:, :], t["g"][:, :], ACT.Square).then_inc(sq_g_done, 1)
                act.wait_ge(centred, i + 1)
                act.activation(t["sq_r"][:, :], t["r"][:, :], ACT.Square).then_inc(sq_r_done, 1)
                act.wait_ge(mm_g, i + 1)
                act.activation(t["n_g"][:, :], flat(ps["g"]), ACT.Sqrt, bias=par("eps_gdn"), scale=1.0 / GD).then_inc(root_done, 1)
                act.wait_ge(mm_r, i + 1)
                act.activation(t["n_r"][:, :], flat(ps["r"]), ACT.Sqrt, bias=par("eps_lnx"), scale=1.0 / RD).then_inc(root_done, 1)
            rounds(act, one)

        @block.vector
        def _(dve):
            def one(i, j, t, up, landed):
                step = Chain(dve, dve_step, i * STEPS)

                def split(n, src):
                    hi, lo = (o[:, bass.ds(i + 4 * n, 1), :].rearrange("p o t -> p (o t)") for o in (oh, ol))
                    dve.tensor_copy(hi, src[:, :]).then_inc(hi_done, 1)
                    dve.wait_ge(hi_done, i * 3 + split.n + 1)
                    split.n += 1
                    step(dve.tensor_tensor(lo, src[:, :], as_f32(hi), ALU.subtract))
                split.n = 0
                dve.wait_ge(mm_mean, i + 1)
                dve.scalar_tensor_tensor(t["r"][:, :], flat(ps["mean"]), -1.0 / RD, t["r"][:, :], ALU.mult, ALU.add).then_inc(centred, 1)
                dve.wait_ge(landed["s"], j * 16 + 16)
                split(2, t["s"])
                dve.wait_ge(root_done, i * 2 + 1)
                step(dve.reciprocal(t["n_g"][:, :], t["n_g"][:, :]))
                step(dve.tensor_tensor(t["g"][:, :], t["g"][:, :], t["n_g"][:, :], ALU.mult))
                dve.wait_ge(silu_done, i + 1)
                step(dve.scalar_tensor_tensor(t["g"][:, :], t["g"][:, :], par("norm_w"), t["z"][:, :], ALU.mult, ALU.mult))
                split(0, t["g"])
                dve.wait_ge(root_done, i * 2 + 2)
                step(dve.reciprocal(t["n_r"][:, :], t["n_r"][:, :]))
                step(dve.tensor_tensor(t["r"][:, :], t["r"][:, :], t["n_r"][:, :], ALU.mult))
                step(dve.tensor_scalar(t["r"][:, :], t["r"][:, :], par("lnx_w", i), par("lnx_b", i), ALU.mult, ALU.add))
                dve.wait_ge(landed["bonus"], j * 16 + 16)
                step(dve.tensor_tensor(t["r"][:, :], t["r"][:, :], t["bonus"][:, :], ALU.add))
                dve.wait_ge(mm_gate, i + 1)
                step(dve.tensor_tensor(t["r"][:, :], t["r"][:, :], flat(ps["gate"]), ALU.mult))
                split(1, t["r"])
                assert step.n == STEPS, step.n
                dve.sem_inc(round_done, 1)
            rounds(dve, one)


def project_branches(nc, A, u, oh, ol, merged):
    with Phase(nc) as local:
        sem = lambda name: local.sem(name)
        sb = lambda name, shape, dt=F32: local.enter_context(nc.sbuf_tensor(name, shape, dt))
        raw = sb("b_raw", [P, 12, P])
        whi = [sb(f"b_hi{b}", [P, 12, P], F32R) for b in range(2)]
        wlo = [sb(f"b_lo{b}", [P, 12, P], F32R) for b in range(2)]
        gate = [sb(f"b_gate{b}", [P, 3, T]) for b in range(2)]
        total, part = [sb(f"b_total{b}", [P, T]) for b in range(2)], sb("b_part", [P, T])
        ps = [local.enter_context(nc.psum_tensor(f"b_ps{n}", [P, 2, HALF], F32)) for n in range(3)]
        flat = lambda p: p[:, :, :].rearrange("p h t -> p (h t)")
        landed = sem("b_landed")
        gate_landed = [sem(f"b_gate_landed{b}") for b in range(2)]
        stored = [sem(f"b_stored{b}") for b in range(2)]
        hi_done, lo_done, gate_done, mm_done, evac, dve_step, total_done = (
            sem("b_" + n) for n in ("hi_done", "lo_done", "gate_done", "mm_done", "evac", "dve", "total_done"))
        block = local.open_block()

        def tiles(eng, step):
            with eng.Fori(0, KT // 2) as i:
                for b in range(2):
                    step(i * 2 + b, i, b)

        @block.sync
        def _(sp):
            sp.sem_inc(evac, 6)
            sp.sem_inc(lo_done, 2)

            def load(n, b):
                sp.wait_ge(lo_done, n + 2)
                for k, name in enumerate("abc"):
                    sp.dma_start(raw[:, 4 * k:4 * k + 4, :], A["w_branch_" + name][0][:, bass.ds(n * P, P)].rearrange("(k p) n -> p k n", p=P)).then_inc(landed, 16)
                sp.wait_ge(evac, n * 3 + 3)
                for k in range(3):
                    sp.dma_start(gate[b][:, k, :], u[bass.ds(n * P + (U_GATE + 8 * k) * P, P), :]).then_inc(gate_landed[b], 16)

            def store(n, b):
                sp.wait_ge(total_done, n + 1)
                sp.dma_start(merged[bass.ds(n, 1), :, :].rearrange("o p t -> (o p) t"), total[b][:, :]).then_inc(stored[b], 16)
            load(0, 0)
            load(1, 1)
            with sp.Fori(0, KT // 2 - 1) as i:
                for b in range(2):
                    store(i * 2 + b, b)
                    load(i * 2 + (b + 2), b)
            for b in range(2):
                store(KT - 2 + b, b)
            for b in range(2):
                sp.wait_ge(stored[b], 16 * (KT // 2))

        @block.scalar
        def _(act):
            act.sem_inc(mm_done, 6)

            def step(n, i, b):
                act.wait_ge(landed, n * 48 + 48)
                act.wait_ge(mm_done, n * 3 + 3)
                act.activation(whi[b][:, :, :], raw[:, :, :], ACT.Copy).then_inc(hi_done, 1)
                act.wait_ge(gate_landed[b], i * 48 + 48)
                act.activation(gate[b][:, :, :], gate[b][:, :, :], ACT.Sigmoid).then_inc(gate_done, 1)
            tiles(act, step)

        @block.gpsimd
        def _(pool):
            def step(n, i, b):
                pool.wait_ge(hi_done, n + 1)
                pool.tensor_tensor(wlo[b][:, :, :], raw[:, :, :], as_f32(whi[b][:, :, :]), ALU.subtract).then_inc(lo_done, 1)
            tiles(pool, step)

        @block.tensor
        def _(pe):
            def step(n, i, b):
                pe.wait_ge(lo_done, n + 3)
                for k in range(3):
                    pe.wait_ge(evac, n * 3 + (k + 4))
                    for q in range(4):
                        for h in range(2):
                            cols = slice(h * HALF, (h + 1) * HALF)
                            last = split_dot(pe, ps[k][:, h, :], whi[b][:, 4 * k + q, :], wlo[b][:, 4 * k + q, :],
                                             oh[:, 4 * k + q, cols], ol[:, 4 * k + q, cols], q == 0, q == 3)
                    last.then_inc(mm_done, 1)
            tiles(pe, step)

        @block.vector
        def _(dve):
            def step(n, i, b, first=False):
                chain = Chain(dve, dve_step, n)
                dve.wait_ge(gate_done, n + 1)
                dve.wait_ge(mm_done, n * 3 + 7)
                if not first:
                    dve.wait_ge(stored[b], i * 16)
                dve.tensor_tensor(total[b][:, :], flat(ps[0]), gate[b][:, 0, :], ALU.mult).then_inc(evac, 1)
                if not (first and b == 0):
                    dve.wait_ge(total_done, n)
                for k in (1, 2):
                    dve.wait_ge(mm_done, n * 3 + (7 + k))
                    dve.tensor_tensor(part[:, :], flat(ps[k]), gate[b][:, k, :], ALU.mult).then_inc(evac, 1)
                    dve.wait_ge(evac, n * 3 + (7 + k))
                    add = dve.tensor_tensor(total[b][:, :], total[b][:, :], part[:, :], ALU.add)
                    if k == 1:
                        chain(add)
                    else:
                        add.then_inc(total_done, 1)
            for b in range(2):
                step(b, 0, b, True)
            with dve.Fori(1, KT // 2) as i:
                for b in range(2):
                    step(i * 2 + b, i, b)


def layer_norm(dve, step, act_root, y, stats, mv, w, b, halves):
    for h in range(2):
        step(dve.bn_stats(stats[:, h, :], halves[h]))
    step(dve.bn_aggr(mv[:, :], stats[:, :, :].rearrange("p h s -> p (h s)")))
    act_root()
    step(dve.reciprocal(mv[:, 1:2], mv[:, 1:2]))
    step(dve.tensor_scalar(y, y, mv[:, 0:1], mv[:, 1:2], ALU.subtract, ALU.mult))
    step(dve.tensor_tensor(y, y, w[:, :], ALU.mult))
    step(dve.tensor_tensor(y, y, b[:, :], ALU.add))


def project_out(nc, A, merged, x1, par):
    with Phase(nc) as local:
        sem = lambda name: local.sem(name)
        sb = lambda name, shape, dt=F32: local.enter_context(nc.sbuf_tensor(name, shape, dt))
        raw_m, raw_w = [sb(f"o_raw_m{b}", [P, T]) for b in range(2)], [sb(f"o_raw_w{b}", [P, D]) for b in range(2)]
        mhi, mlo, whi, wlo = (sb("o_" + n, [P, KT, T], F32R) for n in ("mhi", "mlo", "whi", "wlo"))
        x, y = [sb(f"o_x{b}", [P, D]) for b in range(2)], [sb(f"o_y{b}", [P, D]) for b in range(2)]
        ln_w, ln_b, stats, mv = sb("o_ln_w", [P, D]), sb("o_ln_b", [P, D]), sb("o_stats", [P, 2, 6]), sb("o_mv", [P, 2])
        ps = [local.enter_context(nc.psum_tensor(f"o_ps{n}", [P, 2, HALF], F32)) for n in range(4)]
        landed, x_landed, stored = [sem(f"o_landed{b}") for b in range(2)], [sem(f"o_x_landed{b}") for b in range(2)], [sem(f"o_stored{b}") for b in range(2)]
        ln_landed, hi_done, lo_done, mm_done, added, dve_step, mv_done, root_done, y_done = (
            sem("o_" + n) for n in ("ln_landed", "hi_done", "lo_done", "mm_done", "added", "dve", "mv_done", "root_done", "y_done"))
        block = local.open_block()

        @block.sync
        def _(sp):
            for k in range(KT):
                b = k % 2
                if k >= 2:
                    sp.wait_ge(lo_done, 2 * (k - 1))
                sp.dma_start(raw_m[b][:, :], merged[k]).then_inc(landed[b], 16)
                sp.dma_start(raw_w[b][:, :], A["w_out"][0][k * P:(k + 1) * P, :]).then_inc(landed[b], 16)
            sp.dma_start(ln_w[:, :], A["ln1_w"].to_broadcast([P, D])).then_inc(ln_landed, 16)
            sp.dma_start(ln_b[:, :], A["ln1_b"].to_broadcast([P, D])).then_inc(ln_landed, 16)
            for n in range(8):
                if n >= 2:
                    sp.wait_ge(added, n - 1)
                sp.dma_start(x[n % 2][:, :], A["x"][0][n * P:(n + 1) * P, :]).then_inc(x_landed[n % 2], 16)

        @block.scalar
        def _(act):
            for k in range(KT):
                b = k % 2
                act.wait_ge(landed[b], 32 * (k // 2 + 1))
                act.activation(mhi[:, k, :], raw_m[b][:, :], ACT.Copy).then_inc(hi_done, 1)
                act.activation(whi[:, k, :], raw_w[b][:, :], ACT.Copy).then_inc(hi_done, 1)
            for n in range(8):
                act.wait_ge(mv_done, n + 1)
                act.activation(mv[:, 1:2], mv[:, 1:2], ACT.Sqrt, bias=par("eps_ln")).then_inc(root_done, 1)
                act.wait_ge(y_done, n + 1)
                act.dma_start(x1[n * P:(n + 1) * P, :], y[n % 2][:, :]).then_inc(stored[n % 2], 16)
            for b in range(2):
                act.wait_ge(stored[b], 64)

        @block.tensor
        def _(pe):
            for n in range(8):
                if n >= 4:
                    pe.wait_ge(added, n - 3)
                for h in range(2):
                    for k in range(KT):
                        if n == 0 and h == 0:
                            pe.wait_ge(lo_done, 2 * k + 2)
                        last = split_dot(pe, ps[n % 4][:, h, :], mhi[:, k, n * P:(n + 1) * P], mlo[:, k, n * P:(n + 1) * P],
                                         whi[:, k, h * HALF:(h + 1) * HALF], wlo[:, k, h * HALF:(h + 1) * HALF], k == 0, k == KT - 1)
                last.then_inc(mm_done, 1)

        @block.vector
        def _(dve):
            for k in range(KT):
                b = k % 2
                dve.wait_ge(hi_done, 2 * k + 2)
                dve.tensor_tensor(mlo[:, k, :], raw_m[b][:, :], as_f32(mhi[:, k, :]), ALU.subtract).then_inc(lo_done, 1)
                dve.tensor_tensor(wlo[:, k, :], raw_w[b][:, :], as_f32(whi[:, k, :]), ALU.subtract).then_inc(lo_done, 1)
            dve.wait_ge(ln_landed, 32)
            step = Chain(dve, dve_step)
            for n in range(8):
                b = n % 2
                dve.wait_ge(x_landed[b], 16 * (n // 2 + 1))
                dve.wait_ge(mm_done, n + 1)
                if n >= 2:
                    dve.wait_ge(stored[b], 16 * (n // 2))
                dve.scalar_tensor_tensor(y[b][:, :], x[b][:, :], ALPHA, ps[n % 4][:, :, :].rearrange("p h t -> p (h t)"),
                                         ALU.mult, ALU.add).then_inc(added, 1)
                dve.wait_ge(added, n + 1)

                def root():
                    dve.sem_inc(mv_done, 1)
                    dve.wait_ge(root_done, n + 1)
                layer_norm(dve, step, root, y[b][:, :], stats, mv, ln_w, ln_b, [y[b][:, h * HALF:(h + 1) * HALF] for h in range(2)])
                dve.sem_inc(y_done, 1)


def feed_forward(nc, A, xhi, xlo, y, out, par):
    NF = FF // P
    with Phase(nc) as local:
        sem = lambda name: local.sem(name)
        sb = lambda name, shape, dt=F32: local.enter_context(nc.sbuf_tensor(name, shape, dt))
        NAMES = ("gate", "up", "down")
        raw = [{n: sb(f"ff_raw_{n}{b}", [P, KT, P]) for n in NAMES} for b in range(2)]
        whi = [{n: sb(f"ff_hi_{n}{b}", [P, KT, P], F32R) for n in NAMES} for b in range(2)]
        wlo = [{n: sb(f"ff_lo_{n}{b}", [P, KT, P], F32R) for n in NAMES} for b in range(2)]
        hid = sb("ff_hid", [P, 2, HALF])
        hhi, hlo = [sb(f"ff_hhi{b}", [P, T], F32R) for b in range(2)], [sb(f"ff_hlo{b}", [P, T], F32R) for b in range(2)]
        ps_g, ps_u = (local.enter_context(nc.psum_tensor("ff_" + n, [P, 2, HALF], F32)) for n in ("ps_g", "ps_u"))
        ps_d = [local.enter_context(nc.psum_tensor(f"ff_d{n}", [P, HALF], F32)) for n in range(4)]
        landed = [sem(f"ff_landed{b}") for b in range(2)]
        hi_done, lo_done, mm_g, mm_u, mm_d, silu_done, mul_done, hhi_done, hlo_done, added = (
            sem("ff_" + n) for n in ("hi_done", "lo_done", "mm_g", "mm_u", "mm_d", "silu_done", "mul_done", "hhi_done", "hlo_done", "added"))
        flat = lambda w: w[:, :, :].rearrange("p k n -> p (k n)")

        def steps(eng, make, add):
            make(0, 0, 0)
            with eng.Fori(0, NF // 2 - 1) as i:
                make(i * 2 + 1, i, 1)
                add(i * 2, 0)
                make(i * 2 + 2, i + 1, 0)
                add(i * 2 + 1, 1)
            make(NF - 1, NF // 2 - 1, 1)
            add(NF - 2, 0)
            add(NF - 1, 1)

        block = local.open_block()

        @block.sync
        def _(sp):
            sp.sem_inc(lo_done, 6)
            def make(f, i, b):
                sp.wait_ge(lo_done, f * 3 + 3)
                for n in ("gate", "up"):
                    sp.dma_start(raw[b][n][:, :, :], A["ffn_" + n][0][:, bass.ds(f * P, P)].rearrange("(k p) n -> p k n", p=P)).then_inc(landed[b], 16)
                sp.dma_start(flat(raw[b]["down"]), A["ffn_down"][0][bass.ds(f * P, P), :]).then_inc(landed[b], 16)
            steps(sp, make, lambda f, b: None)

        @block.scalar
        def _(act):
            act.sem_inc(mm_d, 32)
            act.sem_inc(mm_u, 4)
            act.sem_inc(hlo_done, 2)
            def split(b, *names):
                for n in names:
                    act.activation(whi[b][n][:, :, :], raw[b][n][:, :, :], ACT.Copy).then_inc(hi_done, 1)

            def split_gate_up(f, i, b):
                act.wait_ge(landed[b], i * 48 + 48)
                act.wait_ge(mm_u, f * 2 + 2)
                split(b, "gate", "up")

            def split_down(f, b):
                act.wait_ge(mm_d, f * 16 + 16)
                split(b, "down")

            def hidden(f, b):
                act.wait_ge(mm_g, f + 1)
                act.wait_ge(hlo_done, f * 2 + 2)
                act.activation(hid[:, :, :], ps_g[:, :, :], ACT.Silu).then_inc(silu_done, 1)
                for h in range(2):
                    act.wait_ge(mul_done, f * 2 + (h + 3))
                    act.activation(hhi[b][:, h * HALF:(h + 1) * HALF], hid[:, h, :], ACT.Copy).then_inc(hhi_done, 1)
            split_gate_up(0, 0, 0)
            split_down(0, 0)
            with act.Fori(0, NF // 2 - 1) as i:
                split_gate_up(i * 2 + 1, i, 1)
                hidden(i * 2, 0)
                split_down(i * 2 + 1, 1)
                split_gate_up(i * 2 + 2, i + 1, 0)
                hidden(i * 2 + 1, 1)
                split_down(i * 2 + 2, 0)
            split_gate_up(NF - 1, NF // 2 - 1, 1)
            hidden(NF - 2, 0)
            split_down(NF - 1, 1)
            hidden(NF - 1, 1)

        @block.gpsimd
        def _(pool):
            def make(f, i, b):
                for k, n in enumerate(NAMES):
                    pool.wait_ge(hi_done, f * 3 + (k + 1))
                    pool.tensor_tensor(wlo[b][n][:, :, :], raw[b][n][:, :, :], as_f32(whi[b][n][:, :, :]), ALU.subtract).then_inc(lo_done, 1)
            steps(pool, make, lambda f, b: None)

        @block.tensor
        def _(pe):
            def make(f, i, b):
                for name, ps, done in (("gate", ps_g, mm_g), ("up", ps_u, mm_u)):
                    if name == "gate":
                        pe.wait_ge(lo_done, f * 3 + 7)
                        pe.wait_ge(silu_done, f + 1)
                    else:
                        pe.wait_ge(lo_done, f * 3 + 8)
                        pe.wait_ge(mul_done, f * 2 + 2)
                    for h in range(2):
                        for k in range(KT):
                            cols = slice(h * HALF, (h + 1) * HALF)
                            last = split_dot(pe, ps[:, h, :], whi[b][name][:, k, :], wlo[b][name][:, k, :],
                                             xhi[:, k, cols], xlo[:, k, cols], k == 0, k == KT - 1)
                        if name == "up" or h:
                            last.then_inc(done, 1)

            def add(f, b):
                pe.wait_ge(hlo_done, f * 2 + 4)
                pe.wait_ge(lo_done, f * 3 + 9)
                dhi, dlo = flat(whi[b]["down"]), flat(wlo[b]["down"])
                for n in range(16):
                    pe.wait_ge(added, f * 16 + (n + 1))
                    tok, cols = slice(n // 2 * P, (n // 2 + 1) * P), slice(n % 2 * HALF, (n % 2 + 1) * HALF)
                    split_dot(pe, ps_d[n % 4][:, :], hhi[b][:, tok], hlo[b][:, tok], dhi[:, cols], dlo[:, cols], True, True).then_inc(mm_d, 1)
            pe.sem_inc(silu_done, 1)
            pe.sem_inc(mul_done, 2)
            pe.sem_inc(added, 4)
            steps(pe, make, add)

        @block.vector
        def _(dve):
            def make(f, i, b):
                dve.wait_ge(silu_done, f + 2)
                for h in range(2):
                    cols = slice(h * HALF, (h + 1) * HALF)
                    dve.wait_ge(mm_u, f * 2 + (h + 5))
                    dve.wait_ge(mm_d, f * 16 + 16)
                    dve.tensor_tensor(hid[:, h, :], hid[:, h, :], ps_u[:, h, :], ALU.mult).then_inc(mul_done, 1)
                    dve.wait_ge(hhi_done, f * 2 + (h + 1))
                    dve.tensor_tensor(hlo[b][:, cols], hid[:, h, :], as_f32(hhi[b][:, cols]), ALU.subtract).then_inc(hlo_done, 1)

            def add(f, b):
                for n in range(16):
                    dve.wait_ge(mm_d, f * 16 + (n + 33))
                    part = y[:, n // 2, n % 2 * HALF:(n % 2 + 1) * HALF]
                    dve.tensor_tensor(part, part, ps_d[n % 4][:, :], ALU.add).then_inc(added, 1)
            steps(dve, make, add)

    with Phase(nc) as local:
        sem = lambda name: local.sem(name)
        sb = lambda name, shape, dt=F32: local.enter_context(nc.sbuf_tensor(name, shape, dt))
        NT = T // P
        ln_w, ln_b = sb("l_ln_w", [P, D]), sb("l_ln_b", [P, D])
        stats, mv = sb("l_stats", [P, NT, 2, 6]), sb("l_mv", [P, NT, 2])
        ln_landed, stats_done, mv_done, root_done, rstd_done, norm_done, scale_done, y_done, stored = (
            sem("l_" + n) for n in ("ln_landed", "stats_done", "mv_done", "root_done", "rstd_done", "norm_done", "scale_done", "y_done", "stored"))
        block = local.open_block()

        @block.sync
        def _(sp):
            sp.dma_start(ln_w[:, :], A["ln2_w"].to_broadcast([P, D])).then_inc(ln_landed, 16)
            sp.dma_start(ln_b[:, :], A["ln2_b"].to_broadcast([P, D])).then_inc(ln_landed, 16)
            for n in range(NT):
                sp.wait_ge(y_done, n + 1)
                sp.dma_start(out[0][n * P:(n + 1) * P, :], y[:, n, :]).then_inc(stored, 16)
            sp.wait_ge(stored, 16 * NT)

        @block.scalar
        def _(act):
            act.wait_ge(mv_done, NT)
            act.activation(mv[:, :, 1], mv[:, :, 1], ACT.Sqrt, bias=par("eps_ln")).then_inc(root_done, 1)

        @block.vector
        def _(dve):
            for n in range(NT):
                for h in range(2):
                    dve.bn_stats(stats[:, n, h, :], y[:, n, h * HALF:(h + 1) * HALF]).then_inc(stats_done, 1)
                if n:
                    dve.wait_ge(stats_done, 2 * n)
                    dve.bn_aggr(mv[:, n - 1, :], stats[:, n - 1, :, :].rearrange("p h s -> p (h s)")).then_inc(mv_done, 1)
            dve.wait_ge(stats_done, 2 * NT)
            dve.bn_aggr(mv[:, NT - 1, :], stats[:, NT - 1, :, :].rearrange("p h s -> p (h s)")).then_inc(mv_done, 1)
            dve.wait_ge(root_done, 1)
            dve.reciprocal(mv[:, :, 1], mv[:, :, 1]).then_inc(rstd_done, 1)
            dve.wait_ge(rstd_done, 1)
            dve.wait_ge(ln_landed, 32)
            for n in range(NT + 2):
                if n < NT:
                    dve.tensor_scalar(y[:, n, :], y[:, n, :], mv[:, n, 0:1], mv[:, n, 1:2], ALU.subtract, ALU.mult).then_inc(norm_done, 1)
                if 0 < n <= NT:
                    dve.wait_ge(norm_done, n)
                    dve.tensor_tensor(y[:, n - 1, :], y[:, n - 1, :], ln_w[:, :], ALU.mult).then_inc(scale_done, 1)
                if n > 1:
                    dve.wait_ge(scale_done, n - 1)
                    dve.tensor_tensor(y[:, n - 2, :], y[:, n - 2, :], ln_b[:, :], ALU.add).then_inc(y_done, 1)


PARAM_NAMES = ("rwkv_mu", "rwkv_w0", "rwkv_a0", "rwkv_k_k", "rwkv_k_a", "rwkv_r_k", "rwkv_lnx_w", "rwkv_lnx_b",
               "gdn_conv", "gdn_norm_w", "gdn_a_log", "gdn_dt_bias", "swa_sinks")
INPUTS = ("x", "w_in") + PARAM_NAMES + ("rwkv_w_up", "rwkv_a_up", "rwkv_g_up", "w_branch_a", "w_branch_b", "w_branch_c",
                                        "w_out", "ln1_w", "ln1_b", "ffn_gate", "ffn_up", "ffn_down", "ln2_w", "ln2_b")


def hybrid_layer_kernel(nc, A, const_dram, out):
    dram = lambda name, shape: nc.dram_tensor(name, shape, F32, kind="Internal").ap()
    u = dram("u", [(ALL_TILES + 1) * P, T])
    rows, egl = dram("rows", [5, GH, T]), dram("egl", [GH, NCH])
    opnd, bonus = dram("opnd", [NCH, P, N_OP * 4 * C]), dram("bonus", [RH * RD, T])
    nt, xinv = dram("nt", [NCH, P, NPAIR, NB]), dram("xinv", [NCH, P, 2, NPAIR, NB])
    mixed, attended = dram("mixed", [NCH, P, 8, C]), dram("attended", [NCH, P, 4, C])
    merged, x1 = dram("merged", [KT, P, T]), dram("x1", [T, D])
    with ExitStack() as ctx:
        sb = lambda stack, name, shape, dt=F32: stack.enter_context(nc.sbuf_tensor(name, shape, dt))
        par = Params(sb(ctx, "params", [P, N_PARAM]))
        tab = Tables(sb(ctx, "tables", [P, CONST.shape[1]]))
        par_landed = ctx.enter_context(nc.semaphore("par_landed"))
        with ExitStack() as s:
            gl, plast = sb(s, "gl", [P, T]), sb(s, "plast", [P, 4 * NCH])
            with ExitStack() as sx:
                xhi, xlo = sb(sx, "xhi", [P, KT, T], F32R), sb(sx, "xlo", [P, KT, T], F32R)
                with nc.sbuf_tensor("xin", [P, 8, D], F32) as xin:
                    with nc.Block() as block:
                        @block.gpsimd
                        def _(pool):
                            pool.wait_ge(par_landed, load_params(nc, pool, par, A, par_landed))
                    transpose_x(nc, A["x"][0], xin, xhi, xlo, tab, const_dram)
                project_in(nc, A["w_in"][0], xhi, xlo, u)
                wa = sb(sx, "wa", [P, T])
                prepare_rows(nc, u, rows, egl, par, tab, wa, gl)
                prepare_rwkv(nc, A, u, opnd, bonus, plast, par, tab, wa, xhi, xlo)
                prepare_gdn(nc, A, u, rows, opnd, par, tab, xhi, xlo)
            with ExitStack() as s2:
                gates_tile, cols, egl_bc = sb(s2, "decays", [P, NCH, 2, 2, C]), sb(s2, "cols", [P, NCH, 3, 2]), sb(s2, "egl_bc", [P, GH, NCH])
                prepare_decays(nc, rows, egl, gates_tile, cols, egl_bc, tab)
                diagonal_blocks(nc, opnd, gates_tile, nt, tab)
                invert_blocks(nc, nt, xinv)
                scan_chunks(nc, opnd, xinv, gates_tile, cols, egl_bc, plast, mixed, tab)
            window_attention(nc, u, attended, par, tab)
            oh, ol = sb(s, "oh", [P, 12, T], F32R), sb(s, "ol", [P, 12, T], F32R)
            finish_mixers(nc, A, u, mixed, attended, bonus, gl, oh, ol, par, tab)
            project_branches(nc, A, u, oh, ol, merged)
        project_out(nc, A, merged, x1, par)
        with ExitStack() as s:
            y = sb(s, "y", [P, 8, D])
            xhi, xlo = sb(s, "x1hi", [P, KT, T], F32R), sb(s, "x1lo", [P, KT, T], F32R)
            transpose_x(nc, x1, y, xhi, xlo, tab, scaled=ALPHA)
            feed_forward(nc, A, xhi, xlo, y, out, par)


def kernel(**inputs):
    import concourse.bacc as bacc
    from concourse.bass_utils import run_bass_kernel_spmd

    nc = bacc.Bacc("TRN2", target_bir_lowering=False, num_devices=1)
    arrays, A = {}, {}
    for name in INPUTS:
        a = np.ascontiguousarray(inputs[name])
        arrays[f"in_{name}"] = a
        A[name] = nc.dram_tensor(f"in_{name}", a.shape, mybir.dt.from_np(a.dtype), kind="ExternalInput").ap()
    arrays["in_const"] = CONST
    const_dram = nc.dram_tensor("in_const", CONST.shape, F32, kind="ExternalInput").ap()
    out = nc.dram_tensor("out_0", (1, T, D), F32, kind="ExternalOutput").ap()
    hybrid_layer_kernel(nc, A, const_dram, out)
    return run_bass_kernel_spmd(nc, [arrays], core_ids=[0]).results[0]["out_0"]
```

```python
import math
from contextlib import ExitStack

import numpy as np

import concourse.bass as bass
from concourse import mybir

F32 = mybir.dt.float32
F32R = mybir.dt.float32r
ALU = mybir.AluOpType
ACT = mybir.ActivationFunctionType
AX = mybir.AxisListType

P = 128
D = 1024
T = 1024
KT = D // P
HALF = 512
C = 64
NCH = T // C
GH, GD = 4, 128
RH, RD = 8, 64
SH, SKV, SD = 8, 2, 64
FF = 2816
ALPHA = 2 ** 0.25
LN_EPS, GDN_EPS, LNX_EPS, L2_EPS = 1e-5, 1e-6, 64e-5, 1e-6

A_TILES = 16
SMALL = A_TILES * P
REST = SMALL + 2 * GH
N_IN = 7688
ALL_TILES = (N_IN - 2 * GH) // P
U_Q, U_K, U_V, U_Z = 0, 4, 8, 12
U_R, U_RK, U_RV, U_WA, U_G = 16, 20, 24, 28, 29
U_SQ, U_SK, U_SV, U_GATE = 30, 34, 35, 36
U_SMALL = ALL_TILES

O_B, O_A, O_R, O_K, O_V, O_GK, O_GKB, O_GQ, O_GQD, O_GV = range(10)
N_OP = 10
R_GC, R_NBEG, R_TAIL, R_BETA, R_EG = range(5)
NPAIR = 6
NB = 32


def constants():
    at, cols, out = {}, 0, []

    def put(name, a):
        nonlocal cols
        a = np.asarray(a, np.float32)
        at[name] = (cols, a.shape[1])
        cols += a.shape[1]
        out.append(a)

    r, c = np.arange(P)[:, None], np.arange(P)[None, :]
    put("ident", r == c)
    put("ones", np.ones((P, P)))
    put("head_ones", r // 64 == c // 64)
    s, t = np.arange(P)[:, None] % C, np.arange(C)[None, :]
    put("ident2", s == t)
    put("strict", t > s)
    put("causal", t >= s)
    put("minus_strict", -1.0 * (t > s))
    put("causal_again", t >= s)
    put("corner", (s < 32) & (t >= 32))
    put("in_chunk", np.broadcast_to(np.arange(T) % C != 0, (P, T)))
    q, k = np.arange(P)[:, None] % C, np.arange(2 * C)[None, :]
    for first in (0, 1):
        for j in range(4):
            head = 2 * j + np.arange(P)[:, None] // C
            m = -np.exp2(-8.0 * (head + 1) / SH) * np.abs(q + C - k)
            put(f"alibi{first}{j}", np.where((k < C) & (first == 1), -1e30, m))
    return at, np.concatenate(out, axis=1)


CONST_AT, CONST = constants()


class Tables:

    def __init__(self, tile):
        self.tile = tile

    def __call__(self, name, n=None, rows=P):
        at, width = CONST_AT[name]
        return self.tile[0:rows, at:at + (n or width)]


class Phase(ExitStack):

    def __init__(self, nc):
        super().__init__()
        self.nc, self.sems = nc, []

    def sem(self, name):
        self.sems.append(self.enter_context(self.nc.semaphore(name)))
        return self.sems[-1]

    def open_block(self):
        self.callback(self.clear)
        return self.enter_context(self.nc.Block())

    def clear(self):
        with self.nc.Block() as block:
            @block.gpsimd
            def _(pool):
                for s in self.sems:
                    pool.sem_clear(s)


def turn(eng, turns):
    eng.sem_inc(turns, 1)


def split_dot(pe, out, w_hi, w_lo, x_hi, x_lo, first, last):
    pe.matmul(out, w_hi, x_hi, start=first, stop=False)
    pe.matmul(out, w_hi, x_lo, start=False, stop=False)
    return pe.matmul(out, w_lo, x_hi, start=False, stop=last)


def as_f32(t):
    return t.bitcast(F32)


def transpose_x(nc, x, xin, xhi, xlo, tab, const_dram=None, scaled=None):
    with Phase(nc) as local:
        tag = "" if scaled is None else "1"
        bank = [local.enter_context(nc.psum_tensor(f"xt{tag}{b}", [P, HALF], F32)) for b in range(8)]
        landed = [local.sem(f"x_landed{tag}_{i}") for i in range(8)]
        const_landed = local.sem("const_landed" + tag)
        turned = local.sem("x_turned" + tag)
        hi_done = local.sem("x_hi_done" + tag)
        lo_done = local.sem("x_lo_done" + tag)
        block = local.open_block()

        @block.sync
        def _(sp):
            if const_dram is not None:
                sp.dma_start(tab.tile[:, :], const_dram).then_inc(const_landed, 16)
            for i in range(8):
                sp.dma_start(xin[:, i, :], x[i * P:(i + 1) * P, :]).then_inc(landed[i], 16)

        @block.tensor
        def _(pe):
            if const_dram is not None:
                pe.wait_ge(const_landed, 16)
            for n in range(16):
                half, k = n // 8, n % 8
                if k == 0:
                    for i in range(4):
                        pe.wait_ge(landed[4 * half + i], 16)
                if n >= 8:
                    pe.wait_ge(lo_done, n - 7)
                for i in range(4):
                    last = pe.transpose(bank[n % 8][:, i * P:(i + 1) * P],
                                        xin[:, 4 * half + i, k * P:(k + 1) * P], tab("ident"))
                last.then_inc(turned, 1)

        @block.scalar
        def _(act):
            for n in range(16):
                half, k = n // 8, n % 8
                act.wait_ge(turned, n + 1)
                act.activation(xhi[:, k, half * HALF:(half + 1) * HALF], bank[n % 8][:, :],
                               ACT.Copy).then_inc(hi_done, 1)

        @block.vector
        def _(dve):
            for n in range(16):
                half, k = n // 8, n % 8
                cols = slice(half * HALF, (half + 1) * HALF)
                dve.wait_ge(hi_done, n + 1)
                dve.tensor_tensor(xlo[:, k, cols], bank[n % 8][:, :], as_f32(xhi[:, k, cols]),
                                  ALU.subtract).then_inc(lo_done, 1)
                if scaled is not None and k == KT - 1:
                    dve.tensor_scalar(xin[:, 4 * half:4 * half + 4, :], xin[:, 4 * half:4 * half + 4, :], scaled, None, ALU.mult)


def project_in(nc, w_in, xhi, xlo, u):
    W = 2 * P
    w_rows = w_in.rearrange("(k p) n -> p k n", p=P)
    u_rows = u.rearrange("(n p) t -> p n t", p=P)
    with Phase(nc) as local:
        raw = [local.enter_context(nc.sbuf_tensor(f"w_raw{b}", [P, KT, W], F32)) for b in range(2)]
        whi = [local.enter_context(nc.sbuf_tensor(f"w_hi{b}", [P, KT, W], F32R)) for b in range(2)]
        wlo = [local.enter_context(nc.sbuf_tensor(f"w_lo{b}", [P, KT, W], F32R)) for b in range(2)]
        res = [local.enter_context(nc.sbuf_tensor(f"u_out{b}", [P, 2, T], F32)) for b in range(2)]
        bank = [[local.enter_context(nc.psum_tensor(f"u_ps{b}{a}", [P, 2, HALF], F32))
                 for a in range(2)] for b in range(2)]
        sem = lambda name: local.sem(name)
        landed = [sem(f"w_landed{b}") for b in range(2)]
        stored = [sem(f"u_stored{b}") for b in range(2)]
        hi_done, lo_done, mm_done, evacuated = sem("w_hi_done"), sem("w_lo_done"), sem("u_mm_done"), sem("u_evac")
        block = local.open_block()

        LOOPS = ((0, 0, U_Z // 4), (REST, A_TILES, (U_SQ - A_TILES) // 4))

        def loads(eng, step):
            j0 = 0
            for col0, row0, n in LOOPS:
                with eng.Fori(0, n) as i:
                    for b in range(2):
                        step(i * 2 + (2 * j0 + b), i + j0, b, i * (2 * W) + (col0 + b * W),
                             i * 4 + (row0 + 2 * b), 2)
                j0 += n
            step(2 * j0, j0, 0, REST + (U_SQ - 2 - A_TILES) * P, U_SQ - 2, 2)
            step(2 * j0 + 1, j0, 1, REST - P, U_SMALL, 1)

        @block.sync
        def _(sp):
            def step(m, j, b, col, row, tiles):
                sp.wait_ge(hi_done, m + 1)
                sp.wait_ge(lo_done, m + 1)
                sp.dma_start(raw[b][:, :, 0:tiles * P],
                             w_rows[:, :, bass.ds(col, tiles * P)]).then_inc(landed[b], 16)
            loads(sp, step)

        @block.vector
        def _(dve):
            dve.sem_inc(hi_done, 2)
            dve.sem_inc(lo_done, 2)

            def step(m, j, b, col, row, tiles):
                n = slice(0, tiles * P)
                dve.wait_ge(landed[b], j * 16 + 16)
                dve.wait_ge(mm_done, m * 2 + 2)
                dve.tensor_copy(whi[b][:, :, n], raw[b][:, :, n]).then_inc(hi_done, 1)
                dve.wait_ge(hi_done, m + 3)
                dve.tensor_tensor(wlo[b][:, :, n], raw[b][:, :, n], as_f32(whi[b][:, :, n]),
                                  ALU.subtract).then_inc(lo_done, 1)
            loads(dve, step)

        @block.tensor
        def _(pe):
            pe.sem_inc(mm_done, 4)

            def step(m, j, b, col, row, tiles):
                pe.wait_ge(lo_done, m + 3)
                for a in range(tiles):
                    pe.wait_ge(evacuated, m * 2 + (a + 1))
                    for k in range(KT):
                        for h in range(2):
                            last = split_dot(pe, bank[b][a][:, h, :],
                                             whi[b][:, k, a * P:(a + 1) * P], wlo[b][:, k, a * P:(a + 1) * P],
                                             xhi[:, k, h * HALF:(h + 1) * HALF], xlo[:, k, h * HALF:(h + 1) * HALF],
                                             k == 0, k == KT - 1)
                    last.then_inc(mm_done, 1)
            loads(pe, step)

        @block.scalar
        def _(act):
            act.sem_inc(evacuated, 4)
            for b in range(2):
                act.sem_inc(stored[b], 16)

            def step(m, j, b, col, row, tiles):
                act.wait_ge(stored[b], j * 16 + 16)
                for a in range(tiles):
                    act.wait_ge(mm_done, m * 2 + (a + 5))
                    act.activation(res[b][:, a, :], bank[b][a][:, :, :].rearrange("p h t -> p (h t)"),
                                   ACT.Copy).then_inc(evacuated, 1)
                act.wait_ge(evacuated, m * 2 + (tiles + 4))
                act.dma_start(u_rows[:, bass.ds(row, tiles), :], res[b][:, 0:tiles, :]).then_inc(stored[b], 16)
            loads(act, step)
            for b in range(2):
                act.wait_ge(stored[b], 16 * (2 + sum(n for _, _, n in LOOPS)))


class SpareColumns:

    def __init__(self, nc, local, w_in, u, xhi, xlo, first, count, per, tiles=None):
        self.tiles = tiles
        self.nc, self.w_in, self.u, self.xhi, self.xlo = nc, w_in, u, xhi, xlo
        self.first, self.count, self.per = first, count, per
        self.in_last = (count - 1) % per + 1
        sb = lambda name, shape, dt=F32: [local.enter_context(nc.sbuf_tensor(f"{name}{first}_{b}", shape, dt)) for b in range(2)]
        sem = lambda name: local.sem(f"{name}{first}")
        self.raw, self.whi, self.wlo = sb("sc_raw", [P, KT, P]), sb("sc_hi", [P, KT, P], F32R), sb("sc_lo", [P, KT, P], F32R)
        self.res = sb("sc_res", [P, T])
        self.bank = [local.enter_context(nc.psum_tensor(f"sc_ps{first}_{h}", [P, HALF], F32)) for h in range(2)]
        self.landed, self.stored = [sem(f"sc_landed{b}_") for b in range(2)], [sem(f"sc_stored{b}_") for b in range(2)]
        self.hi_done, self.lo_done, self.mm_done, self.evacuated, self.turns = (
            sem("sc_" + n) for n in ("hi_done", "lo_done", "mm_done", "evacuated", "turns"))

    def load(self, act, m, b):
        w_rows = self.w_in.rearrange("(k p) n -> p k n", p=P)
        row = self.row_of(m)
        in_a = self.tiles is not None and row < A_TILES * P
        col = row + (0 if in_a else REST - A_TILES * P)
        act.dma_start(self.raw[b][:, :, :], w_rows[:, :, bass.ds(col, P)]).then_inc(self.landed[b], 16)

    def row_of(self, m):
        return m * P + self.first * P if self.tiles is None else self.tiles[m] * P

    def pool_program(self, pool):
        with pool.Fori(0, self.count // 2) as i:
            for b in range(2):
                m = i * 2 + b
                pool.wait_ge(self.landed[b], i * 16 + 16)
                pool.wait_ge(self.mm_done, m * 2 + 2)
                turn(pool, self.turns)
                pool.tensor_copy(self.whi[b][:, :, :], self.raw[b][:, :, :]).then_inc(self.hi_done, 1)
                pool.wait_ge(self.hi_done, m + 1)
                pool.tensor_tensor(self.wlo[b][:, :, :], self.raw[b][:, :, :], as_f32(self.whi[b][:, :, :]),
                                   ALU.subtract).then_inc(self.lo_done, 1)

    def place(self, i, q):
        m = i * self.per + q
        return m, m % 2 if isinstance(m, int) else q % 2

    def pe_begin(self, pe):
        pe.sem_inc(self.mm_done, 4)

    def pe_tile(self, pe, i, q):
        m, b = self.place(i, q)
        pe.wait_ge(self.lo_done, m + 1)
        for h in range(2):
            pe.wait_ge(self.evacuated, m * 2 + (h + 1))
            for k in range(KT):
                cols = slice(h * HALF, (h + 1) * HALF)
                last = split_dot(pe, self.bank[h][:, :], self.whi[b][:, k, :], self.wlo[b][:, k, :],
                                 self.xhi[:, k, cols], self.xlo[:, k, cols], k == 0, k == KT - 1)
            last.then_inc(self.mm_done, 1)

    def act_begin(self, act):
        for b in range(2):
            self.load(act, b, b)
        act.sem_inc(self.evacuated, 2)
        for b in range(2):
            act.sem_inc(self.stored[b], 16)

    def act_tile(self, act, i, q, last_round):
        m, b = self.place(i, q)
        act.wait_ge(self.stored[b], m // 2 * 16 + 16 if isinstance(m, int) else i * (16 * self.per // 2) + (16 * (q // 2) + 16))
        for h in range(2):
            act.wait_ge(self.mm_done, m * 2 + (h + 5))
            act.activation(self.res[b][:, h * HALF:(h + 1) * HALF], self.bank[h][:, :], ACT.Copy).then_inc(self.evacuated, 1)
        if not (last_round and q + 2 >= self.in_last):
            self.load(act, m + 2, b)
        act.wait_ge(self.evacuated, m * 2 + 4)
        act.dma_start(self.u[bass.ds(self.row_of(m), P), :], self.res[b][:, :]).then_inc(self.stored[b], 16)

    def run_alone(self, block):
        @block.gpsimd
        def _(pool):
            self.pool_program(pool)

        @block.tensor
        def _(pe):
            self.pe_begin(pe)
            with pe.Fori(0, self.count // self.per) as i:
                for q in range(self.per):
                    self.pe_tile(pe, i, q)

        @block.scalar
        def _(act):
            self.act_begin(act)
            rounds = self.count // self.per
            for i in range(rounds):
                for q in range(self.per):
                    self.act_tile(act, i, q, i == rounds - 1)
            self.act_end(act)

    def act_end(self, act):
        for b in range(2):
            act.wait_ge(self.stored[b], 16 + 16 * self.count // 2)


PARAMS = {}


def _params():
    at = 0
    for name, n in (("mu", 14), ("w0", 4), ("a0", 4), ("k_k", 4), ("k_a", 4), ("r_k", 4), ("lnx_w", 4),
                    ("lnx_b", 4), ("conv", 48), ("norm_w", 1), ("a_log", 1), ("dt_bias", 1), ("sinks", 4),
                    ("one_minus_k_a", 4), ("minus_a", 1), ("eps_q", 1), ("eps_k", 1), ("eps_gdn", 1), ("eps_lnx", 1), ("eps_ln", 1)):
        PARAMS[name] = (at, n)
        at += n
    return at


N_PARAM = _params()


class Params:

    def __init__(self, tile):
        self.tile = tile

    def __call__(self, name, j=0, n=1, rows=P):
        return self.tile[0:rows, bass.ds(PARAMS[name][0] + j, n)]


def load_params(nc, sp, par, A, landed):
    n = 0

    def load(name, src, rows=slice(0, P)):
        nonlocal n
        at, width = PARAMS[name]
        sp.dma_start(par.tile[rows, at:at + width] if src.ndim == 2 else src, src).then_inc(landed, 16)
        n += 16

    with nc.allow_non_contiguous_dma(reason="parameters, once"):
        load("mu", A["rwkv_mu"][0].rearrange("(j p) -> p j", p=P))
        for name in ("w0", "a0", "k_k", "k_a", "lnx_w", "lnx_b"):
            load(name, A["rwkv_" + name][0].rearrange("(j p) -> p j", p=P))
        load("r_k", A["rwkv_r_k"][0].rearrange("(j e) d -> (e d) j", e=2))
        at = PARAMS["conv"][0]
        for tap in range(4):
            sp.dma_start(par.tile[:, at + 12 * tap:at + 12 * tap + 12],
                         A["gdn_conv"][0, tap].rearrange("(j p) -> p j", p=P)).then_inc(landed, 16)
            n += 16
        load("norm_w", A["gdn_norm_w"].rearrange("o p -> p o"))
        load("a_log", A["gdn_a_log"].rearrange("o p -> p o"), slice(0, GH))
        load("dt_bias", A["gdn_dt_bias"].rearrange("o p -> p o"), slice(0, GH))
        sinks = A["swa_sinks"].rearrange("o (j e) -> o e j", e=2)
        for e in range(2):
            load("sinks", sinks[:, e, :].to_broadcast([64, 4]), slice(64 * e, 64 * e + 64))
    return n


class Chain:

    def __init__(self, eng, sem, base=0):
        self.eng, self.sem, self.base, self.n = eng, sem, base, 0

    def __call__(self, instruction):
        instruction.then_inc(self.sem, 1)
        self.n += 1
        self.eng.wait_ge(self.sem, self.base + self.n)


def prepare_rows(nc, u, rows, egl, par, tab, wa, gl):
    with Phase(nc) as local:
        sb = lambda name, shape: local.enter_context(nc.sbuf_tensor(name, shape, F32))
        sem = lambda name: local.sem(name)
        r = {n: sb("row_" + n, [GH, T]) for n in ("b", "a", "x", "y", "u", "d", "z", "gc", "beta", "eg", "nbeg", "tail")}
        el = sb("row_el", [GH, NCH])
        uw, ug, dw = sb("uw", [P, 1 + T]), sb("ug", [P, 1 + T]), sb("dw", [P, T])
        landed_rows, landed_w, dve_step, act_step = sem("rows_landed"), sem("wg_landed"), sem("rows_dve"), sem("rows_act")
        stored, shifted = sem("rows_stored"), sem("wg_shifted")
        x_ready, y_ready, gc_ready, gc_exp_ready, b_ready, tail_ready = (
            sem(n) for n in ("x_ready", "y_ready", "gc_ready", "gc_exp_ready", "beta_ready", "tail_arg_ready"))
        rows_ready, tail_exp = sem("rows_ready"), sem("tail_exp")
        block = local.open_block()
        chunks = lambda t: t[:, :].rearrange("p (c s) -> p c s", s=C)

        @block.sync
        def _(sp):
            sp.dma_start(r["b"][:, :], u[U_SMALL * P + P - 2 * GH:U_SMALL * P + P - GH, :]).then_inc(landed_rows, 16)
            sp.dma_start(r["a"][:, :], u[U_SMALL * P + P - GH:U_SMALL * P + P, :]).then_inc(landed_rows, 16)
            sp.dma_start(uw[:, 1:], u[U_WA * P:(U_WA + 1) * P, :]).then_inc(landed_w, 16)
            sp.dma_start(ug[:, 1:], u[U_G * P:(U_G + 1) * P, :]).then_inc(landed_w, 16)
            sp.wait_ge(rows_ready, 1)
            sp.wait_ge(tail_exp, 2)
            for n, name in ((R_GC, "gc"), (R_NBEG, "nbeg"), (R_TAIL, "tail"), (R_BETA, "beta"), (R_EG, "eg")):
                sp.dma_start(rows[n], r[name][:, :]).then_inc(stored, 16)
            sp.dma_start(egl, el[:, :]).then_inc(stored, 16)
            sp.wait_ge(stored, 96)

        @block.vector
        def _(dve):
            step = Chain(dve, dve_step)
            dve.memset(uw[:, 0:1], 0.0)
            step(dve.memset(ug[:, 0:1], 0.0))
            step(dve.tensor_scalar(par("one_minus_k_a", 0, 4), par("k_a", 0, 4), -1.0, 1.0, ALU.mult, ALU.add))
            dve.memset(par("eps_q"), GD * L2_EPS)
            for name, value in (("eps_k", L2_EPS), ("eps_gdn", GDN_EPS), ("eps_lnx", LNX_EPS), ("eps_ln", LN_EPS)):
                step(dve.memset(par(name), value))
            dve.wait_ge(act_step, 1)
            step(dve.tensor_scalar(par("minus_a", rows=GH), par("minus_a", rows=GH), -1.0, None, ALU.mult))
            dve.wait_ge(landed_rows, 32)
            step(dve.tensor_scalar(r["x"][:, :], r["a"][:, :], par("dt_bias", rows=GH), None, ALU.add))
            step(dve.tensor_scalar(r["z"][:, :], r["x"][:, :], -1.0, None, ALU.mult))
            dve.tensor_tensor(r["z"][:, :], r["x"][:, :], r["z"][:, :], ALU.min).then_inc(x_ready, 1)
            dve.wait_ge(y_ready, 1)
            step(dve.tensor_scalar(r["u"][:, :], r["y"][:, :], 1.0, None, ALU.add))
            step(dve.tensor_scalar(r["d"][:, :], r["u"][:, :], -1.0, None, ALU.add))
            step(dve.tensor_scalar(r["z"][:, :], r["d"][:, :], 0.0, None, ALU.is_equal))
            dve.wait_ge(y_ready, 2)
            step(dve.tensor_tensor(r["d"][:, :], r["d"][:, :], r["z"][:, :], ALU.add))
            step(dve.reciprocal(r["d"][:, :], r["d"][:, :]))
            step(dve.tensor_tensor(r["a"][:, :], r["a"][:, :], r["z"][:, :], ALU.add))
            step(dve.tensor_tensor(r["a"][:, :], r["a"][:, :], r["d"][:, :], ALU.mult))
            step(dve.tensor_tensor(r["a"][:, :], r["a"][:, :], r["y"][:, :], ALU.mult))
            step(dve.scalar_tensor_tensor(r["a"][:, :], r["x"][:, :], 0.0, r["a"][:, :], ALU.max, ALU.add))
            step(dve.tensor_scalar(r["a"][:, :], r["a"][:, :], par("minus_a", rows=GH), None, ALU.mult))
            dve.tensor_tensor_scan(r["gc"][:, :], tab("in_chunk", rows=GH), r["a"][:, :], 0.0,
                                   ALU.mult, ALU.add).then_inc(gc_ready, 1)
            dve.wait_ge(gc_ready, 1)
            dve.tensor_tensor(chunks(r["tail"]), chunks(r["gc"])[:, :, C - 1:C].to_broadcast([GH, NCH, C]),
                              chunks(r["gc"]), ALU.subtract).then_inc(tail_ready, 1)
            dve.wait_ge(gc_exp_ready, 1)
            dve.wait_ge(b_ready, 1)
            dve.scalar_tensor_tensor(r["nbeg"][:, :], r["beta"][:, :], -1.0, r["eg"][:, :],
                                     ALU.mult, ALU.mult).then_inc(rows_ready, 1)
            dve.wait_ge(landed_w, 32)
            for raw, out, j in ((uw, wa, 12), (ug, gl, 13)):
                step(dve.tensor_tensor(dw[:, :], raw[:, 0:T], raw[:, 1:], ALU.subtract))
                step(dve.scalar_tensor_tensor(out[:, :], dw[:, :], par("mu", j), raw[:, 1:], ALU.mult, ALU.add))
            dve.sem_inc(shifted, 1)

        @block.scalar
        def _(act):
            act.activation(par("minus_a", rows=GH), par("a_log", rows=GH), ACT.Exp).then_inc(act_step, 1)
            act.wait_ge(x_ready, 1)
            act.activation(r["y"][:, :], r["z"][:, :], ACT.Exp).then_inc(y_ready, 1)
            act.wait_ge(y_ready, 1)
            act.activation(r["a"][:, :], r["y"][:, :], ACT.Ln, bias=1.0).then_inc(y_ready, 1)
            act.wait_ge(gc_ready, 1)
            act.activation(r["eg"][:, :], r["gc"][:, :], ACT.Exp).then_inc(gc_exp_ready, 1)
            act.activation(el[:, :], chunks(r["gc"])[:, :, C - 1], ACT.Exp).then_inc(tail_exp, 1)
            act.wait_ge(tail_ready, 1)
            act.activation(r["tail"][:, :], r["tail"][:, :], ACT.Exp).then_inc(tail_exp, 1)
            act.wait_ge(landed_rows, 32)
            act.activation(r["beta"][:, :], r["b"][:, :], ACT.Sigmoid).then_inc(b_ready, 1)
            act.wait_ge(shifted, 1)
            act.activation(wa[0:64, :], wa[0:64, :], ACT.Tanh).then_inc(act_step, 1)
            act.activation(gl[:, :], gl[:, :], ACT.Sigmoid).then_inc(act_step, 1)
            act.wait_ge(act_step, 3)


def prepare_rwkv(nc, A, u, opnd, bonus, plast, par, tab, wa, xhi, xlo, scratch):
    E5 = -math.exp(-0.5)
    with Phase(nc) as local:
        sb = lambda name, shape: local.enter_context(nc.sbuf_tensor(name, shape, F32))
        sem = lambda name: local.sem(name)
        raw = [sb("raw_" + n, [P, 1 + T]) for n in "rkv"]
        low_up = sb("low_up", [P, P])
        t = {n: sb("rw_" + n, [P, T]) for n in
             ("r", "k", "v", "a", "ep", "en", "ec", "kk", "nrm", "ao", "bo", "ko", "ro", "bonus")}
        t.update({n: scratch[:, k, :] for k, n in enumerate(("d", "sw", "lc", "lp"))})
        t["sq"] = t["ep"]
        t["rk"] = t["bonus"]
        z_ps, a_ps, n_ps = (local.enter_context(nc.psum_tensor(n, [P, 2, HALF], F32)) for n in ("z_ps", "a_ps", "n_ps"))
        b_ps = z_ps
        spare = SpareColumns(nc, local, A["w_in"][0], u, xhi, xlo, U_GATE + 8, 16, 4)
        flat = lambda p: p[:, :, :].rearrange("p h t -> p (h t)")
        landed, up_landed, stored = [sem(f"rkv_landed{n}") for n in range(3)], sem("up_landed"), sem("rw_stored")
        low_done, sig_done, dve_step, lc_done, exp_done = (sem(n) for n in ("low_done", "sig_done", "rw_dve", "lc_done", "rw_exp_done"))
        kk0_done, sq_done, norm_mm, norm_done, rk_done, rk_mm, outs = (
            sem(n) for n in ("kk0_done", "sq_done", "norm_mm", "norm_done", "rk_done", "rk_mm", "rw_outs"))
        round_done, raw_used = sem("rw_round_done"), sem("raw_used")
        block = local.open_block()
        STEPS = 20

        def opnd_part(n, j):
            return opnd[:, :, bass.ds(j * C + n * 256, C)].rearrange("c p s -> p c s")

        @block.sync
        def _(sp):
            sp.sem_inc(round_done, 1)

            def load(i):
                for n, row in enumerate((U_R, U_RK, U_RV)):
                    sp.dma_start(raw[n][:, 1:], u[bass.ds(i * P + row * P, P), :]).then_inc(landed[n], 16)
                sp.dma_start(low_up[0:64, :], A["rwkv_w_up"][0][:, bass.ds(i * P, P)]).then_inc(up_landed, 16)
                sp.dma_start(low_up[64:128, :], A["rwkv_a_up"][0][:, bass.ds(i * P, P)]).then_inc(up_landed, 16)

            def store(i):
                sp.wait_ge(outs, i + 2)
                for n, name in ((O_A, "ao"), (O_R, "ro"), (O_B, "bo"), (O_K, "ko"), (O_V, "v")):
                    sp.dma_start(opnd_part(n, i), t[name][:, :].rearrange("p (c s) -> p c s", s=C)).then_inc(stored, 16)
                sp.dma_start(bonus[bass.ds(i * P, P), :], t["bonus"][:, :]).then_inc(stored, 16)
                sp.wait_ge(stored, i * 96 + 96)
                sp.sem_inc(round_done, 1)
            load(0)
            with sp.Fori(0, 3) as i:
                sp.wait_ge(raw_used, i + 1)
                load(i + 1)
                store(i)
            store(3)

        @block.gpsimd
        def _(pool):
            spare.pool_program(pool)

        @block.tensor
        def _(pe):
            spare.pe_begin(pe)
            with pe.Fori(0, 4) as i:
                pe.wait_ge(up_landed, i * 32 + 32)
                pe.wait_ge(outs, i + 1)
                for h in range(2):
                    cols = slice(h * HALF, (h + 1) * HALF)
                    pe.matmul(z_ps[:, h, :], low_up[0:64, :], wa[0:64, cols], start=True, stop=True)
                    last = pe.matmul(a_ps[:, h, :], low_up[64:128, :], wa[64:128, cols], start=True, stop=True)
                last.then_inc(low_done, 1)
                spare.pe_tile(pe, i, 0)
                pe.wait_ge(sq_done, i + 1)
                for h in range(2):
                    last = pe.matmul(n_ps[:, h, :], tab("head_ones"), t["sq"][:, h * HALF:(h + 1) * HALF], start=True, stop=True)
                last.then_inc(norm_mm, 1)
                spare.pe_tile(pe, i, 1)
                pe.wait_ge(rk_done, i + 1)
                for h in range(2):
                    last = pe.matmul(b_ps[:, h, :], tab("head_ones"), t["rk"][:, h * HALF:(h + 1) * HALF], start=True, stop=True)
                last.then_inc(rk_mm, 1)
                spare.pe_tile(pe, i, 2)
                spare.pe_tile(pe, i, 3)

        @block.scalar
        def _(act):
            act.sem_inc(outs, 1)
            spare.act_begin(act)
            def one_round(i, last):
                act.wait_ge(low_done, i + 1)
                act.activation(t["sw"][:, :], flat(z_ps), ACT.Sigmoid, bias=par("w0", i)).then_inc(sig_done, 1)
                act.activation(t["a"][:, :], flat(a_ps), ACT.Sigmoid, bias=par("a0", i)).then_inc(sig_done, 1)
                act.wait_ge(kk0_done, i + 1)
                act.activation(t["sq"][:, :], t["kk"][:, :], ACT.Square).then_inc(sq_done, 1)
                spare.act_tile(act, i, 0, last)
                act.wait_ge(norm_mm, i + 1)
                act.activation(t["nrm"][:, :], flat(n_ps), ACT.Sqrt, bias=par("eps_k")).then_inc(norm_done, 1)
                act.wait_ge(lc_done, i + 1)
                act.activation(t["ep"][:, :], t["lp"][:, :], ACT.Exp).then_inc(exp_done, 1)
                act.activation(t["en"][:, :], t["lc"][:, :], ACT.Exp, scale=-1.0).then_inc(exp_done, 1)
                act.activation(t["ec"][:, :], t["lc"][:, :], ACT.Exp).then_inc(exp_done, 1)
                for q in (1, 2, 3):
                    spare.act_tile(act, i, q, last)
            with act.Fori(0, 4 - 1) as i:
                one_round(i, False)
            one_round(4 - 1, True)
            spare.act_end(act)

        @block.vector
        def _(dve):
            for n in range(3):
                dve.memset(raw[n][:, 0:1], 0.0).then_inc(dve_step, 1)
            dve.wait_ge(dve_step, 3)
            with dve.Fori(0, 4) as i:
                step = Chain(dve, dve_step, i * STEPS + 3)
                def shift(n, name):
                    dve.wait_ge(landed[n], i * 16 + 16)
                    step(dve.tensor_tensor(t["d"][:, :], raw[n][:, 0:T], raw[n][:, 1:], ALU.subtract))
                    step(dve.scalar_tensor_tensor(t[name][:, :], t["d"][:, :], par("mu", i + 4 * n), raw[n][:, 1:], ALU.mult, ALU.add))
                shift(0, "r")
                shift(1, "k")
                dve.tensor_scalar(t["kk"][:, :], t["k"][:, :], par("k_k", i), None, ALU.mult).then_inc(kk0_done, 1)
                dve.wait_ge(sig_done, i * 2 + 2)
                step(dve.tensor_scalar(t["sw"][:, :], t["sw"][:, :], E5, None, ALU.mult))
                step(dve.tensor_tensor_scan(t["lc"][:, :], tab("in_chunk"), t["sw"][:, :], 0.0, ALU.mult, ALU.add))
                dve.tensor_tensor(t["lp"][:, :], t["lc"][:, :], t["sw"][:, :], ALU.subtract).then_inc(lc_done, 1)
                step(dve.tensor_scalar(t["d"][:, :], t["a"][:, :], par("k_a", i), par("one_minus_k_a", i), ALU.mult, ALU.add))
                step(dve.tensor_tensor(t["k"][:, :], t["k"][:, :], t["d"][:, :], ALU.mult))
                step(dve.tensor_scalar(t["d"][:, :], t["r"][:, :], par("r_k", i), None, ALU.mult))
                dve.wait_ge(round_done, i + 1)
                dve.tensor_tensor(t["rk"][:, :], t["d"][:, :], t["k"][:, :], ALU.mult).then_inc(rk_done, 1)
                dve.wait_ge(rk_done, i + 1)
                shift(2, "v")
                dve.sem_inc(raw_used, 1)
                dve.wait_ge(norm_done, i + 1)
                step(dve.reciprocal(t["nrm"][:, :], t["nrm"][:, :]))
                step(dve.tensor_tensor(t["kk"][:, :], t["kk"][:, :], t["nrm"][:, :], ALU.mult))
                dve.wait_ge(exp_done, i * 3 + 3)
                step(dve.scalar_tensor_tensor(t["ao"][:, :], t["kk"][:, :], -1.0, t["ep"][:, :], ALU.mult, ALU.mult))
                step(dve.tensor_tensor(t["bo"][:, :], t["kk"][:, :], t["a"][:, :], ALU.mult))
                step(dve.tensor_tensor(t["bo"][:, :], t["bo"][:, :], t["en"][:, :], ALU.mult))
                step(dve.tensor_tensor(t["ko"][:, :], t["k"][:, :], t["en"][:, :], ALU.mult))
                step(dve.tensor_tensor(t["ro"][:, :], t["r"][:, :], t["ec"][:, :], ALU.mult))
                step(dve.tensor_copy(plast[:, bass.ds(i * NCH, NCH)], t["ec"][:, :].rearrange("p (c s) -> p c s", s=C)[:, :, C - 1]))
                dve.wait_ge(rk_mm, i + 1)
                step(dve.tensor_tensor(t["bonus"][:, :], flat(b_ps), t["v"][:, :], ALU.mult))
                assert step.n == STEPS
                dve.sem_inc(outs, 1)


def prepare_gdn(nc, A, u, rows, opnd, par, tab, xhi, xlo, scratch):
    with Phase(nc) as local:
        sb = lambda name, shape: local.enter_context(nc.sbuf_tensor(name, shape, F32))
        sem = lambda name: local.sem(name)
        raw = [sb("graw_" + n, [P, 3 + T]) for n in "qkv"]
        conv = [sb("conv_" + n, [P, T]) for n in "qkv"]
        out = [{n: sb(f"g_{n}{b}", [P, T]) for n in "qkv"} for b in range(2)]
        for k, n in enumerate(("qd", "kb")):
            out[0][n], out[1][n] = scratch[:, k, :], sb(f"g_{n}1", [P, T])
        sq, nrm = [scratch[:, 2 + n, :] for n in range(2)], [sb(f"g_nrm{n}", [P, T]) for n in range(2)]
        eg, beta = sb("g_eg", [P, T]), sb("g_beta", [P, T])
        ps = [local.enter_context(nc.psum_tensor(f"g_ps{n}", [P, 2, HALF], F32)) for n in range(2)]
        landed, rows_landed, stored = [sem(f"g_landed{n}") for n in range(3)], sem("g_rows_landed"), sem("g_stored")
        conv_done, silu_done, sq_done, norm_mm, norm_done, dve_step, outs, round_done = (
            sem(n) for n in ("conv_done", "silu_done", "g_sq_done", "g_norm_mm", "g_norm_done", "g_dve", "g_outs", "g_round_done"))
        spare = SpareColumns(nc, local, A["w_in"][0], u, xhi, xlo, U_GATE, 8, 2)
        block = local.open_block()
        taps_done = sem("g_taps")

        @block.sync
        def _(sp):
            def load(i):
                for n, row in enumerate((U_Q, U_K, U_V)):
                    sp.dma_start(raw[n][:, 3:], u[(i + row) * P:(i + row + 1) * P, :]).then_inc(landed[n], 16)

            def load_scales(i):
                for q, tile in ((R_EG, eg), (R_BETA, beta)):
                    sp.dma_start(tile[:, :], rows[q][i:i + 1, :].to_broadcast([P, T])).then_inc(rows_landed, 16)

            load(0)
            load_scales(0)
            sp.wait_ge(conv_done, 3)
            load(1)
            for i in range(GH):
                if i + 2 < GH:
                    sp.wait_ge(conv_done, 3 * (i + 2))
                    load(i + 2)
                sp.wait_ge(outs, i + 1)
                if i + 1 < GH:
                    load_scales(i + 1)
                for n, name in ((O_GQ, "q"), (O_GQD, "qd"), (O_GK, "k"), (O_GKB, "kb"), (O_GV, "v")):
                    sp.dma_start(opnd[:, :, n * 256 + i * C:n * 256 + (i + 1) * C].rearrange("c p s -> p c s"),
                                 out[i % 2][name][:, :].rearrange("p (c s) -> p c s", s=C)).then_inc(stored, 16)
                sp.wait_ge(stored, (i + 1) * 80)
                sp.sem_inc(round_done, 1)

        @block.gpsimd
        def _(pool):
            spare.pool_program(pool)

        @block.tensor
        def _(pe):
            spare.pe_begin(pe)
            for i in range(GH):
                spare.pe_tile(pe, i, 0)
                for n in range(2):
                    pe.wait_ge(sq_done, i * 2 + n + 1)
                    for h in range(2):
                        last = pe.matmul(ps[n][:, h, :], tab("ones"), sq[n][:, h * HALF:(h + 1) * HALF], start=True, stop=True)
                    last.then_inc(norm_mm, 1)
                for q in range(1, spare.per):
                    spare.pe_tile(pe, i, q)

        @block.scalar
        def _(act):
            spare.act_begin(act)
            for i in range(GH):
                o = out[i % 2]
                if i >= 2:
                    act.wait_ge(round_done, i - 1)
                for n, name in enumerate("qkv"):
                    act.wait_ge(conv_done, i * 3 + n + 1)
                    act.activation(o[name][:, :], conv[n][:, :], ACT.Silu).then_inc(silu_done, 1)
                act.wait_ge(silu_done, i * 3 + 3)
                for n, name in enumerate("qk"):
                    act.activation(sq[n][:, :], o[name][:, :], ACT.Square).then_inc(sq_done, 1)
                spare.act_tile(act, i, 0, i == GH - 1)
                if i:
                    act.wait_ge(outs, i)
                for n, name in enumerate("qk"):
                    act.wait_ge(norm_mm, i * 2 + n + 1)
                    act.activation(nrm[n][:, :], ps[n][:, :, :].rearrange("p h t -> p (h t)"), ACT.Sqrt,
                                   bias=par("eps_" + name), scale=float(GD) if n == 0 else 1.0).then_inc(norm_done, 1)
                for q in range(1, spare.per):
                    spare.act_tile(act, i, q, i == GH - 1)
            spare.act_end(act)

        @block.vector
        def _(dve):
            for n in range(3):
                dve.memset(raw[n][:, 0:3], 0.0).then_inc(dve_step, 1)
            dve.wait_ge(dve_step, 3)

            def convolve(i):
                for n in range(3):
                    dve.wait_ge(landed[n], i * 16 + 16)
                if i:
                    dve.wait_ge(silu_done, i * 3)
                for k in (3, 2, 1, 0):
                    for n in range(3):
                        tap = par("conv", i + (12 * k + 4 * n))
                        if k == 3:
                            dve.tensor_scalar(conv[n][:, :], raw[n][:, 3:], tap, None, ALU.mult).then_inc(taps_done, 1)
                            continue
                        dve.wait_ge(taps_done, i * 9 + (2 - k) * 3 + n + 1)
                        dve.scalar_tensor_tensor(conv[n][:, :], raw[n][:, k:k + T], tap, conv[n][:, :],
                                                 ALU.mult, ALU.add).then_inc(taps_done if k else conv_done, 1)

            def scale(i):
                o = out[i % 2]
                dve.wait_ge(rows_landed, i * 32 + 32)
                if i >= 2:
                    dve.wait_ge(round_done, i - 1)
                for n, (name, other, by) in enumerate((("q", "qd", eg), ("k", "kb", beta))):
                    dve.wait_ge(norm_done, i * 2 + n + 1)
                    step(dve.reciprocal(nrm[n][:, :], nrm[n][:, :]))
                    step(dve.tensor_tensor(o[name][:, :], o[name][:, :], nrm[n][:, :], ALU.mult))
                    step(dve.tensor_tensor(o[other][:, :], o[name][:, :], by[:, :], ALU.mult))
                dve.sem_inc(outs, 1)
            step = Chain(dve, dve_step, 3)
            convolve(0)
            for i in range(GH):
                if i + 1 < GH:
                    convolve(i + 1)
                scale(i)


def prepare_decays(nc, rows, egl, gates_tile, cols, egl_bc, tab):
    with Phase(nc) as local:
        sb = lambda name, shape: local.enter_context(nc.sbuf_tensor(name, shape, F32))
        sem = lambda name: local.sem(name)
        along, col = sb("gc_along", [P, NCH, 2, C]), sb("gc_col", [P, NCH, 2])
        landed, step_done, exp_done = sem("gc_landed"), sem("gc_step"), sem("gc_exp")
        block = local.open_block()

        @block.sync
        def _(sp):
            n = 0
            with nc.allow_non_contiguous_dma(reason="one value per head and token, once"):
                for e in range(2):
                    half = slice(64 * e, 64 * e + 64)
                    for p in range(2):
                        row = rows[R_GC, 2 * p + e].rearrange("(c s) -> c s", s=C)
                        sp.dma_start(along[half, :, p, :], row.unsqueeze(0).to_broadcast([64, NCH, C])).then_inc(landed, 16)
                        sp.dma_start(col[half, :, p], row.rearrange("c s -> s c")).then_inc(landed, 16)
                        n += 32
                        for k, q in enumerate((R_TAIL, R_BETA, R_NBEG)):
                            sp.dma_start(cols[half, :, k, p], rows[q, 2 * p + e].rearrange("(c s) -> s c", s=C)).then_inc(landed, 16)
                            n += 16
                sp.dma_start(egl_bc[:, :, :], egl.unsqueeze(0).to_broadcast([P, GH, NCH])).then_inc(landed, 16)
                n += 16
            sp.wait_ge(landed, n)
            sp.sem_inc(step_done, 1)

        @block.vector
        def _(dve):
            dve.wait_ge(step_done, 1)
            step = Chain(dve, step_done, 1)
            step(dve.tensor_tensor(along[:, :, :, :], along[:, :, :, :], col[:, :, :].unsqueeze(3).to_broadcast([P, NCH, 2, C]), ALU.subtract))
            step(dve.tensor_scalar(along[:, :, :, :], along[:, :, :, :], 0.0, None, ALU.min))
            dve.wait_ge(exp_done, 1)
            for k, mask in enumerate(("minus_strict", "causal_again")):
                for p in range(2):
                    step(dve.tensor_tensor(gates_tile[:, :, p, k, :], along[:, :, p, :],
                                           tab(mask).unsqueeze(1).to_broadcast([P, NCH, C]), ALU.mult))

        @block.scalar
        def _(act):
            act.wait_ge(step_done, 3)
            act.activation(along[:, :, :, :], along[:, :, :, :], ACT.Exp).then_inc(exp_done, 1)


def rwkv_rows(e):
    return slice(64 * e, 64 * e + 64)


def diagonal_blocks(nc, opnd, gates_tile, nt, tab):
    DEEP = 4
    with Phase(nc) as local:
        sem = lambda name: local.sem(name)
        op = [local.enter_context(nc.sbuf_tensor(f"dop{b}", [P, 4, 4, C], F32)) for b in range(DEEP)]
        n = [local.enter_context(nc.sbuf_tensor(f"dn{b}", [P, NPAIR, C], F32)) for b in range(DEEP)]
        ps = [local.enter_context(nc.psum_tensor(f"dps{b}", [P, 8, C], F32)) for b in range(DEEP)]
        landed, stored = [sem(f"dop_landed{b}") for b in range(DEEP)], [sem(f"nt_stored{b}") for b in range(DEEP)]
        mm_done, masked, turns = sem("d_mm_done"), sem("d_masked"), sem("d_turns")
        block = local.open_block()

        def chunks(eng, step):
            with eng.Fori(0, NCH // DEEP) as i:
                for b in range(DEEP):
                    step(i * DEEP + b, i, b)

        @block.sync
        def _(sp):
            def step(c, i, b):
                sp.wait_ge(mm_done, c + 1)
                for at, first in ((0, O_B), (2, O_GK)):
                    sp.dma_start(op[b][:, at:at + 2, :, :], opnd[bass.ds(c, 1), :, first * 256:(first + 2) * 256].rearrange("o p (n j s) -> p (o n) j s", n=2, j=4)).then_inc(landed[b], 16)
            chunks(sp, step)

        @block.tensor
        def _(pe):
            pe.sem_inc(mm_done, DEEP)

            def step(c, i, b):
                pe.wait_ge(landed[b], i * 32 + 32)
                pe.wait_ge(masked, c * 2 + 2)
                turn(pe, turns)
                for j in range(4):
                    for e in range(2):
                        h = rwkv_rows(e)
                        pe.matmul(ps[b][h, j, :], op[b][h, 0, j, :], op[b][h, 1, j, :], start=True, stop=True)
                for p in range(2):
                    for e in range(2):
                        last = pe.matmul(ps[b][rwkv_rows(e), 4 + p, :], op[b][:, 2, 2 * p + e, :], op[b][:, 3, 2 * p + e, :],
                                         start=True, stop=True)
                last.then_inc(mm_done, 1)
            chunks(pe, step)

        @block.vector
        def _(dve):
            dve.sem_inc(masked, 2 * DEEP)
            for b in range(DEEP):
                dve.sem_inc(stored[b], 64)

            def step(c, i, b):
                dve.wait_ge(mm_done, c + (1 + DEEP))
                dve.wait_ge(stored[b], i * 64 + 64)
                dve.tensor_tensor(n[b][:, 0:4, :], ps[b][:, 0:4, :], tab("strict").unsqueeze(1).to_broadcast([P, 4, C]), ALU.mult).then_inc(masked, 1)
                dve.tensor_tensor(n[b][:, 4:6, :], ps[b][:, 4:6, :], gates_tile[:, bass.ds(c, 1), :, 0, :].rearrange("p o g s -> p (o g) s"), ALU.mult).then_inc(masked, 1)
            chunks(dve, step)

        @block.scalar
        def _(act):
            def step(c, i, b):
                act.wait_ge(masked, c * 2 + (2 + 2 * DEEP))
                for q in range(4):
                    t0 = NB * (q % 2)
                    act.dma_start(nt[bass.ds(c, 1), 32 * q:32 * q + 32, :, :].rearrange("o s p t -> s (o p) t"),
                                  n[b][32 * q:32 * q + 32, :, t0:t0 + NB]).then_inc(stored[b], 16)
            chunks(act, step)
            for b in range(DEEP):
                act.wait_ge(stored[b], 64 + 64 * (NCH // DEEP))


def invert_blocks(nc, A, u, xhi, xlo, nt, xinv):
    R = NPAIR // 2
    with Phase(nc) as local:
        sb = lambda name, shape: local.enter_context(nc.sbuf_tensor(name, shape, F32))
        sem = lambda name: local.sem(name)
        n, x, xt = sb("inv_n", [P, R, NB, NB]), sb("inv_x", [P, R, NB, NB]), sb("inv_xt", [P, R, NB, NB])
        prod = sb("inv_prod", [P, R, NB, NB])
        landed, step_done, stored = sem("inv_landed"), [sem(f"inv_step{k}") for k in range(2)], sem("inv_stored")
        PARTS = (slice(0, 2), slice(2, R))
        cleared = sem("inv_cleared")
        tiles = [*range(U_Z, A_TILES), *range(U_SQ, U_GATE)]
        spare = SpareColumns(nc, local, A["w_in"][0], u, xhi, xlo, 0, len(tiles), 2, tiles)
        block = local.open_block()
        spare.run_alone(block)
        STEPS = 2 + 2 * (NB - 1)
        blocks = nt.rearrange("c (b s) p t -> (c b) s p t", s=NB)
        out = xinv.rearrange("c (b s) x p t -> (c b) s x p t", s=NB)

        @block.sync
        def _(sp):
            for pp in range(2):
                for r in range(R):
                    sp.dma_start(n[64 * pp:64 * pp + 64, r, :, :], blocks[:, :, 2 * r + pp, :]).then_inc(landed, 16)
            for k in range(2):
                sp.wait_ge(step_done[k], STEPS)
            for which, tile in enumerate((x, xt)):
                for pp in range(2):
                    for r in range(R):
                        sp.dma_start(out[:, :, which, 2 * r + pp, :], tile[64 * pp:64 * pp + 64, r, :, :]).then_inc(stored, 16)
            sp.wait_ge(stored, 16 * 4 * R)

        @block.vector
        def _(dve):
            dve.memset(x[:, :, :, :], 0.0).then_inc(cleared, 1)
            dve.wait_ge(cleared, 1)

            def steps(k, part):
                g = part.stop - part.start
                flat = x[:, part, :, :].rearrange("p r i j -> p r (i j)")
                yield dve.memset(flat[:, :, 0:NB * NB:NB + 1], 1.0)
                for i in range(1, NB):
                    yield dve.tensor_tensor(prod[:, part, 0:i, 0:i], n[:, part, 0:i, i].unsqueeze(2).to_broadcast([P, g, i, i]),
                                            x[:, part, 0:i, 0:i].rearrange("p r j c -> p r c j"), ALU.mult)
                    yield dve.tensor_reduce(x[:, part, i, 0:i], prod[:, part, 0:i, 0:i], AX.X, ALU.add)
                yield dve.tensor_copy(xt[:, part, :, :], x[:, part, :, :].rearrange("p r i j -> p r j i"))
            dve.wait_ge(landed, 16 * 2 * R)
            chains = [steps(k, part) for k, part in enumerate(PARTS)]
            for done in range(STEPS):
                for k in range(2):
                    if done:
                        dve.wait_ge(step_done[k], done)
                    next(chains[k]).then_inc(step_done[k], 1)


def scan_chunks(nc, opnd, xinv, gates_tile, cols, egl_bc, plast, mixed, tab):
    with Phase(nc) as local:
        sem = lambda name: local.sem(name)
        two = lambda name, shape: [local.enter_context(nc.sbuf_tensor(f"{name}{b}", [P] + shape, F32)) for b in range(2)]
        bank = lambda name, shape: local.enter_context(nc.psum_tensor(name, [P] + shape, F32))
        op = two("op", [N_OP, 4, C])
        packed = two("inv_packed", [2, NPAIR, NB])
        inv = two("inv", [2, NPAIR, C])
        m1, m2 = two("m1", [NPAIR, 2, C]), two("m2", [4, 2, C])
        tok_bk, tok_v = two("tok_bk", [2, 4, C]), two("tok_v", [4, C])
        tok_g = two("tok_g", [2, 2, GD])
        join, y = two("join", [NPAIR, C]), two("y", [NPAIR, C])
        zt = two("zt", [NPAIR, C])
        r_rw, r_g, w = two("r_rw", [4, C]), two("r_g", [2, GD]), two("w", [512])
        s_rw, s_g, s_dec = two("s_rw", [4, C]), two("s_g", [GH, GD]), two("s_dec", [GH, GD])
        s_sum, r_tmp = two("s_sum", [4, C]), two("r_tmp", [2, GD])
        o = two("o", [8, C])
        ps_m1, ps_m2 = bank("ps_m1", [8, C]), bank("ps_m2", [8, C])
        ps_bk, ps_vg, ps_kv = bank("ps_bk", [2, 4, C]), bank("ps_vg", [8, C]), bank("ps_kv", [2, 2, GD])
        ps_r, ps_w, ps_o = bank("ps_r", [512]), bank("ps_w", [512]), bank("ps_o", [8, C])

        landed, inv_landed, stored = ([sem(f"{n}{b}") for b in range(2)] for n in ("op_landed", "inv_landed", "o_stored"))
        mm_m1, mm_m2, mm_bk, mm_vg, mm_kv, mm_y, mm_zt = (sem("mm_" + n) for n in ("m1", "m2", "bk", "vg", "kv", "y", "zt"))
        mm_r, mm_w, mm_s, mm_o = (sem("mm_" + n) for n in ("r", "w", "s", "o"))
        m1_done, m1g_done, m2_done, bk_done, v_done, kv_done, inv_done, join_done, y_done, zt_done = (
            sem(n) for n in ("m1_done", "m1g_done", "m2_done", "bk_done", "v_done", "kv_done", "inv_done", "join_done", "y_done", "zt_done"))
        r_rw_done, r_tmp_done, r_g_done, w_done, s_sum_done, s_rw_done, dec_done, s_g_done, o_done, cleared, turns = (
            sem(n) for n in ("r_rw_done", "r_tmp_done", "r_g_done", "w_done", "s_sum_done", "s_rw_done", "dec_done", "s_g_done", "o_done", "s_cleared", "turns"))
        block = local.open_block()
        bc = lambda name, n: tab(name).unsqueeze(1).to_broadcast([P, n, C])
        both = lambda name: tab(name, 2 * C).rearrange("p (k s) -> p k s", k=2)

        def at_least(eng, s, n, scale=1):
            if not (isinstance(n, int) and n <= 0):
                eng.wait_ge(s, n * scale)

        def run(eng, product, state):
            def beside(c, n, b, j, nj):
                s, p = state(c, j, b), product(n, nj, 1 - b)
                for part in TURNS:
                    next(s if part == "state" else p, None)
            first = product(0, 0, 0)
            for _ in range(4):
                next(first, None)
            with eng.Fori(0, NCH // 2 - 1) as i:
                beside(i * 2, i * 2 + 1, 0, i, i)
                beside(i * 2 + 1, i * 2 + 2, 1, i, i + 1)
            beside(NCH - 2, NCH - 1, 0, NCH // 2 - 1, NCH // 2 - 1)
            last = state(NCH - 1, NCH // 2 - 1, 1)
            for _ in range(4):
                next(last, None)

        TURNS = ("state", "product", "state", "product", "state", "product", "state", "product")

        @block.sync
        def _(sp):
            sp.sem_inc(mm_o, 2)
            def load(c, i, b):
                sp.wait_ge(mm_o, c + 1)
                sp.dma_start(op[b][:, :, :, :], opnd[bass.ds(c, 1), :, :].rearrange("o p (n j s) -> p (o n) j s", n=N_OP, j=4)).then_inc(landed[b], 16)
                sp.dma_start(packed[b][:, :, :, :], xinv[bass.ds(c, 1)].rearrange("o r x p t -> r (o x) p t")).then_inc(inv_landed[b], 16)
            with sp.Fori(0, NCH // 2) as i:
                for b in range(2):
                    load(i * 2 + b, i, b)

        def flip(pe, e, out, x, identity):
            if e == 0:
                return pe.transpose(out, x, identity)
            return pe.matmul(out, x, identity, start=True, stop=True)

        @block.tensor
        def _(pe):
            def product(c, i, b):
                pe.wait_ge(landed[b], i * 16 + 16)
                at_least(pe, y_done, c)
                turn(pe, turns)
                for j in range(4):
                    for e in range(2):
                        h = rwkv_rows(e)
                        last = pe.matmul(ps_m1[h, 2 * j:2 * j + 2, :], op[b][h, O_B, j, :], op[b][h, O_A:O_R + 1, j, :], start=True, stop=True)
                last.then_inc(mm_m1, 1)
                at_least(pe, zt_done, c)
                turn(pe, turns)
                for j in range(4):
                    for e in range(2):
                        h = rwkv_rows(e)
                        last = pe.matmul(ps_m2[h, 2 * j:2 * j + 2, :], op[b][h, O_K, j, :], op[b][h, O_A:O_R + 1, j, :], start=True, stop=True)
                last.then_inc(mm_m2, 1)
                yield
                at_least(pe, bk_done, c)
                turn(pe, turns)
                for n, src in enumerate((O_B, O_K)):
                    for j in range(4):
                        for e in range(2):
                            h = rwkv_rows(e)
                            last = flip(pe, e, ps_bk[h, n, j, :], op[b][h, src, j, :], tab("ident2")[h, :])
                last.then_inc(mm_bk, 1)
                at_least(pe, v_done, c)
                at_least(pe, m1g_done, c)
                turn(pe, turns)
                for j in range(4):
                    for e in range(2):
                        h = rwkv_rows(e)
                        flip(pe, e, ps_vg[h, j, :], op[b][h, O_V, j, :], tab("ident2")[h, :])
                for p in range(2):
                    for e in range(2):
                        last = pe.matmul(ps_vg[rwkv_rows(e), 4 + 2 * p:6 + 2 * p, :], op[b][:, O_GK, 2 * p + e, :],
                                         op[b][:, O_GKB:O_GQ + 1, 2 * p + e, :], start=True, stop=True)
                last.then_inc(mm_vg, 1)
                yield
                at_least(pe, kv_done, c)
                turn(pe, turns)
                for n, src in enumerate((O_GK, O_GV)):
                    for p in range(2):
                        for e in range(2):
                            last = flip(pe, e, ps_kv[rwkv_rows(e), n, p, :], op[b][:, src, 2 * p + e, :], tab("ident"))
                last.then_inc(mm_kv, 1)
                pe.wait_ge(join_done, c + 1)
                pe.wait_ge(inv_done, c * 4 + 4)
                pe.wait_ge(m1_done, c + 1)
                turn(pe, turns)
                for u in range(NPAIR):
                    for e in range(2):
                        h = rwkv_rows(e)
                        last = pe.matmul(ps_m1[h, u, :], join[b][h, u, :], inv[b][h, 0, u, :], start=True, stop=True)
                last.then_inc(mm_y, 1)
                yield
                pe.wait_ge(y_done, c + 1)
                pe.wait_ge(m2_done, c + 1)
                turn(pe, turns)
                for u in range(NPAIR):
                    for e in range(2):
                        h = rwkv_rows(e)
                        last = pe.matmul(ps_m2[h, u, :], y[b][h, u, :], inv[b][h, 1, u, :], start=True, stop=True)
                last.then_inc(mm_zt, 1)
                yield

            def state(c, i, b):
                pe.wait_ge(bk_done, c + 1)
                pe.wait_ge(v_done, c + 1)
                pe.wait_ge(s_rw_done, c + 1)
                pe.wait_ge(s_g_done, c * 2 + 2)
                for p in range(2):
                    for e in range(2):
                        at = 256 + p * GD
                        pe.matmul(ps_r[rwkv_rows(e), at:at + GD], op[b][:, O_GK, 2 * p + e, :], s_g[b][:, 2 * p + e, :], start=True, stop=True)
                for j in range(4):
                    for e in range(2):
                        h = rwkv_rows(e)
                        out = ps_r[h, j * C:(j + 1) * C]
                        pe.matmul(out, op[b][h, O_A, j, :], s_rw[b][h, j, :], start=True, stop=False)
                        last = pe.matmul(out, m2[b][h, j, 0, :], tok_v[b][h, j, :], start=False, stop=True)
                last.then_inc(mm_r, 1)
                yield
                at_least(pe, o_done, c, 3)
                pe.wait_ge(zt_done, c + 1)
                pe.wait_ge(r_rw_done, c + 1)
                pe.wait_ge(r_g_done, c + 1)
                turn(pe, turns)
                for j in range(4):
                    for e in range(2):
                        h = rwkv_rows(e)
                        pe.matmul(ps_w[h, j * C:(j + 1) * C], zt[b][h, j, :], r_rw[b][h, j, :], start=True, stop=True)
                for p in range(2):
                    for e in range(2):
                        h, at = rwkv_rows(e), 256 + p * GD
                        last = pe.matmul(ps_w[h, at:at + GD], zt[b][h, 4 + p, :], r_g[b][h, p, :], start=True, stop=True)
                last.then_inc(mm_w, 1)
                yield
                pe.wait_ge(w_done, c + 1)
                pe.wait_ge(kv_done, c + 1)
                for p in range(2):
                    for e in range(2):
                        h, out = rwkv_rows(e), (ps_w[:, p * GD:(p + 1) * GD], ps_r[:, 256 + p * GD:256 + (p + 1) * GD])[e]
                        pe.matmul(out, tok_g[b][h, 0, p, :], w[b][h, 256 + p * GD:256 + (p + 1) * GD], start=True, stop=True)
                for j in range(4):
                    for e in range(2):
                        h = rwkv_rows(e)
                        out = ps_r[h, j * C:(j + 1) * C]
                        pe.matmul(out, tok_bk[b][h, 0, j, :], w[b][h, j * C:(j + 1) * C], start=True, stop=False)
                        last = pe.matmul(out, tok_bk[b][h, 1, j, :], tok_v[b][h, j, :], start=False, stop=True)
                last.then_inc(mm_s, 1)
                yield
                at_least(pe, o_done, c, 3)
                pe.wait_ge(m1g_done, c + 1)
                pe.wait_ge(s_g_done, c * 2 + 4)
                turn(pe, turns)
                for j in range(4):
                    for e in range(2):
                        h = rwkv_rows(e)
                        out = ps_o[h, j, :]
                        pe.matmul(out, s_rw[b][h, j, :], op[b][h, O_R, j, :], start=True, stop=False)
                        pe.matmul(out, w[b][h, j * C:(j + 1) * C], m1[b][h, j, 1, :], start=False, stop=False)
                        pe.matmul(out, tok_v[b][h, j, :], m2[b][h, j, 1, :], start=False, stop=True)
                for p in range(2):
                    for e in range(2):
                        h = rwkv_rows(e)
                        out = (ps_o[:, 4 + p, :], ps_w[:, 256 + p * C:256 + (p + 1) * C])[e]
                        pe.matmul(out, s_g[b][:, 2 * p + e, :], op[b][:, O_GQD, 2 * p + e, :], start=True, stop=False)
                        last = pe.matmul(out, w[b][h, 256 + p * GD:256 + (p + 1) * GD], m1[b][h, 4 + p, 1, :], start=False, stop=True)
                last.then_inc(mm_o, 1)
                yield

            run(pe, product, state)

        @block.vector
        def _(dve):
            dve.memset(s_rw[0][:, :, :], 0.0).then_inc(s_rw_done, 1)
            dve.memset(s_g[0][:, :, :], 0.0).then_inc(s_g_done, 2)

            def product(c, i, b):
                dve.wait_ge(mm_m1, c + 1)
                dve.tensor_tensor(m1[b][:, 0:4, :, :], ps_m1[:, :, :].rearrange("p (j k) s -> p j k s", k=2),
                                  both("strict").unsqueeze(1).to_broadcast([P, 4, 2, C]), ALU.mult).then_inc(m1_done, 1)
                dve.wait_ge(mm_m2, c + 1)
                dve.tensor_tensor(m2[b][:, :, :, :], ps_m2[:, :, :].rearrange("p (j k) s -> p j k s", k=2),
                                  both("strict").unsqueeze(1).to_broadcast([P, 4, 2, C]), ALU.mult).then_inc(m2_done, 1)
                yield
                dve.wait_ge(mm_vg, c + 1)
                dve.tensor_tensor(m1[b][:, 4:6, :, :].rearrange("p g k s -> p (g k s)"), ps_vg[:, 4:8, :].rearrange("p g s -> p (g s)"),
                                  gates_tile[:, bass.ds(c, 1), :, :, :].rearrange("p o g k s -> p (o g k s)"), ALU.mult).then_inc(m1g_done, 1)
                yield
                dve.wait_ge(mm_kv, c + 1)
                dve.tensor_tensor(tok_g[b][:, :, :, :].rearrange("p n g d -> p (n g) d"), ps_kv[:, :, :, :].rearrange("p n g d -> p (n g) d"),
                                  cols[:, bass.ds(c, 1), 0:2, :].rearrange("p o n g -> p (o n g)").unsqueeze(2).to_broadcast([P, 4, GD]),
                                  ALU.mult).then_inc(kv_done, 1)
                yield
                dve.wait_ge(mm_zt, c + 1)
                dve.wait_ge(inv_done, c * 4 + 4)
                dve.tensor_tensor(zt[b][:, :, :], ps_m2[:, 0:NPAIR, :], inv[b][:, 1, :, :], ALU.add).then_inc(zt_done, 1)
                yield

            def state(c, i, b):
                dve.wait_ge(mm_r, c + 1)
                dve.tensor_tensor(r_tmp[b][:, :, :], ps_r[:, 256:512].rearrange("p (g d) -> p g d", g=2),
                                  cols[:, bass.ds(c, 1), 2, :].rearrange("p o g -> p (o g)").unsqueeze(2).to_broadcast([P, 2, GD]), ALU.mult).then_inc(r_tmp_done, 1)
                dve.wait_ge(r_tmp_done, c + 1)
                dve.wait_ge(kv_done, c + 1)
                dve.tensor_tensor(r_g[b][:, :, :], r_tmp[b][:, :, :], tok_g[b][:, 1, :, :], ALU.add).then_inc(r_g_done, 1)
                yield
                yield
                dve.wait_ge(mm_s, c + 1)
                dve.wait_ge(dec_done, c + 1)
                for e, src in enumerate((ps_w[:, 0:256], ps_r[:, 256:512])):
                    last = dve.tensor_tensor(s_g[1 - b][:, :, :].rearrange("p (g e) d -> p g e d", e=2)[:, :, e, :],
                                             s_dec[b][:, :, :].rearrange("p (g e) d -> p g e d", e=2)[:, :, e, :],
                                             src.rearrange("p (g d) -> p g d", g=2), ALU.add)
                    last.then_inc(s_g_done, 1)
                dve.tensor_tensor(s_sum[b][:, :, :], s_rw[b][:, :, :], ps_r[:, 0:256].rearrange("p (j d) -> p j d", j=4), ALU.add).then_inc(s_sum_done, 1)
                dve.wait_ge(s_sum_done, c + 1)
                dve.tensor_tensor(s_rw[1 - b][:, :, :], s_sum[b][:, :, :],
                                  plast[:, :].rearrange("p (j c) -> p j c", j=4)[:, :, bass.ds(c, 1)].to_broadcast([P, 4, C]), ALU.mult).then_inc(s_rw_done, 1)
                yield

            run(dve, product, state)

        @block.scalar
        def _(act):
            for b in range(2):
                act.sem_inc(stored[b], 16)

            def product(c, i, b):
                act.wait_ge(mm_bk, c + 1)
                act.activation(tok_bk[b][:, :, :, :], ps_bk[:, :, :, :], ACT.Copy).then_inc(bk_done, 1)
                act.wait_ge(m1g_done, c + 1)
                act.activation(tok_v[b][:, :, :], ps_vg[:, 0:4, :], ACT.Copy).then_inc(v_done, 1)
                yield
                act.wait_ge(mm_y, c + 1)
                act.activation(y[b][:, :, :], ps_m1[:, 0:NPAIR, :], ACT.Copy).then_inc(y_done, 1)
                yield

            def state(c, i, b):
                act.wait_ge(r_tmp_done, c + 1)
                act.activation(r_rw[b][:, :, :], ps_r[:, 0:256].rearrange("p (j d) -> p j d", j=4), ACT.Copy).then_inc(r_rw_done, 1)
                act.wait_ge(mm_w, c + 1)
                act.activation(w[b][:, :], ps_w[:, :], ACT.Copy).then_inc(w_done, 1)
                yield
                act.wait_ge(mm_o, c + 3)
                act.wait_ge(stored[b], i * 16 + 16)
                act.activation(o[b][:, 0:4, :], ps_o[:, 0:4, :], ACT.Copy).then_inc(o_done, 1)
                heads = o[b][:, 4:8, :].rearrange("p (g e) s -> p g e s", e=2)
                act.activation(heads[:, :, 0, :], ps_o[:, 4:6, :], ACT.Copy).then_inc(o_done, 1)
                act.activation(heads[:, :, 1, :], ps_w[:, 256:384].rearrange("p (g s) -> p g s", g=2), ACT.Copy).then_inc(o_done, 1)
                act.wait_ge(o_done, c * 3 + 3)
                act.dma_start(mixed[bass.ds(c, 1)].rearrange("o p n s -> p (o n) s"), o[b][:, :, :]).then_inc(stored[b], 16)
                yield
            run(act, product, state)
            for b in range(2):
                act.wait_ge(stored[b], 16 + 16 * (NCH // 2))

        @block.gpsimd
        def _(pool):
            for b in range(2):
                pool.memset(inv[b][:, :, :, :], 0.0).then_inc(cleared, 1)
            pool.wait_ge(cleared, 2)

            def product(c, i, b):
                pool.wait_ge(inv_landed[b], i * 16 + 16)
                at_least(pool, dec_done, c)
                turn(pool, turns)
                for q in range(4):
                    rows, t0 = slice(32 * q, 32 * q + 32), NB * (q % 2)
                    last = pool.tensor_copy(inv[b][rows, :, :, t0:t0 + NB], packed[b][rows, :, :, :])
                    last.then_inc(inv_done, 1)
                pool.wait_ge(inv_done, c * 4 + 4)
                pool.wait_ge(m1_done, c + 1)
                pool.wait_ge(m1g_done, c + 1)
                pool.tensor_tensor(join[b][:, :, :], m1[b][:, :, 0, :], bc("corner", NPAIR), ALU.mult).then_inc(join_done, 1)
                yield

            def state(c, i, b):
                pool.wait_ge(join_done, c + 1)
                pool.wait_ge(s_g_done, c * 2 + 2)
                pool.tensor_tensor(s_dec[b][:, :, :], s_g[b][:, :, :], egl_bc[:, :, bass.ds(c, 1)].to_broadcast([P, GH, GD]), ALU.mult).then_inc(dec_done, 1)
                yield
            run(pool, product, state)


def window_attention(nc, u, attended, par, tab):
    W = 2 * C
    with Phase(nc) as local:
        sem = lambda name: local.sem(name)
        two = lambda name, shape: [local.enter_context(nc.sbuf_tensor(f"{name}{b}", [P] + shape, F32)) for b in range(2)]
        bank = lambda name, shape: [local.enter_context(nc.psum_tensor(f"{name}{b}", [P] + shape, F32)) for b in range(2)]
        q, k, v = two("at_q", [4, C]), two("at_k", [SKV, W]), two("at_v", [W])
        s, pt, vt, o = two("at_s", [4, W]), two("at_pt", [4, W]), two("at_vt", [P]), two("at_o", [4, C])
        top, own, rest = two("at_top", [4]), two("at_own", [4]), two("at_rest", [4])
        ps_s, ps_t, ps_vo, ps_o = bank("ps_s", [4, W]), bank("ps_t", [4, W]), bank("ps_v", [P]), bank("ps_ao", [4, C])
        landed, stored = [sem(f"at_landed{b}") for b in range(2)], [sem(f"at_stored{b}") for b in range(2)]
        mm_s, mm_v, mm_t, mm_o = (sem("at_mm_" + n) for n in "svto")
        dve_step, shifted, exp_done, p_done, vt_done, pt_done, o_done, padded, turns = (
            sem("at_" + n) for n in ("dve", "shifted", "exp_done", "p_done", "vt_done", "pt_done", "o_done", "padded", "turns"))
        scored, topped, rested = ([sem(f"at_{n}{b}") for b in range(2)] for n in ("scored", "topped", "rested"))
        block = local.open_block()
        STAGES = 8

        def over_chunks(eng, score, gather):
            score(0, 0, True)
            with eng.Fori(0, NCH // 2 - 1) as i:
                score(i * 2 + 2, i + 1, False)
                gather(i * 2, i)
            gather(NCH - 2, NCH // 2 - 1)

        @block.sync
        def _(sp):
            def score(c0, i, first):
                for b in range(2):
                    load(c0 + b, b, first and b == 0)

            def load(c, b, first):
                if first:
                    sp.wait_ge(padded, 1)
                elif not (isinstance(c, int) and c == 1):
                    sp.wait_ge(mm_s, c - 1)
                    sp.wait_ge(mm_v, c - 1)
                n = C if first else W
                at = 0 if first else c * C - C
                to = slice(W - n, W)
                sp.dma_start(q[b][:, :, :], u[U_SQ * P:(U_SQ + 4) * P, bass.ds(c * C, C)].rearrange("(j p) t -> p j t", p=P)).then_inc(landed[b], 16)
                for g in range(SKV):
                    src = u[U_SK * P + g * SD:U_SK * P + (g + 1) * SD, bass.ds(at, n)]
                    for e in range(2):
                        sp.dma_start(k[b][rwkv_rows(e), g, to], src).then_inc(landed[b], 16)
                sp.dma_start(v[b][:, to], u[U_SV * P:(U_SV + 1) * P, bass.ds(at, n)]).then_inc(landed[b], 16)

            over_chunks(sp, score, lambda *a: None)

        @block.tensor
        def _(pe):
            def score(c0, i, first):
                for b in range(2):
                    score_one(c0 + b, i, b, first)

            def score_one(c, i, b, first):
                pe.wait_ge(landed[b], i * 96 + 96)
                if not first:
                    pe.wait_ge(p_done, c - 1)
                    pe.wait_ge(vt_done, c - 1)
                    turn(pe, turns)
                for j in range(4):
                    for e in range(2):
                        h = rwkv_rows(e)
                        last = pe.matmul(ps_s[b][h, j, :], q[b][h, j, :], k[b][h, j // 2, :], start=True, stop=True)
                last.then_inc(mm_s, 1)
                pe.transpose(ps_vo[b][:, :], v[b][:, :], tab("ident")).then_inc(mm_v, 1)

            def gather(c0, i):
                for b in range(2):
                    turn_weights(c0 + b, b)
                for b in range(2):
                    sum_values(c0 + b, b)

            def turn_weights(c, b):
                pe.wait_ge(p_done, c + 1)
                pe.wait_ge(pt_done, c + 1)
                for j in range(4):
                    last = pe.transpose(ps_t[b][:, j, :], s[b][:, j, :], tab("ident"))
                last.then_inc(mm_t, 1)

            def sum_values(c, b):
                pe.wait_ge(vt_done, c + 1)
                pe.wait_ge(pt_done, c + 3)
                pe.wait_ge(o_done, c + 1)
                for g in range(SKV):
                    for e in range(2):
                        last = pe.matmul(ps_o[b][rwkv_rows(e), 2 * g:2 * g + 2, :], vt[b][:, g * SD:(g + 1) * SD],
                                         pt[b][:, 2 * g:2 * g + 2, e * C:(e + 1) * C], start=True, stop=True)
                last.then_inc(mm_o, 1)

            pe.sem_inc(o_done, 2)
            pe.sem_inc(pt_done, 2)
            pe.sem_inc(mm_o, 2)
            over_chunks(pe, score, gather)

        @block.vector
        def _(dve):
            dve.memset(k[0][:, :, 0:C], 0.0).then_inc(dve_step, 1)
            dve.memset(v[0][:, 0:C], 0.0).then_inc(dve_step, 1)
            dve.wait_ge(dve_step, 2)
            dve.sem_inc(padded, 1)

            def score(c0, i, first):
                parts = [one(c0 + b, i, b, first) for b in range(2)]
                for _ in range(STAGES):
                    for part in parts:
                        next(part, None)

            def one(c, i, b, first):
                at = CONST_AT["alibi10" if first and b == 0 else "alibi00"][0]
                alibi = tab.tile[:, at:at + 4 * W]
                flat = lambda x: x[:, :, :].rearrange("p j k -> p (j k)")
                wide = lambda x: x[:, :].unsqueeze(2).to_broadcast([P, 4, W])
                dve.wait_ge(mm_s, c + 1)
                if not first:
                    dve.wait_ge(mm_t, c - 1)
                dve.scalar_tensor_tensor(flat(s[b]), flat(ps_s[b]), SD ** -0.5, alibi, ALU.mult, ALU.add).then_inc(scored[b], 1)
                yield
                dve.wait_ge(scored[b], i + 1)
                dve.tensor_reduce(top[b][:, :], s[b][:, :, :], AX.X, ALU.max).then_inc(topped[b], 1)
                yield
                dve.wait_ge(topped[b], i * 2 + 1)
                dve.tensor_tensor(top[b][:, :], top[b][:, :], par("sinks", 0, 4), ALU.max).then_inc(topped[b], 1)
                yield
                dve.wait_ge(topped[b], i * 2 + 2)
                dve.tensor_tensor(own[b][:, :], par("sinks", 0, 4), top[b][:, :], ALU.subtract).then_inc(shifted, 1)
                dve.tensor_tensor(s[b][:, :, :], s[b][:, :, :], wide(top[b]), ALU.subtract).then_inc(shifted, 1)
                yield
                dve.wait_ge(exp_done, c * 2 + 2)
                dve.tensor_reduce(rest[b][:, :], s[b][:, :, :], AX.X, ALU.add).then_inc(rested[b], 1)
                yield
                dve.wait_ge(rested[b], i * 3 + 1)
                dve.tensor_tensor(rest[b][:, :], rest[b][:, :], own[b][:, :], ALU.add).then_inc(rested[b], 1)
                yield
                dve.wait_ge(rested[b], i * 3 + 2)
                dve.reciprocal(rest[b][:, :], rest[b][:, :]).then_inc(rested[b], 1)
                yield
                dve.wait_ge(rested[b], i * 3 + 3)
                dve.tensor_tensor(s[b][:, :, :], s[b][:, :, :], wide(rest[b]), ALU.mult).then_inc(p_done, 1)
                yield

            over_chunks(dve, score, lambda *a: None)

        @block.scalar
        def _(act):
            for b in range(2):
                act.sem_inc(stored[b], 16)

            def both(step, c0, i):
                for b in range(2):
                    step(c0 + b, i, b)

            def turn_values(c, i, b):
                act.wait_ge(mm_v, c + 1)
                act.wait_ge(mm_o, c + 1)
                act.activation(vt[b][:, :], ps_vo[b][:, :], ACT.Copy).then_inc(vt_done, 1)

            def exponentials(c, i, b):
                act.wait_ge(shifted, c * 2 + 2)
                act.activation(own[b][:, :], own[b][:, :], ACT.Exp).then_inc(exp_done, 1)
                act.activation(s[b][:, :, :], s[b][:, :, :], ACT.Exp).then_inc(exp_done, 1)

            def copy_weights(c, i, b):
                act.wait_ge(mm_t, c + 1)
                act.activation(pt[b][:, :, :], ps_t[b][:, :, :], ACT.Copy).then_inc(pt_done, 1)

            def store(c, i, b):
                act.wait_ge(mm_o, c + 3)
                act.wait_ge(stored[b], i * 16 + 16)
                act.activation(o[b][:, :, :], ps_o[b][:, :, :], ACT.Copy).then_inc(o_done, 1)
                act.wait_ge(o_done, c + 3)
                act.dma_start(attended[bass.ds(c, 1)].rearrange("o p n s -> p (o n) s"), o[b][:, :, :]).then_inc(stored[b], 16)
            both(turn_values, 0, 0)
            both(exponentials, 0, 0)
            with act.Fori(0, NCH // 2 - 1) as i:
                both(copy_weights, i * 2, i)
                both(turn_values, i * 2 + 2, i + 1)
                both(exponentials, i * 2 + 2, i + 1)
                both(store, i * 2, i)
            both(copy_weights, NCH - 2, NCH // 2 - 1)
            both(store, NCH - 2, NCH // 2 - 1)
            for b in range(2):
                act.wait_ge(stored[b], 16 + 16 * (NCH // 2))


def finish_mixers(nc, A, u, mixed, attended, bonus, gl, oh, ol, par, tab):
    ROUNDS = 4
    with Phase(nc) as local:
        sb = lambda name, shape: local.enter_context(nc.sbuf_tensor(name, shape, F32))
        sem = lambda name: local.sem(name)
        t = [{n: sb(f"f_{n}{b}", [P, T]) for n in ("g", "r", "s", "z", "bonus", "n_g", "n_r")} for b in range(2)]
        sq_g, sq_r = sb("f_sq_g", [P, T]), sb("f_sq_r", [P, T])
        up = [sb(f"f_up{b}", [P, P]) for b in range(2)]
        ps = {n: local.enter_context(nc.psum_tensor("f_ps_" + n, [P, 2, HALF], F32)) for n in ("mean", "gate", "r", "g")}
        flat = lambda p: p[:, :, :].rearrange("p h t -> p (h t)")
        landed = [{n: sem(f"f_landed_{n}{b}") for n in ("g", "r", "s", "z", "bonus", "up")} for b in range(2)]
        mm_mean, mm_gate, mm_r, mm_g = (sem("f_mm_" + n) for n in ("mean", "gate", "r", "g"))
        centred, sq_r_done, sq_g_done, root_g, root_r, silu_done, dve_step, g_ready, r_ready, hi_done, lo_done = (
            sem("f_" + n) for n in ("centred", "sq_r_done", "sq_g_done", "root_g", "root_r", "silu_done", "dve", "g_ready", "r_ready", "hi_done", "lo_done"))
        block = local.open_block()
        of_tile = lambda src, n: src[:, :, n:n + 1, :].rearrange("c p o s -> p c (o s)")
        chunks = lambda x: x[:, :].rearrange("p (c s) -> p c s", s=C)
        first_tile = {"g": 0, "r": 4, "s": 8}
        lag = lambda i: [("g", i), ("r", i)] if 0 <= i < ROUNDS else []
        SPLITS = [[("s", i)] * (i < ROUNDS) + lag(i - 1) for i in range(ROUNDS + 1)]

        @block.sync
        def _(sp):
            for i in range(ROUNDS):
                b = i % 2
                if i >= 2:
                    sp.wait_ge(lo_done, 3 * (i - 1) + 1)
                load = lambda name, to, src: sp.dma_start(to, src).then_inc(landed[b][name], 16)
                load("r", chunks(t[b]["r"]), of_tile(mixed, i))
                load("g", chunks(t[b]["g"]), of_tile(mixed, i + 4))
                load("z", t[b]["z"][:, :], u[(i + U_Z) * P:(i + U_Z + 1) * P, :])
                load("s", chunks(t[b]["s"]), of_tile(attended, i))
                load("up", up[b][:, :], A["rwkv_g_up"][0][:, i * P:(i + 1) * P])
                load("bonus", t[b]["bonus"][:, :], bonus[i * P:(i + 1) * P, :])

        @block.tensor
        def _(pe):
            def dot(out, w, x, done):
                for h in range(2):
                    last = pe.matmul(out[:, h, :], w, x[:, h * HALF:(h + 1) * HALF], start=True, stop=True)
                last.then_inc(done, 1)

            def mean(i):
                pe.wait_ge(landed[i % 2]["r"], i // 2 * 16 + 16)
                if i:
                    pe.wait_ge(centred, i)
                dot(ps["mean"], tab("head_ones"), t[i % 2]["r"], mm_mean)
            mean(0)
            for i in range(ROUNDS):
                pe.wait_ge(sq_g_done, i + 1)
                if i:
                    pe.wait_ge(root_g, i)
                dot(ps["g"], tab("ones"), sq_g, mm_g)
                pe.wait_ge(sq_r_done, i + 1)
                if i:
                    pe.wait_ge(root_r, i)
                dot(ps["r"], tab("head_ones"), sq_r, mm_r)
                pe.wait_ge(landed[i % 2]["up"], i // 2 * 16 + 16)
                if i:
                    pe.wait_ge(r_ready, i)
                dot(ps["gate"], up[i % 2][:, :], gl, mm_gate)
                if i + 1 < ROUNDS:
                    mean(i + 1)

        @block.scalar
        def _(act):
            for i in range(ROUNDS + 1):
                if i < ROUNDS:
                    x, on = t[i % 2], landed[i % 2]
                    act.wait_ge(on["z"], i // 2 * 16 + 16)
                    act.activation(x["z"][:, :], x["z"][:, :], ACT.Silu).then_inc(silu_done, 1)
                    act.wait_ge(on["g"], i // 2 * 16 + 16)
                    act.activation(sq_g[:, :], x["g"][:, :], ACT.Square).then_inc(sq_g_done, 1)
                    act.wait_ge(centred, i + 1)
                    act.activation(sq_r[:, :], x["r"][:, :], ACT.Square).then_inc(sq_r_done, 1)
                    if i >= 2:
                        act.wait_ge(r_ready, i - 1)
                    act.wait_ge(mm_g, i + 1)
                    act.activation(x["n_g"][:, :], flat(ps["g"]), ACT.Sqrt, bias=par("eps_gdn"), scale=1.0 / GD).then_inc(root_g, 1)
                    act.wait_ge(mm_r, i + 1)
                    act.activation(x["n_r"][:, :], flat(ps["r"]), ACT.Sqrt, bias=par("eps_lnx"), scale=1.0 / RD).then_inc(root_r, 1)
                for name, j in SPLITS[i]:
                    if name == "s":
                        act.wait_ge(landed[j % 2]["s"], j // 2 * 16 + 16)
                    else:
                        act.wait_ge({"g": g_ready, "r": r_ready}[name], j + 1)
                    act.activation(oh[:, first_tile[name] + j, :], t[j % 2][name][:, :], ACT.Copy).then_inc(hi_done, 1)

        @block.gpsimd
        def _(pool):
            done = 0
            for splits in SPLITS:
                for name, j in splits:
                    done += 1
                    pool.wait_ge(hi_done, done)
                    n = first_tile[name] + j
                    pool.tensor_tensor(ol[:, n, :], t[j % 2][name][:, :], as_f32(oh[:, n, :]), ALU.subtract).then_inc(lo_done, 1)

        @block.vector
        def _(dve):
            step = Chain(dve, dve_step)

            def centre(i):
                r = t[i % 2]["r"]
                dve.wait_ge(mm_mean, i + 1)
                dve.scalar_tensor_tensor(r[:, :], flat(ps["mean"]), -1.0 / RD, r[:, :], ALU.mult, ALU.add).then_inc(centred, 1)
            centre(0)
            for i in range(ROUNDS):
                x, on = t[i % 2], landed[i % 2]
                dve.wait_ge(root_g, i + 1)
                step(dve.reciprocal(x["n_g"][:, :], x["n_g"][:, :]))
                step(dve.tensor_tensor(x["g"][:, :], x["g"][:, :], x["n_g"][:, :], ALU.mult))
                dve.wait_ge(silu_done, i + 1)
                dve.scalar_tensor_tensor(x["g"][:, :], x["g"][:, :], par("norm_w"), x["z"][:, :], ALU.mult, ALU.mult).then_inc(g_ready, 1)
                dve.wait_ge(root_r, i + 1)
                step(dve.reciprocal(x["n_r"][:, :], x["n_r"][:, :]))
                step(dve.tensor_tensor(x["r"][:, :], x["r"][:, :], x["n_r"][:, :], ALU.mult))
                step(dve.tensor_scalar(x["r"][:, :], x["r"][:, :], par("lnx_w", i), par("lnx_b", i), ALU.mult, ALU.add))
                dve.wait_ge(on["bonus"], i // 2 * 16 + 16)
                step(dve.tensor_tensor(x["r"][:, :], x["r"][:, :], x["bonus"][:, :], ALU.add))
                dve.wait_ge(mm_gate, i + 1)
                dve.tensor_tensor(x["r"][:, :], x["r"][:, :], flat(ps["gate"]), ALU.mult).then_inc(r_ready, 1)
                if i + 1 < ROUNDS:
                    centre(i + 1)


def project_branches(nc, A, u, oh, ol, merged):
    with Phase(nc) as local:
        sem = lambda name: local.sem(name)
        sb = lambda name, shape, dt=F32: local.enter_context(nc.sbuf_tensor(name, shape, dt))
        raw = sb("b_raw", [P, 12, P])
        whi = [sb(f"b_hi{b}", [P, 12, P], F32R) for b in range(2)]
        wlo = [sb(f"b_lo{b}", [P, 12, P], F32R) for b in range(2)]
        gate = [sb(f"b_gate{b}", [P, 3, T]) for b in range(2)]
        total, part = [sb(f"b_total{b}", [P, T]) for b in range(2)], sb("b_part", [P, T])
        ps = [local.enter_context(nc.psum_tensor(f"b_ps{n}", [P, 2, HALF], F32)) for n in range(3)]
        flat = lambda p: p[:, :, :].rearrange("p h t -> p (h t)")
        landed = sem("b_landed")
        gate_landed = [sem(f"b_gate_landed{b}") for b in range(2)]
        stored = [sem(f"b_stored{b}") for b in range(2)]
        hi_done, lo_done, gate_done, mm_done, evac, dve_step, total_done = (
            sem("b_" + n) for n in ("hi_done", "lo_done", "gate_done", "mm_done", "evac", "dve", "total_done"))
        block = local.open_block()

        def tiles(eng, step):
            with eng.Fori(0, KT // 2) as i:
                for b in range(2):
                    step(i * 2 + b, i, b)

        @block.sync
        def _(sp):
            sp.sem_inc(evac, 6)
            sp.sem_inc(lo_done, 2)

            def load(n, b):
                sp.wait_ge(lo_done, n + 2)
                for k, name in enumerate("abc"):
                    sp.dma_start(raw[:, 4 * k:4 * k + 4, :], A["w_branch_" + name][0][:, bass.ds(n * P, P)].rearrange("(k p) n -> p k n", p=P)).then_inc(landed, 16)
                sp.wait_ge(evac, n * 3 + 3)
                for k in range(3):
                    sp.dma_start(gate[b][:, k, :], u[bass.ds(n * P + (U_GATE + 8 * k) * P, P), :]).then_inc(gate_landed[b], 16)

            def store(n, b):
                sp.wait_ge(total_done, n + 1)
                sp.dma_start(merged[bass.ds(n, 1), :, :].rearrange("o p t -> (o p) t"), total[b][:, :]).then_inc(stored[b], 16)
            load(0, 0)
            load(1, 1)
            with sp.Fori(0, KT // 2 - 1) as i:
                for b in range(2):
                    store(i * 2 + b, b)
                    load(i * 2 + (b + 2), b)
            for b in range(2):
                store(KT - 2 + b, b)
            for b in range(2):
                sp.wait_ge(stored[b], 16 * (KT // 2))

        @block.scalar
        def _(act):
            act.sem_inc(mm_done, 6)

            def step(n, i, b):
                act.wait_ge(landed, n * 48 + 48)
                act.wait_ge(mm_done, n * 3 + 3)
                act.activation(whi[b][:, :, :], raw[:, :, :], ACT.Copy).then_inc(hi_done, 1)
                act.wait_ge(gate_landed[b], i * 48 + 48)
                act.activation(gate[b][:, :, :], gate[b][:, :, :], ACT.Sigmoid).then_inc(gate_done, 1)
            tiles(act, step)

        @block.gpsimd
        def _(pool):
            def step(n, i, b):
                pool.wait_ge(hi_done, n + 1)
                pool.tensor_tensor(wlo[b][:, :, :], raw[:, :, :], as_f32(whi[b][:, :, :]), ALU.subtract).then_inc(lo_done, 1)
            tiles(pool, step)

        @block.tensor
        def _(pe):
            def step(n, i, b):
                pe.wait_ge(lo_done, n + 3)
                for k in range(3):
                    pe.wait_ge(evac, n * 3 + (k + 4))
                    for q in range(4):
                        for h in range(2):
                            cols = slice(h * HALF, (h + 1) * HALF)
                            last = split_dot(pe, ps[k][:, h, :], whi[b][:, 4 * k + q, :], wlo[b][:, 4 * k + q, :],
                                             oh[:, 4 * k + q, cols], ol[:, 4 * k + q, cols], q == 0, q == 3)
                    last.then_inc(mm_done, 1)
            tiles(pe, step)

        @block.vector
        def _(dve):
            def step(n, i, b, first=False):
                chain = Chain(dve, dve_step, n)
                dve.wait_ge(gate_done, n + 1)
                dve.wait_ge(mm_done, n * 3 + 7)
                if not first:
                    dve.wait_ge(stored[b], i * 16)
                dve.tensor_tensor(total[b][:, :], flat(ps[0]), gate[b][:, 0, :], ALU.mult).then_inc(evac, 1)
                if not (first and b == 0):
                    dve.wait_ge(total_done, n)
                for k in (1, 2):
                    dve.wait_ge(mm_done, n * 3 + (7 + k))
                    dve.tensor_tensor(part[:, :], flat(ps[k]), gate[b][:, k, :], ALU.mult).then_inc(evac, 1)
                    dve.wait_ge(evac, n * 3 + (7 + k))
                    add = dve.tensor_tensor(total[b][:, :], total[b][:, :], part[:, :], ALU.add)
                    if k == 1:
                        chain(add)
                    else:
                        add.then_inc(total_done, 1)
            for b in range(2):
                step(b, 0, b, True)
            with dve.Fori(1, KT // 2) as i:
                for b in range(2):
                    step(i * 2 + b, i, b)


def layer_norm(dve, step, act_root, y, stats, mv, w, b, halves):
    for h in range(2):
        step(dve.bn_stats(stats[:, h, :], halves[h]))
    step(dve.bn_aggr(mv[:, :], stats[:, :, :].rearrange("p h s -> p (h s)")))
    act_root()
    step(dve.reciprocal(mv[:, 1:2], mv[:, 1:2]))
    step(dve.tensor_scalar(y, y, mv[:, 0:1], mv[:, 1:2], ALU.subtract, ALU.mult))
    step(dve.tensor_tensor(y, y, w[:, :], ALU.mult))
    step(dve.tensor_tensor(y, y, b[:, :], ALU.add))


def project_out(nc, A, merged, x1, par):
    with Phase(nc) as local:
        sem = lambda name: local.sem(name)
        sb = lambda name, shape, dt=F32: local.enter_context(nc.sbuf_tensor(name, shape, dt))
        raw_m, raw_w = [sb(f"o_raw_m{b}", [P, T]) for b in range(2)], [sb(f"o_raw_w{b}", [P, D]) for b in range(2)]
        mhi, mlo, whi, wlo = (sb("o_" + n, [P, KT, T], F32R) for n in ("mhi", "mlo", "whi", "wlo"))
        x, y = [sb(f"o_x{b}", [P, D]) for b in range(2)], [sb(f"o_y{b}", [P, D]) for b in range(2)]
        ln_w, ln_b, stats, mv = sb("o_ln_w", [P, D]), sb("o_ln_b", [P, D]), sb("o_stats", [P, 2, 6]), sb("o_mv", [P, 2])
        ps = [local.enter_context(nc.psum_tensor(f"o_ps{n}", [P, 2, HALF], F32)) for n in range(4)]
        landed, x_landed, stored = [sem(f"o_landed{b}") for b in range(2)], [sem(f"o_x_landed{b}") for b in range(2)], [sem(f"o_stored{b}") for b in range(2)]
        ln_landed, hi_done, lo_done, mm_done, added, dve_step, mv_done, root_done, y_done = (
            sem("o_" + n) for n in ("ln_landed", "hi_done", "lo_done", "mm_done", "added", "dve", "mv_done", "root_done", "y_done"))
        block = local.open_block()

        @block.sync
        def _(sp):
            for k in range(KT):
                b = k % 2
                if k >= 2:
                    sp.wait_ge(lo_done, 2 * (k - 1))
                sp.dma_start(raw_m[b][:, :], merged[k]).then_inc(landed[b], 16)
                sp.dma_start(raw_w[b][:, :], A["w_out"][0][k * P:(k + 1) * P, :]).then_inc(landed[b], 16)
            sp.dma_start(ln_w[:, :], A["ln1_w"].to_broadcast([P, D])).then_inc(ln_landed, 16)
            sp.dma_start(ln_b[:, :], A["ln1_b"].to_broadcast([P, D])).then_inc(ln_landed, 16)
            for n in range(8):
                if n >= 2:
                    sp.wait_ge(added, n - 1)
                sp.dma_start(x[n % 2][:, :], A["x"][0][n * P:(n + 1) * P, :]).then_inc(x_landed[n % 2], 16)

        @block.scalar
        def _(act):
            for k in range(KT):
                b = k % 2
                act.wait_ge(landed[b], 32 * (k // 2 + 1))
                act.activation(mhi[:, k, :], raw_m[b][:, :], ACT.Copy).then_inc(hi_done, 1)
                act.activation(whi[:, k, :], raw_w[b][:, :], ACT.Copy).then_inc(hi_done, 1)
            for n in range(8):
                act.wait_ge(mv_done, n + 1)
                act.activation(mv[:, 1:2], mv[:, 1:2], ACT.Sqrt, bias=par("eps_ln")).then_inc(root_done, 1)
                act.wait_ge(y_done, n + 1)
                act.dma_start(x1[n * P:(n + 1) * P, :], y[n % 2][:, :]).then_inc(stored[n % 2], 16)
            for b in range(2):
                act.wait_ge(stored[b], 64)

        @block.tensor
        def _(pe):
            for n in range(8):
                if n >= 4:
                    pe.wait_ge(added, n - 3)
                for h in range(2):
                    for k in range(KT):
                        if n == 0 and h == 0:
                            pe.wait_ge(lo_done, 2 * k + 2)
                        last = split_dot(pe, ps[n % 4][:, h, :], mhi[:, k, n * P:(n + 1) * P], mlo[:, k, n * P:(n + 1) * P],
                                         whi[:, k, h * HALF:(h + 1) * HALF], wlo[:, k, h * HALF:(h + 1) * HALF], k == 0, k == KT - 1)
                last.then_inc(mm_done, 1)

        @block.vector
        def _(dve):
            for k in range(KT):
                b = k % 2
                dve.wait_ge(hi_done, 2 * k + 2)
                dve.tensor_tensor(mlo[:, k, :], raw_m[b][:, :], as_f32(mhi[:, k, :]), ALU.subtract).then_inc(lo_done, 1)
                dve.tensor_tensor(wlo[:, k, :], raw_w[b][:, :], as_f32(whi[:, k, :]), ALU.subtract).then_inc(lo_done, 1)
            dve.wait_ge(ln_landed, 32)
            step = Chain(dve, dve_step)
            for n in range(8):
                b = n % 2
                dve.wait_ge(x_landed[b], 16 * (n // 2 + 1))
                dve.wait_ge(mm_done, n + 1)
                if n >= 2:
                    dve.wait_ge(stored[b], 16 * (n // 2))
                dve.scalar_tensor_tensor(y[b][:, :], x[b][:, :], ALPHA, ps[n % 4][:, :, :].rearrange("p h t -> p (h t)"),
                                         ALU.mult, ALU.add).then_inc(added, 1)
                dve.wait_ge(added, n + 1)

                def root():
                    dve.sem_inc(mv_done, 1)
                    dve.wait_ge(root_done, n + 1)
                layer_norm(dve, step, root, y[b][:, :], stats, mv, ln_w, ln_b, [y[b][:, h * HALF:(h + 1) * HALF] for h in range(2)])
                dve.sem_inc(y_done, 1)


def feed_forward(nc, A, xhi, xlo, y, out, par):
    NF = FF // P
    with Phase(nc) as local:
        sem = lambda name: local.sem(name)
        sb = lambda name, shape, dt=F32: local.enter_context(nc.sbuf_tensor(name, shape, dt))
        NAMES = ("gate", "up", "down")
        raw = [{n: sb(f"ff_raw_{n}{b}", [P, KT, P]) for n in NAMES} for b in range(2)]
        whi = [{n: sb(f"ff_hi_{n}{b}", [P, KT, P], F32R) for n in NAMES} for b in range(2)]
        wlo = [{n: sb(f"ff_lo_{n}{b}", [P, KT, P], F32R) for n in NAMES} for b in range(2)]
        hid = sb("ff_hid", [P, 2, HALF])
        hhi, hlo = [sb(f"ff_hhi{b}", [P, T], F32R) for b in range(2)], [sb(f"ff_hlo{b}", [P, T], F32R) for b in range(2)]
        ps_g, ps_u = (local.enter_context(nc.psum_tensor("ff_" + n, [P, 2, HALF], F32)) for n in ("ps_g", "ps_u"))
        ps_d = [local.enter_context(nc.psum_tensor(f"ff_d{n}", [P, HALF], F32)) for n in range(4)]
        landed = [sem(f"ff_landed{b}") for b in range(2)]
        hi_done, lo_done, mm_g, mm_u, mm_d, silu_done, mul_done, hhi_done, hlo_done, added = (
            sem("ff_" + n) for n in ("hi_done", "lo_done", "mm_g", "mm_u", "mm_d", "silu_done", "mul_done", "hhi_done", "hlo_done", "added"))
        flat = lambda w: w[:, :, :].rearrange("p k n -> p (k n)")

        def steps(eng, make, add):
            make(0, 0, 0)
            with eng.Fori(0, NF // 2 - 1) as i:
                make(i * 2 + 1, i, 1)
                add(i * 2, 0)
                make(i * 2 + 2, i + 1, 0)
                add(i * 2 + 1, 1)
            make(NF - 1, NF // 2 - 1, 1)
            add(NF - 2, 0)
            add(NF - 1, 1)

        block = local.open_block()

        @block.sync
        def _(sp):
            sp.sem_inc(lo_done, 6)
            def make(f, i, b):
                sp.wait_ge(lo_done, f * 3 + 3)
                for n in ("gate", "up"):
                    sp.dma_start(raw[b][n][:, :, :], A["ffn_" + n][0][:, bass.ds(f * P, P)].rearrange("(k p) n -> p k n", p=P)).then_inc(landed[b], 16)
                sp.dma_start(flat(raw[b]["down"]), A["ffn_down"][0][bass.ds(f * P, P), :]).then_inc(landed[b], 16)
            steps(sp, make, lambda f, b: None)

        @block.scalar
        def _(act):
            act.sem_inc(mm_d, 32)
            act.sem_inc(mm_u, 4)
            act.sem_inc(hlo_done, 2)
            def split(b, *names):
                for n in names:
                    act.activation(whi[b][n][:, :, :], raw[b][n][:, :, :], ACT.Copy).then_inc(hi_done, 1)

            def split_gate_up(f, i, b):
                act.wait_ge(landed[b], i * 48 + 48)
                act.wait_ge(mm_u, f * 2 + 2)
                split(b, "gate", "up")

            def split_down(f, b):
                act.wait_ge(mm_d, f * 16 + 16)
                split(b, "down")

            def hidden(f, b):
                act.wait_ge(mm_g, f + 1)
                act.wait_ge(hlo_done, f * 2 + 2)
                act.activation(hid[:, :, :], ps_g[:, :, :], ACT.Silu).then_inc(silu_done, 1)
                for h in range(2):
                    act.wait_ge(mul_done, f * 2 + (h + 3))
                    act.activation(hhi[b][:, h * HALF:(h + 1) * HALF], hid[:, h, :], ACT.Copy).then_inc(hhi_done, 1)
            split_gate_up(0, 0, 0)
            split_down(0, 0)
            with act.Fori(0, NF // 2 - 1) as i:
                split_gate_up(i * 2 + 1, i, 1)
                hidden(i * 2, 0)
                split_down(i * 2 + 1, 1)
                split_gate_up(i * 2 + 2, i + 1, 0)
                hidden(i * 2 + 1, 1)
                split_down(i * 2 + 2, 0)
            split_gate_up(NF - 1, NF // 2 - 1, 1)
            hidden(NF - 2, 0)
            split_down(NF - 1, 1)
            hidden(NF - 1, 1)

        @block.gpsimd
        def _(pool):
            def make(f, i, b):
                for k, n in enumerate(NAMES):
                    pool.wait_ge(hi_done, f * 3 + (k + 1))
                    pool.tensor_tensor(wlo[b][n][:, :, :], raw[b][n][:, :, :], as_f32(whi[b][n][:, :, :]), ALU.subtract).then_inc(lo_done, 1)
            steps(pool, make, lambda f, b: None)

        @block.tensor
        def _(pe):
            def make(f, i, b):
                for name, ps, done in (("gate", ps_g, mm_g), ("up", ps_u, mm_u)):
                    if name == "gate":
                        pe.wait_ge(lo_done, f * 3 + 7)
                        pe.wait_ge(silu_done, f + 1)
                    else:
                        pe.wait_ge(lo_done, f * 3 + 8)
                        pe.wait_ge(mul_done, f * 2 + 2)
                    for h in range(2):
                        for k in range(KT):
                            cols = slice(h * HALF, (h + 1) * HALF)
                            last = split_dot(pe, ps[:, h, :], whi[b][name][:, k, :], wlo[b][name][:, k, :],
                                             xhi[:, k, cols], xlo[:, k, cols], k == 0, k == KT - 1)
                        if name == "up" or h:
                            last.then_inc(done, 1)

            def add(f, b):
                pe.wait_ge(hlo_done, f * 2 + 4)
                pe.wait_ge(lo_done, f * 3 + 9)
                dhi, dlo = flat(whi[b]["down"]), flat(wlo[b]["down"])
                for n in range(16):
                    pe.wait_ge(added, f * 16 + (n + 1))
                    tok, cols = slice(n // 2 * P, (n // 2 + 1) * P), slice(n % 2 * HALF, (n % 2 + 1) * HALF)
                    split_dot(pe, ps_d[n % 4][:, :], hhi[b][:, tok], hlo[b][:, tok], dhi[:, cols], dlo[:, cols], True, True).then_inc(mm_d, 1)
            pe.sem_inc(silu_done, 1)
            pe.sem_inc(mul_done, 2)
            pe.sem_inc(added, 4)
            steps(pe, make, add)

        @block.vector
        def _(dve):
            def make(f, i, b):
                dve.wait_ge(silu_done, f + 2)
                for h in range(2):
                    cols = slice(h * HALF, (h + 1) * HALF)
                    dve.wait_ge(mm_u, f * 2 + (h + 5))
                    dve.wait_ge(mm_d, f * 16 + 16)
                    dve.tensor_tensor(hid[:, h, :], hid[:, h, :], ps_u[:, h, :], ALU.mult).then_inc(mul_done, 1)
                    dve.wait_ge(hhi_done, f * 2 + (h + 1))
                    dve.tensor_tensor(hlo[b][:, cols], hid[:, h, :], as_f32(hhi[b][:, cols]), ALU.subtract).then_inc(hlo_done, 1)

            def add(f, b):
                for n in range(16):
                    dve.wait_ge(mm_d, f * 16 + (n + 33))
                    part = y[:, n // 2, n % 2 * HALF:(n % 2 + 1) * HALF]
                    dve.tensor_tensor(part, part, ps_d[n % 4][:, :], ALU.add).then_inc(added, 1)
            steps(dve, make, add)

    with Phase(nc) as local:
        sem = lambda name: local.sem(name)
        sb = lambda name, shape, dt=F32: local.enter_context(nc.sbuf_tensor(name, shape, dt))
        NT = T // P
        ln_w, ln_b = sb("l_ln_w", [P, D]), sb("l_ln_b", [P, D])
        stats, mv = sb("l_stats", [P, NT, 2, 6]), sb("l_mv", [P, NT, 2])
        ln_landed, stats_done, mv_done, root_done, rstd_done, norm_done, scale_done, y_done, stored = (
            sem("l_" + n) for n in ("ln_landed", "stats_done", "mv_done", "root_done", "rstd_done", "norm_done", "scale_done", "y_done", "stored"))
        block = local.open_block()

        @block.sync
        def _(sp):
            sp.dma_start(ln_w[:, :], A["ln2_w"].to_broadcast([P, D])).then_inc(ln_landed, 16)
            sp.dma_start(ln_b[:, :], A["ln2_b"].to_broadcast([P, D])).then_inc(ln_landed, 16)
            for n in range(NT):
                sp.wait_ge(y_done, n + 1)
                sp.dma_start(out[0][n * P:(n + 1) * P, :], y[:, n, :]).then_inc(stored, 16)
            sp.wait_ge(stored, 16 * NT)

        @block.scalar
        def _(act):
            act.wait_ge(mv_done, NT)
            act.activation(mv[:, :, 1], mv[:, :, 1], ACT.Sqrt, bias=par("eps_ln")).then_inc(root_done, 1)

        @block.vector
        def _(dve):
            for n in range(NT):
                for h in range(2):
                    dve.bn_stats(stats[:, n, h, :], y[:, n, h * HALF:(h + 1) * HALF]).then_inc(stats_done, 1)
                if n:
                    dve.wait_ge(stats_done, 2 * n)
                    dve.bn_aggr(mv[:, n - 1, :], stats[:, n - 1, :, :].rearrange("p h s -> p (h s)")).then_inc(mv_done, 1)
            dve.wait_ge(stats_done, 2 * NT)
            dve.bn_aggr(mv[:, NT - 1, :], stats[:, NT - 1, :, :].rearrange("p h s -> p (h s)")).then_inc(mv_done, 1)
            dve.wait_ge(root_done, 1)
            dve.reciprocal(mv[:, :, 1], mv[:, :, 1]).then_inc(rstd_done, 1)
            dve.wait_ge(rstd_done, 1)
            dve.wait_ge(ln_landed, 32)
            for n in range(NT + 2):
                if n < NT:
                    dve.tensor_scalar(y[:, n, :], y[:, n, :], mv[:, n, 0:1], mv[:, n, 1:2], ALU.subtract, ALU.mult).then_inc(norm_done, 1)
                if 0 < n <= NT:
                    dve.wait_ge(norm_done, n)
                    dve.tensor_tensor(y[:, n - 1, :], y[:, n - 1, :], ln_w[:, :], ALU.mult).then_inc(scale_done, 1)
                if n > 1:
                    dve.wait_ge(scale_done, n - 1)
                    dve.tensor_tensor(y[:, n - 2, :], y[:, n - 2, :], ln_b[:, :], ALU.add).then_inc(y_done, 1)


PARAM_NAMES = ("rwkv_mu", "rwkv_w0", "rwkv_a0", "rwkv_k_k", "rwkv_k_a", "rwkv_r_k", "rwkv_lnx_w", "rwkv_lnx_b",
               "gdn_conv", "gdn_norm_w", "gdn_a_log", "gdn_dt_bias", "swa_sinks")
INPUTS = ("x", "w_in") + PARAM_NAMES + ("rwkv_w_up", "rwkv_a_up", "rwkv_g_up", "w_branch_a", "w_branch_b", "w_branch_c",
                                        "w_out", "ln1_w", "ln1_b", "ffn_gate", "ffn_up", "ffn_down", "ln2_w", "ln2_b")


def hybrid_layer_kernel(nc, A, const_dram, out):
    dram = lambda name, shape: nc.dram_tensor(name, shape, F32, kind="Internal").ap()
    u = dram("u", [(ALL_TILES + 1) * P, T])
    rows, egl = dram("rows", [5, GH, T]), dram("egl", [GH, NCH])
    opnd, bonus = dram("opnd", [NCH, P, N_OP * 4 * C]), dram("bonus", [RH * RD, T])
    nt, xinv = dram("nt", [NCH, P, NPAIR, NB]), dram("xinv", [NCH, P, 2, NPAIR, NB])
    mixed, attended = dram("mixed", [NCH, P, 8, C]), dram("attended", [NCH, P, 4, C])
    merged, x1 = dram("merged", [KT, P, T]), dram("x1", [T, D])
    with ExitStack() as ctx:
        sb = lambda stack, name, shape, dt=F32: stack.enter_context(nc.sbuf_tensor(name, shape, dt))
        par = Params(sb(ctx, "params", [P, N_PARAM]))
        tab = Tables(sb(ctx, "tables", [P, CONST.shape[1]]))
        par_landed = ctx.enter_context(nc.semaphore("par_landed"))
        with ExitStack() as s:
            gl, plast = sb(s, "gl", [P, T]), sb(s, "plast", [P, 4 * NCH])
            cols, egl_bc = sb(s, "cols", [P, NCH, 3, 2]), sb(s, "egl_bc", [P, GH, NCH])
            decays = sb(s, "decays", [P, 4, T])
            gates_tile = decays[:, :, :].rearrange("p k t -> p (k t)").rearrange("p (c g k s) -> p c g k s", c=NCH, g=2, k=2)
            with ExitStack() as sx:
                xhi, xlo = sb(sx, "xhi", [P, KT, T], F32R), sb(sx, "xlo", [P, KT, T], F32R)
                with nc.sbuf_tensor("xin", [P, 8, D], F32) as xin:
                    with nc.Block() as block:
                        @block.gpsimd
                        def _(pool):
                            pool.wait_ge(par_landed, load_params(nc, pool, par, A, par_landed))
                    transpose_x(nc, A["x"][0], xin, xhi, xlo, tab, const_dram)
                project_in(nc, A["w_in"][0], xhi, xlo, u)
                wa = sb(sx, "wa", [P, T])
                prepare_rows(nc, u, rows, egl, par, tab, wa, gl)
                prepare_rwkv(nc, A, u, opnd, bonus, plast, par, tab, wa, xhi, xlo, decays)
                prepare_gdn(nc, A, u, rows, opnd, par, tab, xhi, xlo, decays)
                prepare_decays(nc, rows, egl, gates_tile, cols, egl_bc, tab)
                diagonal_blocks(nc, opnd, gates_tile, nt, tab)
                invert_blocks(nc, A, u, xhi, xlo, nt, xinv)
            scan_chunks(nc, opnd, xinv, gates_tile, cols, egl_bc, plast, mixed, tab)
            window_attention(nc, u, attended, par, tab)
            oh, ol = sb(s, "oh", [P, 12, T], F32R), sb(s, "ol", [P, 12, T], F32R)
            finish_mixers(nc, A, u, mixed, attended, bonus, gl, oh, ol, par, tab)
            project_branches(nc, A, u, oh, ol, merged)
        project_out(nc, A, merged, x1, par)
        with ExitStack() as s:
            y = sb(s, "y", [P, 8, D])
            xhi, xlo = sb(s, "x1hi", [P, KT, T], F32R), sb(s, "x1lo", [P, KT, T], F32R)
            transpose_x(nc, x1, y, xhi, xlo, tab, scaled=ALPHA)
            feed_forward(nc, A, xhi, xlo, y, out, par)


def kernel(**inputs):
    import concourse.bacc as bacc
    from concourse.bass_utils import run_bass_kernel_spmd

    nc = bacc.Bacc("TRN2", target_bir_lowering=False, num_devices=1)
    arrays, A = {}, {}
    for name in INPUTS:
        a = np.ascontiguousarray(inputs[name])
        arrays[f"in_{name}"] = a
        A[name] = nc.dram_tensor(f"in_{name}", a.shape, mybir.dt.from_np(a.dtype), kind="ExternalInput").ap()
    arrays["in_const"] = CONST
    const_dram = nc.dram_tensor("in_const", CONST.shape, F32, kind="ExternalInput").ap()
    out = nc.dram_tensor("out_0", (1, T, D), F32, kind="ExternalOutput").ap()
    hybrid_layer_kernel(nc, A, const_dram, out)
    return run_bass_kernel_spmd(nc, [arrays], core_ids=[0]).results[0]["out_0"]
```
